# Optimizing a Trainium2 kernel written in Bass

```python
import jax, jax.numpy as jnp
from jax import lax
import numpy as np

D_MODEL = 1024
BATCH = 1
SEQ = 256
DEPTH = 1
DEC_BATCH = 8
DEC_SEQ = 8
PAST_LEN = 2048
PAGE_SIZE = 128

S5_WIDTH = D_MODEL // 2
S5_GROUP = 16
S5_NGROUPS = S5_WIDTH // S5_GROUP
S5_STATE = 64
RWKV_WIDTH = D_MODEL - S5_WIDTH
RWKV_HEAD = 64
RWKV_HEADS = RWKV_WIDTH // RWKV_HEAD
RWKV_IN = 4 * RWKV_WIDTH
IN_WIDTH = S5_WIDTH + RWKV_IN
MIX_WIDTH = S5_WIDTH + RWKV_WIDTH
LORA_DECAY = 64
LORA_AAA = 64
LORA_GATE = 128
DECAY_SCALE = 0.6065306597
N_MEM = 256
MEM_HEADS = 4
MEM_HEAD_DIM = D_MODEL // MEM_HEADS
MEM_SCALE = MEM_HEAD_DIM ** -0.5
N_EXPERTS = 32
TOP_K = 4
D_FF = D_MODEL
SWIGLU_LIMIT = 7.0
SWIGLU_ALPHA = 1.702
MOE_BLOCK = 128
RMS_EPS = 1e-5
GN_EPS = 64e-5

kernel_name = "hymba_s5_rwkv7_memxattn_moe_step"

def rmsnorm(x, g):
    xf = x.astype(jnp.float32)
    xf = xf * lax.rsqrt(jnp.mean(xf * xf, axis=-1, keepdims=True) + RMS_EPS)
    return xf.astype(x.dtype) * g

def _complex_affine_combine(e1, e2):
    a1r, a1i, b1r, b1i = e1
    a2r, a2i, b2r, b2i = e2
    return (a2r * a1r - a2i * a1i,
            a2r * a1i + a2i * a1r,
            a2r * b1r - a2i * b1i + b2r,
            a2r * b1i + a2i * b1r + b2i)

def s5_mixer(u, h0_re, h0_im, lam_re, lam_im, log_dt, b_re, b_im, c_re, c_im, d, glu_w, glu_b):
    f32 = jnp.float32
    bsz, t, _ = u.shape
    uf = u.astype(f32).reshape(bsz, t, S5_NGROUPS, S5_GROUP)
    dt = jnp.exp(log_dt.astype(f32))[:, None]
    lr = lam_re.astype(f32)
    li = lam_im.astype(f32)
    mag = jnp.exp(lr * dt)
    ar = mag * jnp.cos(li * dt)
    ai = mag * jnp.sin(li * dt)
    den = lr * lr + li * li
    cr = ((ar - 1.0) * lr + ai * li) / den
    ci = (ai * lr - (ar - 1.0) * li) / den
    br = b_re.astype(f32)
    bi = b_im.astype(f32)
    bbar_r = cr[..., None] * br - ci[..., None] * bi
    bbar_i = cr[..., None] * bi + ci[..., None] * br
    bu_r = jnp.einsum('btgc,gpc->btgp', uf, bbar_r)
    bu_i = jnp.einsum('btgc,gpc->btgp', uf, bbar_i)
    a_r = jnp.broadcast_to(ar, bu_r.shape)
    a_i = jnp.broadcast_to(ai, bu_i.shape)
    acc_r, acc_i, x_r, x_i = lax.associative_scan(_complex_affine_combine, (a_r, a_i, bu_r, bu_i), axis=1)
    if h0_re is not None:
        hr = h0_re.astype(f32)[:, None]
        hi = h0_im.astype(f32)[:, None]
        x_r, x_i = x_r + acc_r * hr - acc_i * hi, x_i + acc_r * hi + acc_i * hr
    y = (jnp.einsum('gcp,btgp->btgc', c_re.astype(f32), x_r)
         - jnp.einsum('gcp,btgp->btgc', c_im.astype(f32), x_i)
         + d.astype(f32).reshape(S5_NGROUPS, S5_GROUP) * uf)
    y = y.reshape(bsz, t, S5_WIDTH)
    z = jax.nn.gelu(y)
    out = z * jax.nn.sigmoid(z @ glu_w.astype(f32) + glu_b.astype(f32))
    return out.astype(u.dtype), x_r[:, -1], x_i[:, -1]

def rwkv7_mixer(p, prev, s0, mu, w0, w1, w2, a0, a1, a2, g1, g2, k_k, k_a, r_k, ln_w, ln_b):
    f32 = jnp.float32
    bsz, t, _ = p.shape
    pf = p.astype(f32)
    shifted = jnp.concatenate([prev.astype(f32)[:, None], pf[:, :-1]], axis=1)
    delta = shifted - pf
    r_p, k_p, v_p, z_p = jnp.split(pf, 4, axis=-1)
    r_d, k_d, v_d, z_d = jnp.split(delta, 4, axis=-1)
    mu = mu.astype(f32)
    r = r_p + r_d * mu[0]
    k = k_p + k_d * mu[1]
    v = v_p + v_d * mu[2]
    zw = z_p + z_d * mu[3]
    za = z_p + z_d * mu[4]
    zg = z_p + z_d * mu[5]
    decay = jnp.exp(-DECAY_SCALE * jax.nn.sigmoid(w0 + jnp.tanh(zw @ w1) @ w2))
    a = jax.nn.sigmoid(a0 + (za @ a1) @ a2)
    g = jax.nn.sigmoid(zg @ g1) @ g2
    hd = lambda z: z.astype(f32).reshape(bsz, t, RWKV_HEADS, RWKV_HEAD)
    r, decay, k, v, a = hd(r), hd(decay), hd(k), hd(v), hd(a)
    kk = k * k_k.astype(f32).reshape(RWKV_HEADS, RWKV_HEAD)
    kk = kk * lax.rsqrt(jnp.maximum(jnp.sum(kk * kk, axis=-1, keepdims=True), 1e-24))
    k = k * (1.0 + (a - 1.0) * k_a.astype(f32).reshape(RWKV_HEADS, RWKV_HEAD))

    def step(s, inp):
        r_t, w_t, k_t, v_t, kk_t, a_t = inp
        sa = jnp.einsum('bhvk,bhk->bhv', s, -kk_t)
        s = (s * w_t[:, :, None, :] + sa[..., None] * (kk_t * a_t)[:, :, None, :]
             + v_t[..., None] * k_t[:, :, None, :])
        return s, jnp.einsum('bhvk,bhk->bhv', s, r_t)

    xs = tuple(jnp.moveaxis(z, 1, 0) for z in (r, decay, k, v, kk, a))
    s_final, ys = lax.scan(step, s0.astype(f32), xs)
    y = jnp.moveaxis(ys, 0, 1)
    m = jnp.mean(y, axis=-1, keepdims=True)
    var = jnp.mean(jnp.square(y - m), axis=-1, keepdims=True)
    y = ((y - m) * lax.rsqrt(var + GN_EPS)).reshape(bsz, t, RWKV_WIDTH) * ln_w + ln_b
    bonus = (jnp.sum(r * k * r_k.astype(f32), axis=-1, keepdims=True) * v).reshape(bsz, t, RWKV_WIDTH)
    out = (y + bonus) * g
    return out.astype(p.dtype), p[:, -1], s_final

def memory_kv(mem, g_mem, w_mem_kv):
    m = rmsnorm(mem, g_mem) @ w_mem_kv
    mk, mv = jnp.split(m, 2, axis=-1)
    bsz = mem.shape[0]
    return (mk.reshape(bsz, N_MEM, MEM_HEADS, MEM_HEAD_DIM),
            mv.reshape(bsz, N_MEM, MEM_HEADS, MEM_HEAD_DIM))

def cross_attention(x, mem_k, mem_v, w_cq, w_co):
    bsz, t, _ = x.shape
    q = (x @ w_cq).reshape(bsz, t, MEM_HEADS, MEM_HEAD_DIM)
    s = jnp.einsum('bthd,bmhd->bhtm', q, mem_k.astype(q.dtype)).astype(jnp.float32) * MEM_SCALE
    prob = jax.nn.softmax(s, axis=-1)
    o = jnp.einsum('bhtm,bmhd->bthd', prob.astype(x.dtype), mem_v.astype(x.dtype))
    return o.reshape(bsz, t, D_MODEL) @ w_co

def moe_ffn(x, router_w, router_b, w_gu, b_gu, w_down, b_down):
    f32 = jnp.float32
    n_tok, d = x.shape
    n_assign = n_tok * TOP_K
    logits = x.astype(f32) @ router_w.astype(f32) + router_b.astype(f32)
    top_logit, top_e = lax.top_k(logits, TOP_K)
    gate = jax.nn.softmax(top_logit, axis=-1)
    flat_e = top_e.reshape(-1)
    flat_g = gate.reshape(-1)
    flat_t = jnp.arange(n_assign, dtype=jnp.int32) // TOP_K
    order = jnp.argsort(flat_e)
    sorted_e = flat_e[order]
    counts = jnp.bincount(flat_e, length=N_EXPERTS)
    padded = (counts + MOE_BLOCK - 1) // MOE_BLOCK * MOE_BLOCK
    pad_end = jnp.cumsum(padded)
    pad_start = pad_end - padded
    raw_start = jnp.cumsum(counts) - counts
    dest = pad_start[sorted_e] + jnp.arange(n_assign, dtype=jnp.int32) - raw_start[sorted_e]
    n_rows = -(-n_assign // MOE_BLOCK) * MOE_BLOCK + N_EXPERTS * MOE_BLOCK
    n_blocks = n_rows // MOE_BLOCK
    row_tok = jnp.zeros((n_rows,), jnp.int32).at[dest].set(flat_t[order])
    row_gate = jnp.zeros((n_rows,), f32).at[dest].set(flat_g[order])
    block_start = jnp.arange(n_blocks, dtype=jnp.int32) * MOE_BLOCK
    block_e = jnp.minimum(jnp.sum(pad_end[None, :] <= block_start[:, None], axis=1), N_EXPERTS - 1)
    xb = x[row_tok].reshape(n_blocks, MOE_BLOCK, d)

    def expert_block(args):
        xblk, e = args
        h = xblk @ w_gu[e] + b_gu[e]
        hg, hu = jnp.split(h, 2, axis=-1)
        hg = jnp.minimum(hg, SWIGLU_LIMIT)
        hu = jnp.clip(hu, -SWIGLU_LIMIT, SWIGLU_LIMIT)
        act = (hu + 1.0) * hg * jax.nn.sigmoid(SWIGLU_ALPHA * hg)
        return act @ w_down[e] + b_down[e]

    yb = lax.map(expert_block, (xb, block_e))
    y = jax.ops.segment_sum(yb.reshape(n_rows, d).astype(f32) * row_gate[:, None], row_tok, num_segments=n_tok)
    return y.astype(x.dtype)

def layer(x, mem_k, mem_v, h0_re, h0_im, prev, s0, P, l):
    bsz, t, _ = x.shape
    n1 = rmsnorm(x, P['norm_mix_g'][l])
    proj = n1 @ P['w_in'][l]
    u = proj[..., :S5_WIDTH]
    prk = proj[..., S5_WIDTH:]
    s5_y, h_re, h_im = s5_mixer(u, h0_re, h0_im, P['s5_lambda_re'][l], P['s5_lambda_im'][l], P['s5_log_dt'][l],
                                P['s5_b_re'][l], P['s5_b_im'][l], P['s5_c_re'][l], P['s5_c_im'][l],
                                P['s5_d'][l], P['s5_glu_w'][l], P['s5_glu_b'][l])
    rw_y, shift_last, s_final = rwkv7_mixer(prk, prev, s0, P['rwkv_mu'][l], P['rwkv_w0'][l], P['rwkv_w1'][l],
                                            P['rwkv_w2'][l], P['rwkv_a0'][l], P['rwkv_a1'][l], P['rwkv_a2'][l],
                                            P['rwkv_g1'][l], P['rwkv_g2'][l], P['rwkv_k_k'][l], P['rwkv_k_a'][l],
                                            P['rwkv_r_k'][l], P['rwkv_ln_w'][l], P['rwkv_ln_b'][l])
    x = x + jnp.concatenate([s5_y, rw_y], axis=-1) @ P['w_out'][l]
    x = x + cross_attention(rmsnorm(x, P['norm_ca_g'][l]), mem_k, mem_v, P['w_cq'][l], P['w_co'][l])
    h = rmsnorm(x, P['norm_ffn_g'][l]).reshape(bsz * t, D_MODEL)
    x = x + moe_ffn(h, P['router_w'][l], P['router_b'][l], P['ex_w_gu'][l], P['ex_b_gu'][l],
                    P['ex_w_down'][l], P['ex_b_down'][l]).reshape(bsz, t, D_MODEL)
    return x, h_re, h_im, shift_last, s_final

def setup_inputs(seed: int = 0) -> dict:
    key = jax.random.key(seed)
    ks = jax.random.split(key, 64)
    f32 = jnp.float32
    L = DEPTH
    nrm = lambda k, shape, scale: jax.random.normal(k, shape, f32) * scale
    uni = lambda k, shape, lo, hi: jax.random.uniform(k, shape, f32, lo, hi)
    inp = {}
    inp['x_prompt'] = nrm(ks[0], (BATCH, SEQ, D_MODEL), 1.0)
    inp['x_sample'] = nrm(ks[1], (DEC_BATCH, DEC_SEQ, D_MODEL), 1.0)
    inp['mem_prompt'] = nrm(ks[2], (BATCH, N_MEM, D_MODEL), 1.0)
    inp['state_s5_re'] = nrm(ks[3], (L, DEC_BATCH, S5_NGROUPS, S5_STATE), 0.5)
    inp['state_s5_im'] = nrm(ks[4], (L, DEC_BATCH, S5_NGROUPS, S5_STATE), 0.5)
    inp['state_rwkv_shift'] = nrm(ks[5], (L, DEC_BATCH, RWKV_IN), 1.0)
    inp['state_rwkv_wkv'] = nrm(ks[6], (L, DEC_BATCH, RWKV_HEADS, RWKV_HEAD, RWKV_HEAD), 0.3)
    inp['cache_mem_k'] = nrm(ks[7], (L, DEC_BATCH, N_MEM, MEM_HEADS, MEM_HEAD_DIM), 1.0)
    inp['cache_mem_v'] = nrm(ks[8], (L, DEC_BATCH, N_MEM, MEM_HEADS, MEM_HEAD_DIM), 1.0)
    inp['norm_mix_g'] = 1.0 + nrm(ks[9], (L, D_MODEL), 0.01)
    inp['w_in'] = nrm(ks[10], (L, D_MODEL, IN_WIDTH), D_MODEL ** -0.5)
    inp['s5_lambda_re'] = -0.5 + nrm(ks[11], (L, S5_NGROUPS, S5_STATE), 0.01)
    inp['s5_lambda_im'] = (jnp.pi * jnp.arange(S5_STATE, dtype=f32)) + nrm(ks[12], (L, S5_NGROUPS, S5_STATE), 0.01)
    inp['s5_log_dt'] = uni(ks[13], (L, S5_NGROUPS), float(np.log(0.001)), float(np.log(0.1)))
    inp['s5_b_re'] = nrm(ks[14], (L, S5_NGROUPS, S5_STATE, S5_GROUP), (2 * S5_GROUP) ** -0.5)
    inp['s5_b_im'] = nrm(ks[15], (L, S5_NGROUPS, S5_STATE, S5_GROUP), (2 * S5_GROUP) ** -0.5)
    inp['s5_c_re'] = nrm(ks[16], (L, S5_NGROUPS, S5_GROUP, S5_STATE), (2 * S5_STATE) ** -0.5)
    inp['s5_c_im'] = nrm(ks[17], (L, S5_NGROUPS, S5_GROUP, S5_STATE), (2 * S5_STATE) ** -0.5)
    inp['s5_d'] = nrm(ks[18], (L, S5_WIDTH), 1.0)
    inp['s5_glu_w'] = nrm(ks[19], (L, S5_WIDTH, S5_WIDTH), S5_WIDTH ** -0.5)
    inp['s5_glu_b'] = nrm(ks[20], (L, S5_WIDTH), 0.01)
    inp['rwkv_mu'] = uni(ks[21], (L, 6, RWKV_WIDTH), 0.0, 1.0)
    inp['rwkv_w0'] = nrm(ks[22], (L, RWKV_WIDTH), 1.0)
    inp['rwkv_w1'] = nrm(ks[23], (L, RWKV_WIDTH, LORA_DECAY), RWKV_WIDTH ** -0.5)
    inp['rwkv_w2'] = nrm(ks[24], (L, LORA_DECAY, RWKV_WIDTH), 0.1)
    inp['rwkv_a0'] = nrm(ks[25], (L, RWKV_WIDTH), 0.1)
    inp['rwkv_a1'] = nrm(ks[26], (L, RWKV_WIDTH, LORA_AAA), RWKV_WIDTH ** -0.5)
    inp['rwkv_a2'] = nrm(ks[27], (L, LORA_AAA, RWKV_WIDTH), 0.1)
    inp['rwkv_g1'] = nrm(ks[28], (L, RWKV_WIDTH, LORA_GATE), RWKV_WIDTH ** -0.5)
    inp['rwkv_g2'] = nrm(ks[29], (L, LORA_GATE, RWKV_WIDTH), LORA_GATE ** -0.5)
    inp['rwkv_k_k'] = 0.85 + nrm(ks[30], (L, RWKV_WIDTH), 0.05)
    inp['rwkv_k_a'] = 1.0 + nrm(ks[31], (L, RWKV_WIDTH), 0.05)
    inp['rwkv_r_k'] = nrm(ks[32], (L, RWKV_HEADS, RWKV_HEAD), 0.1)
    inp['rwkv_ln_w'] = 1.0 + nrm(ks[33], (L, RWKV_WIDTH), 0.01)
    inp['rwkv_ln_b'] = nrm(ks[34], (L, RWKV_WIDTH), 0.01)
    inp['w_out'] = nrm(ks[35], (L, MIX_WIDTH, D_MODEL), MIX_WIDTH ** -0.5)
    inp['norm_ca_g'] = 1.0 + nrm(ks[36], (L, D_MODEL), 0.01)
    inp['norm_mem_g'] = 1.0 + nrm(ks[37], (L, D_MODEL), 0.01)
    inp['w_cq'] = nrm(ks[38], (L, D_MODEL, D_MODEL), D_MODEL ** -0.5)
    inp['w_mem_kv'] = nrm(ks[39], (L, D_MODEL, 2 * D_MODEL), D_MODEL ** -0.5)
    inp['w_co'] = nrm(ks[40], (L, D_MODEL, D_MODEL), D_MODEL ** -0.5)
    inp['norm_ffn_g'] = 1.0 + nrm(ks[41], (L, D_MODEL), 0.01)
    inp['router_w'] = nrm(ks[42], (L, D_MODEL, N_EXPERTS), D_MODEL ** -0.5)
    inp['router_b'] = nrm(ks[43], (L, N_EXPERTS), 0.01)
    inp['ex_w_gu'] = nrm(ks[44], (L, N_EXPERTS, D_MODEL, 2 * D_FF), D_MODEL ** -0.5)
    inp['ex_b_gu'] = nrm(ks[45], (L, N_EXPERTS, 2 * D_FF), 0.01)
    inp['ex_w_down'] = nrm(ks[46], (L, N_EXPERTS, D_FF, D_MODEL), D_FF ** -0.5)
    inp['ex_b_down'] = nrm(ks[47], (L, N_EXPERTS, D_MODEL), 0.01)
    inp['norm_final_g'] = 1.0 + nrm(ks[48], (D_MODEL,), 0.01)
    return inp

def reference(x_prompt, x_sample, mem_prompt, state_s5_re, state_s5_im, state_rwkv_shift, state_rwkv_wkv,
              cache_mem_k, cache_mem_v, norm_mix_g, w_in, s5_lambda_re, s5_lambda_im, s5_log_dt,
              s5_b_re, s5_b_im, s5_c_re, s5_c_im, s5_d, s5_glu_w, s5_glu_b, rwkv_mu, rwkv_w0, rwkv_w1,
              rwkv_w2, rwkv_a0, rwkv_a1, rwkv_a2, rwkv_g1, rwkv_g2, rwkv_k_k, rwkv_k_a, rwkv_r_k,
              rwkv_ln_w, rwkv_ln_b, w_out, norm_ca_g, norm_mem_g, w_cq, w_mem_kv, w_co, norm_ffn_g,
              router_w, router_b, ex_w_gu, ex_b_gu, ex_w_down, ex_b_down, norm_final_g):
    P = dict(norm_mix_g=norm_mix_g, w_in=w_in, s5_lambda_re=s5_lambda_re, s5_lambda_im=s5_lambda_im,
             s5_log_dt=s5_log_dt, s5_b_re=s5_b_re, s5_b_im=s5_b_im, s5_c_re=s5_c_re, s5_c_im=s5_c_im,
             s5_d=s5_d, s5_glu_w=s5_glu_w, s5_glu_b=s5_glu_b, rwkv_mu=rwkv_mu, rwkv_w0=rwkv_w0,
             rwkv_w1=rwkv_w1, rwkv_w2=rwkv_w2, rwkv_a0=rwkv_a0, rwkv_a1=rwkv_a1, rwkv_a2=rwkv_a2,
             rwkv_g1=rwkv_g1, rwkv_g2=rwkv_g2, rwkv_k_k=rwkv_k_k, rwkv_k_a=rwkv_k_a, rwkv_r_k=rwkv_r_k,
             rwkv_ln_w=rwkv_ln_w, rwkv_ln_b=rwkv_ln_b, w_out=w_out, norm_ca_g=norm_ca_g, w_cq=w_cq,
             w_co=w_co, norm_ffn_g=norm_ffn_g, router_w=router_w, router_b=router_b, ex_w_gu=ex_w_gu,
             ex_b_gu=ex_b_gu, ex_w_down=ex_w_down, ex_b_down=ex_b_down)
    bp = x_prompt.shape[0]
    hp = x_prompt
    hs = x_sample
    p_re, p_im, p_sh, p_wkv, p_mk, p_mv = [], [], [], [], [], []
    s_re, s_im, s_sh, s_wkv = [], [], [], []
    for l in range(DEPTH):
        mk, mv = memory_kv(mem_prompt, norm_mem_g[l], w_mem_kv[l])
        prev0 = jnp.zeros((bp, RWKV_IN), x_prompt.dtype)
        s00 = jnp.zeros((bp, RWKV_HEADS, RWKV_HEAD, RWKV_HEAD), jnp.float32)
        hp, re_p, im_p, sh_p, wkv_p = layer(hp, mk, mv, None, None, prev0, s00, P, l)
        p_re.append(re_p); p_im.append(im_p); p_sh.append(sh_p); p_wkv.append(wkv_p)
        p_mk.append(mk); p_mv.append(mv)
        hs, re_s, im_s, sh_s, wkv_s = layer(hs, cache_mem_k[l], cache_mem_v[l], state_s5_re[l], state_s5_im[l],
                                            state_rwkv_shift[l], state_rwkv_wkv[l], P, l)
        s_re.append(re_s); s_im.append(im_s); s_sh.append(sh_s); s_wkv.append(wkv_s)
    y_prompt = rmsnorm(hp, norm_final_g)
    y_sample = rmsnorm(hs, norm_final_g)
    prompt_s5_re = jnp.stack(p_re)
    prompt_s5_im = jnp.stack(p_im)
    prompt_rwkv_shift = jnp.stack(p_sh)
    prompt_rwkv_wkv = jnp.stack(p_wkv)
    prompt_mem_k = jnp.stack(p_mk)
    prompt_mem_v = jnp.stack(p_mv)
    sample_s5_re = jnp.stack(s_re)
    sample_s5_im = jnp.stack(s_im)
    sample_rwkv_shift = jnp.stack(s_sh)
    sample_rwkv_wkv = jnp.stack(s_wkv)
    return (y_prompt, y_sample, prompt_s5_re, prompt_s5_im, prompt_rwkv_shift, prompt_rwkv_wkv,
            prompt_mem_k, prompt_mem_v, sample_s5_re, sample_s5_im, sample_rwkv_shift, sample_rwkv_wkv)


_drawn_inputs = setup_inputs


def setup_inputs(seed=0):
    import zlib

    import numpy as np

    out = dict(_drawn_inputs(seed))
    spreads = {}
    factors = {'s5_lambda_re': 80.261,
     's5_glu_b': 6.893,
     'rwkv_ln_b': 2.865,
     'norm_ca_g': 3.722,
     'norm_mem_g': 5.457,
     'ex_b_gu': 8.0,
     'ex_b_down': 48.986,
     'norm_final_g': 200.0,
     'rwkv_k_k': 2.785,
     'rwkv_ln_w': 4.016,
     'norm_ffn_g': 3.49,
     'router_b': 3.231}
    for name, (base, spread) in spreads.items():
        noise = np.random.default_rng([zlib.crc32(name.encode()), seed]).standard_normal(out[name].shape)
        drawn = base * np.exp(spread * noise) if base else spread * noise
        out[name] = __import__('jax').numpy.asarray(drawn.astype(out[name].dtype))
    for name, factor in factors.items():
        out[name] = (out[name] * factor).astype(out[name].dtype)
    return out
```

```python
from contextlib import ExitStack

import numpy as np

import concourse.bass as bass
from concourse import mybir

F32 = mybir.dt.float32
U32 = mybir.dt.uint32
I32 = mybir.dt.int32
ALU = mybir.AluOpType
ACT = mybir.ActivationFunctionType
AX = mybir.AxisListType

P = 128
D = 1024
KT = D // P
TP, NB, TS = 256, 8, 8
T = TP + NB * TS
NM = 256
W5 = 512
CT = W5 // P
GC, NS = 16, 64
BL = 8
NBL = T // BL
PBL = TP // BL
PAIRS = 4
HN = 64
CH = 64
NC = T // CH
PC = TP // CH
MH, MD = 4, 256
NE, TOPK, FF = 32, 4, 1024
CAP = 64
PASSES = T // CAP
TT = 3
SCALE = MD ** -0.5
LIMIT, ALPHA = 7.0, 1.702
DECAY = 0.6065306597
RMS_EPS, GN_EPS = 1e-5, 64e-5
TWO_PI_HI, TWO_PI_LO = 6.28125, float(2 * np.pi - 6.28125)
ROUND = 12582912.0

VEC = {}
for _name, _n in (("norm_mix_g", 8), ("norm_ca_g", 8), ("norm_mem_g", 8), ("norm_ffn_g", 8), ("s5_d", 4), ("s5_glu_b", 4),
                  ("rwkv_mu", 24), ("rwkv_w0", 4), ("rwkv_a0", 4), ("rwkv_k_k", 4), ("rwkv_k_a", 4), ("rwkv_r_k", 4),
                  ("rwkv_ln_w", 4), ("rwkv_ln_b", 4), ("prev", 128)):
    VEC[_name] = (sum(n for _, n in VEC.values()), _n)
NVEC = sum(n for _, n in VEC.values())

CON = {}
for _name, _n in (("ident", 128), ("headones", 128), ("ones", 128), ("level", 6 * 64), ("strict", 128), ("incl", 128),
                  ("seqmask", 8), ("carry", T), ("window", T), ("iota", 128), ("earlier", 128), ("sign", 1),
                  ("ident64", 64), ("onerow", 64)):
    CON[_name] = (sum(n for _, n in CON.values()), _n)
NCON = sum(n for _, n in CON.values())

SMW = {}
for _name, _n in (("w1", 256), ("a1", 256), ("g1", 512), ("w2", 512), ("a2", 512), ("g2", 512), ("router_w", 256)):
    SMW[_name] = (sum(n for _, n in SMW.values()), _n)
NSMW = sum(n for _, n in SMW.values())

S5P = {}
for _name, _n in (("lr", 16), ("li", 16), ("dt", 16), ("br", 256), ("bi", 256), ("cr", 512), ("ci", 512), ("h0", 256)):
    S5P[_name] = (sum(n for _, n in S5P.values()), _n)
NS5P = sum(n for _, n in S5P.values())

CHUNK = 2048
SLOTS = 12
EARLY = 4
PRE = (["in"] * 10 + ["glu"] + ["memk"] * 4 + ["memv"] * 4 + ["out"] * 4 + ["cq"] * 4
       + ["kcache"] * 8 + ["vcache"] * 8 + ["co"] * 4)
NPRE = len(PRE)
MIXER_CHUNKS = 23
FIRST = {k: PRE.index(k) for k in dict.fromkeys(PRE)}


def _slots():
    order = [c % EARLY for c in range(MIXER_CHUNKS)]
    free = [s for s in range(EARLY, SLOTS)] + [order[-EARLY + i] for i in range(EARLY)]
    while len(order) < NPRE:
        s = free.pop(0)
        order.append(s)
        free.append(s)
    return order, free


SLOT, EXPERT_SLOT = _slots()
PREV = [max([b for b in range(c) if SLOT[b] == SLOT[c]], default=None) for c in range(NPRE)]
USES = [SLOT.count(s) for s in range(SLOTS)]
NTH = [SLOT[:c].count(SLOT[c]) for c in range(NPRE)]
EXPERT_CHUNKS = 12


class Regions:

    def __init__(self, at):
        self.at = at

    def take(self, n):
        self.at += n
        return self.at - n


LATE = EARLY * CHUNK
ROW = CT * T
RW = [LATE + ROW * i for i in range(12)]
SCAN = LATE + 12 * ROW
_keep = Regions(SLOTS * CHUNK)
XT, VECO, CONO, SMWO = (_keep.take(n) for n in (KT * T, NVEC, NCON, NSMW))
MK, MV, M0 = (_keep.take(2048) for _ in range(3))
WORK = _keep.at
_w = Regions(WORK)
N1, UWIN, FO, EO, S5O, PWO, UT = (_w.take(n) for n in (KT * T, 8 * T, 1024, 1024, NS5P, 448, CT * (T + 7)))
X0T, YL, KKO, MIX, PEND, SHIFT = (_w.take(n) for n in (T, T, 256, KT * T, 48, 144))
RW += [N1 + ROW * i for i in range(8)]
CAO = RW[10]
TOTAL = 53200
_w = Regions(WORK)
NT, QT, PROB, SPROB, PT, SPT, OT = (_w.take(n) for n in (KT * T, KT * T, 2048, 512, 2048, 512, KT * T))
QBLK = M0
RX, STAT = TOTAL - 400, TOTAL - 80
assert _w.at <= RX and SHIFT + 144 <= RX
HTOK, YACC = MK, MK + TT * D
_w = Regions(PROB)
(BIAS, XTE, HG, HU, SIG, HACT, ACTT, YB, SELG, SEL, GTT, TAB, CUR, GFIN, RB, SCR) = (
    _w.take(n) for n in (2 * FF, KT * CAP, 512, 512, 512, 512, 512, 512, TT * P, TT * CAP, TT * P, 6 * (NE + 1), 8, D, NE, 1200))
assert _w.at <= TOTAL
BDOWN = HG
assert SCAN + 1024 <= SLOTS * CHUNK and RW[19] + ROW <= X0T and _w.at <= TOTAL



def _tiles(kind, name, lo, hi):
    return [(kind, f"{name}{i}" if name else i) for i in range(lo, hi)]


IN_ORDER = "kzrv"
MIX_ORDER = ([("load", 0), ("load", 1), ("f", 0)] + _tiles("in", "k", 0, 4) + [("win", 0), ("par", 0)] + _tiles("in", "z", 0, 2)
             + [("f", 1), ("blk", 0), ("y", 0), ("win", 1)] + _tiles("in", "z", 2, 4)
             + [("mix", "k"), ("par", 1), ("load", 2), ("blk", 1), ("f", 2), ("y", 1)] + _tiles("in", "r", 0, 2)
             + [("mix", "z"), ("out", 0), ("win", 2)] + _tiles("in", "r", 2, 4)
             + [("par", 2), ("load", 3), ("blk", 2), ("f", 3), ("y", 2), ("mix", "r")] + _tiles("in", "v", 0, 2)
             + [("win", 3), ("out", 1), ("par", 3), ("blk", 3), ("y", 3)] + _tiles("in", "v", 2, 4)
             + [("mix", "v"), ("lora_up", 0), ("memk", 0), ("memk", 1), ("lora_down", 0), ("memk", 2), ("out", 2), ("memk", 3),
                ("knorm", 0), ("out", 3), ("glu", 0), ("memk", 4), ("memk", 5), ("memk", 6), ("memk", 7)])
TILES4 = range(4)


def rwkv_names():
    yield from [f"t{a}{i}" for i in TILES4 for a in "bvka"]
    yield from [f"g{a}{i}" for i in range(5) for a in "bk"]
    yield from [f"y0_{i}" for i in TILES4]
    for lv in range(1, 6):
        for i in TILES4:
            yield f"y{lv}_{i}"
        for i in TILES4:
            yield f"dt{lv}_{i}"
            if lv < 5:
                yield f"dx{lv}_{i}"
    for i in TILES4:
        yield from [f"gt{i}", f"bv{i}"]
    yield from [f"hh{i}" for i in TILES4]


MEM_V = [f"mv{q}{t}" for q in range(4) for t in range(2)]


def job_names():
    yield from ["ss_x", "ss_m"] + [f"u{i}" for i in TILES4]
    for kind, n in MIX_ORDER:
        if kind == "par":
            yield from [f"er{n}", f"ei{n}", f"kk{n}"]
        elif kind == "in":
            yield n
        elif kind == "blk":
            yield from [f"ve{n}", f"loc{n}"]
        elif kind == "out":
            yield f"st{n}"
        elif kind == "lora_up":
            yield from ["lw", "la", "lg"]
        elif kind == "lora_down":
            yield from [f"{a}{i}" for a in ("dw", "da", "dg") for i in TILES4]
        elif kind == "memk":
            yield f"mk{n}"
        elif kind == "knorm":
            yield from [f"kn{i}" for i in TILES4]
        elif kind == "glu":
            yield from [f"gl{i}" for i in TILES4]
    yield from [f"bo{i}" for i in TILES4]
    yield from rwkv_names()
    yield from MEM_V
    for c in range(PC):
        if c:
            yield f"u_{c}"
        yield from [f"m_{c}", f"yy{c}"]
    yield from [f"us{i}" for i in TILES4]
    yield from [f"ys{i}" for i in TILES4]
    yield from [f"sf{i}" for i in TILES4]
    yield from [f"me{i}" for i in TILES4]
    yield from [f"va{i}" for i in TILES4]
    yield from [f"o{n}" for n in range(8)]
    yield "ss_c"
    yield from [f"q{n}" for n in range(8)]
    yield from [f"sp{h}" for h in range(MH)]
    yield from [f"sb{i}" for i in range(2)]
    yield from [f"tp{i}" for i in range(4)]
    yield "tb"
    yield from [f"op{n}" for n in range(8)]
    yield from ["ob0", "ob1"]
    yield from [f"co{n}" for n in range(8)]
    yield "ss_f"
    yield from [f"th{t}{h}" for t in range(TT) for h in range(2)]
    yield from [f"tx{t}{h}" for t in range(TT) for h in range(2)]
    yield "lgt"
    yield from ["pos", "cnt", "gtr"]
    yield from [f"bd{t}{h}" for t in range(TT) for h in range(2)]


RWKV_JOBS = list(rwkv_names())
_units = [(job, k) for job in MEM_V for k in range(KT)]
FILL_AT = {job: _units[i * len(_units) // len(RWKV_JOBS):(i + 1) * len(_units) // len(RWKV_JOBS)] for i, job in enumerate(RWKV_JOBS)}
FILL_DONE = {job: [f for f, k in units if k == KT - 1] for job, units in FILL_AT.items()}


def _banks():
    job, uses, at = {}, [0] * 8, 0
    for name in job_names():
        assert name not in job
        if name in MEM_V:
            bank = 6 + MEM_V.index(name) % 2
        elif name in RWKV_JOBS:
            bank = RWKV_JOBS.index(name) % 6
        else:
            bank, at = at % 8, at + 1
        job[name] = (bank, uses[bank])
        uses[bank] += 1
    return job, uses


JOB, _uses = _banks()
BANK_USES = list(_uses)


LAST_JOB = (["u1", "u3"] + [f"{c}{i}" for c in IN_ORDER for i in (1, 3)] + ["gl3"] + [f"mk{i}" for i in (1, 3, 5, 7)]
            + [f"mv{q}1" for q in range(4)]
            + [f"o{i}" for i in (1, 3, 5, 7)] + [f"q{i}" for i in (1, 3, 5, 7)] + ["sb0"] * 4 + ["sb1"] * 4
            + ["ob0"] * 4 + ["ob1"] * 4 + [f"co{i}" for i in (1, 3, 5, 7)])
assert len(LAST_JOB) == NPRE


def build(nc, a, o):
    with ExitStack() as ctx:
        BIG = ctx.enter_context(nc.sbuf_tensor("big", [P, TOTAL], F32))
        ps = [ctx.enter_context(nc.psum_tensor(f"bank{i}", [P, 512], F32)) for i in range(8)]
        u_dram = nc.dram_tensor("u_windows", [W5, T + 7], F32)
        sems = {}

        def S(name):
            if name not in sems:
                sems[name] = ctx.enter_context(nc.semaphore(name))
            return sems[name]

        psum_full = [S(f"psum_full{i}") for i in range(8)]
        psum_free = [S(f"psum_free{i}") for i in range(8)]
        ring_full = [S(f"ring_full{i}") for i in range(SLOTS)]

        def view(at, *shape, lo=0, hi=P):
            n = int(np.prod(shape))
            v = BIG[lo:hi, at:at + n]
            names = "abcd"[:len(shape)]
            if len(shape) == 1:
                return v
            return v.rearrange(f"p ({' '.join(names)}) -> p {' '.join(names)}", **dict(zip(names, shape)))

        def con(name, lo=0, hi=P):
            at, n = CON[name]
            return BIG[lo:hi, CONO + at:CONO + at + n]

        def vec(name, i=0):
            at, _ = VEC[name]
            return BIG[:, VECO + at + i:VECO + at + i + 1]

        def smw(name, *shape):
            return view(SMWO + SMW[name][0], *shape)

        def s5p(name, *shape):
            return view(S5O + S5P[name][0], *shape)

        def over(ap, axis, n):
            v = ap.unsqueeze(axis)
            shape = list(v.shape)
            shape[axis] = n
            return v.to_broadcast(shape)

        class Steps:

            def __init__(self, eng, own):
                self.eng, self.own, self.count = eng, S(own), {}

            def __call__(self, ins, signal=None):
                sem = self.own if signal is None else S(signal)
                key = signal or ""
                self.count[key] = self.count.get(key, 0) + 1
                ins.then_inc(sem, 1)
                self.eng.wait_ge(sem, self.count[key])

            def read_out(self, ins, job):
                bank, n = JOB[job]
                ins.then_inc(psum_free[bank], 1)
                self.eng.wait_ge(psum_free[bank], n + 1)

        def computed(eng, job):
            bank, n = JOB[job]
            eng.wait_ge(psum_full[bank], n + 1)
            return ps[bank]

        def stored(eng, job):
            bank, n = JOB[job]
            eng.wait_ge(psum_free[bank], n + 1)

        xT, n1 = view(XT, KT, T), view(N1, KT, T)
        memT = view(M0, KT, NM)
        m0 = view(M0, CT, NB, HN)
        mkT, mv = view(MK, KT, NM), view(MV, 2, D)
        mix = view(MIX, KT, T)
        uT = view(UT, CT, T + 7)
        uwins = [view(at, 8, T) for at in (UWIN, RW[8])]
        F_r, F_i = (view(FO + 512 * i, PAIRS, P) for i in range(2))
        E_r, E_i = (view(EO + 512 * i, PAIRS, P) for i in range(2))
        ca_r, ca_i = (view(CAO + 1024 * i, PAIRS, BL, 32) for i in range(2))
        pw_r, pw_i = (view(PWO + 144 * i, BL + 1, 16) for i in range(2))
        x0 = view(X0T, 2, PAIRS, NBL)
        kkz = view(KKO, 8, 32)
        R = [view(at, CT, T) for at in RW]
        Rc = [view(at, CT, NC, CH) for at in RW]
        xsq, memsq = view(UWIN, KT, T), view(RW[8], KT, NM)
        prj = {"r": R[0], "k": R[1], "v": R[2], "z": R[3]}
        dlt = {"r": R[4], "k": R[5], "v": R[6], "z": R[7]}
        PRJ_ORDER = ("r", "k", "v", "z")
        hidden = {nm: view(RW[8] + i * T, T) for i, nm in enumerate(("dw", "da", "dg"))}
        cbd_r, cbd_i = s5p("cr", 16, 32), s5p("ci", 16, 32)
        xes = [view(SCAN + 320 * i, 2, PAIRS, NBL) for i in range(2)]
        w1, w2 = (view(CAO + 2048 + 256 * i, 2, PAIRS, PBL) for i in range(2))
        yl = [mix[:, CT + 1 + ct % 3, :] for ct in range(CT)]
        s5fin = view(MIX + CT * T, 2, 16, NB + 1)
        pend = view(PEND, CT, PC + NB)
        shift = view(SHIFT, 4, CT, NB + 1)
        ar = view(RW[10], CT, NC, 2, CH)
        bT, vT, kT, aT = Rc[3], Rc[4], Rc[9], Rc[12]
        AT, BT, C1, C2 = Rc[8], Rc[13], Rc[14], Rc[15]
        X, XI, Y, al = Rc[16], Rc[17], Rc[18], Rc[19]
        GT, BV, H, U = Rc[6], Rc[7], Rc[18], Rc[19]
        M = view(RW[16], PC, CT, HN)
        um, vm = (view(at, 2, NB * HN) for at in (RW[0], RW[17]))
        YT, ysq, gn = R[13], R[14], R[15]

        most_i32 = ctx.enter_context(nc.sbuf_tensor("most_tokens", [P, 1], I32))

        def most_tokens(eng):
            eng.wait_ge(S("counts"), 1)
            return eng.value_load(most_i32[0:1, 0:1], min_val=0, max_val=T)

        def all_passes(eng, expert, next_pass=None):
            with eng.Fori(0, NE) as e:
                expert(e, e)
            most = most_tokens(eng)
            with eng.Fori(1, PASSES) as p:
                with eng.If(most > p * CAP):
                    if next_pass:
                        next_pass(p)
                    with eng.Fori(0, NE) as e:
                        expert(p * NE + e, e)

        nT, qT, oT, rx2 = view(NT, KT, T), view(QT, KT, T), view(OT, KT, T), view(RX, T)
        prob, sprob = view(PROB, MH, 2, NM), view(SPROB, 2, NM)
        pT, spT = view(PT, MH, 2, TP), view(SPT, 2, 2, P)
        qblk = view(QBLK, KT, NB, MH * TS)
        hT, htok, yacc = view(QT, KT, T), view(HTOK, TT, D), view(YACC, TT, D)
        bias, xte = view(BIAS, 2 * FF), view(XTE, KT, CAP)
        hg, hu, sig, hact = (view(x, 512) for x in (HG, HU, SIG, HACT))
        actT, yb = view(ACTT, 4, P), view(YB, 512)
        selg, sel, gtt = view(SELG, TT, P), view(SEL, TT, CAP), view(GTT, TT, P)
        tab, cur = view(TAB, NE + 1, 6), view(CUR, 8)
        gfin, rbias, bdown = view(GFIN, D), view(RB, NE), view(BDOWN, D, hi=NE)
        logit, mask, gate = (view(SCR + 96 * i, TT, NE) for i in range(3))
        top, idx = view(SCR + 288, TT, 8), view(SCR + 312, TT, 8)
        idx_u = idx.bitcast(U32)
        idxf, g4, gsum = view(SCR + 336, TT, 8), view(SCR + 360, TT, 4), view(SCR + 372, TT)
        eq, eg = view(SCR + 384, TT, NE), view(SCR + 480, TT, NE)
        gtr = view(SCR + 600, TT * P, hi=NE)
        tile_rows = [P, P, T - 2 * P]

        block = ctx.enter_context(nc.Block())

        @block.sync
        def _(sp):
            sp.dma_start(view(S5O, NS5P), a["s5p"]).then_inc(S("s5p_in"), 16)
            sp.dma_start(view(VECO, NVEC), a["vecs"]).then_inc(S("vecs_in"), 16)
            sp.dma_start(view(CONO, NCON), a["consts"]).then_inc(S("consts_in"), 16)
            sp.dma_start(xT, a["xT"]).then_inc(S("x_in"), 16)
            sp.dma_start(memT, a["memT"]).then_inc(S("mem_in"), 16)
            sp.dma_start(view(SMWO, NSMW), a["smw"]).then_inc(S("smw_in"), 16)
            for c in range(NPRE):
                if c == FIRST["out"]:
                    computed(sp, MEM_V[-1])
                    sp.dma_start(m0, a["m0"]).then_inc(S("m0_in"), 16)
                if SLOT[c] >= EARLY and PREV[c] is None:
                    sp.wait_ge(S("mix_ready"), CT)
                if PREV[c] is not None:
                    computed(sp, LAST_JOB[PREV[c]])
                sp.dma_start(view(SLOT[c] * CHUNK, CHUNK), a["dense"][c]).then_inc(ring_full[SLOT[c]], 16)

            def expert_chunk(j, e):
                return a["w_gu"][e, j * P:(j + 1) * P, :] if j < 8 else \
                    a["w_down"][e, (j - 8) * 2 * P:(j - 7) * 2 * P, :].rearrange("(i p) n -> p i n", i=2)

            def expert_dst(j):
                at = EXPERT_SLOT[j] * CHUNK
                return view(at, CHUNK) if j < 8 else view(at, 2, D)

            for j in range(EXPERT_CHUNKS):
                computed(sp, LAST_JOB[NPRE - EXPERT_CHUNKS + j])
                sp.dma_start(expert_dst(j), expert_chunk(j, 0)).then_inc(ring_full[EXPERT_SLOT[j]], 16)
            sp.wait_ge(S("bias_zero"), 1)
            sp.dma_start(BIG[0:1, BIAS:BIAS + 2 * FF], a["b_gu"][0:1, :]).then_inc(S("bias_in"), 16)

            def load_expert(it, e):
                for j in range(EXPERT_CHUNKS):
                    if j == 7:
                        sp.wait_ge(psum_full[1], it + BANK_USES[1])
                    elif j == 11:
                        sp.wait_ge(psum_full[4], it * 2 + (BANK_USES[4] - 1))
                    else:
                        sp.wait_ge(S("chunk_used"), it * 10 + ((j if j < 7 else j - 1) - 9))
                    sp.dma_start(expert_dst(j), expert_chunk(j, e)).then_inc(ring_full[EXPERT_SLOT[j]], 16)
                    if j == 0:
                        sp.wait_ge(S("bias_used"), it)
                        sp.dma_start(BIG[0:1, BIAS:BIAS + 2 * FF], a["b_gu"][bass.ds(e, 1), :]).then_inc(S("bias_in"), 16)

            with sp.Fori(1, NE) as e:
                load_expert(e, e)
            most = most_tokens(sp)
            with sp.Fori(1, PASSES) as p:
                with sp.If(most > p * CAP):
                    with sp.Fori(0, NE) as e:
                        load_expert(p * NE + e, e)
            sp.wait_ge(S("final"), TT)
            sp.dma_start(o["y"], view(HTOK, TT, D)).then_inc(S("y_out"), 16)
            sp.wait_ge(S("stores"), 16 * 3)
            sp.wait_ge(S("wkv_p_stored"), 16)
            sp.wait_ge(S("wkv_stored"), 16)
            sp.wait_ge(S("s5_stored"), 16)
            sp.wait_ge(S("y_out"), 16)

        @block.tensor
        def _(pe):
            def start_job(job):
                for filler, k in FILL_AT.get(job, ()):
                    mem_v(filler, k)
                bank, n = JOB[job]
                if n:
                    pe.wait_ge(psum_free[bank], n)
                return ps[bank]

            def end_job(ins, job):
                ins.then_inc(psum_full[JOB[job][0]], 1)

            def chunk(c, *shape):
                pe.wait_ge(ring_full[SLOT[c]], 16 * (NTH[c] + 1))
                return view(SLOT[c] * CHUNK, *shape)

            mm = nc.tensor.matmul

            def sums(job, src, n, ones):
                b = start_job(job)
                for k in range(KT):
                    last = mm(b[:, 0:n], ones, src[:, k, :], start=(k == 0), stop=(k == KT - 1))
                end_job(last, job)

            def dense(job, w, src, n, kt=KT):
                b = start_job(job)
                for k in range(kt):
                    last = mm(b[:, 0:n], w[:, k, :], src[:, k, :], start=(k == 0), stop=(k == kt - 1))
                end_job(last, job)

            def dense_stream(first, i, job, src, n):
                dense(job, chunk(first + i // 2, 2, KT, P)[:, i % 2], src, n)

            pe.wait_ge(S("consts_in"), 16)
            ones, ident, headones = con("ones"), con("ident"), con("headones")
            pe.wait_ge(S("xsq"), KT)
            sums("ss_x", xsq, T, ones)
            pe.wait_ge(S("memsq"), 1)
            sums("ss_m", memsq, NM, ones)
            pe.wait_ge(S("n1"), KT)
            for i in TILES4:
                dense_stream(FIRST["in"], i, f"u{i}", n1, T)

            def s5_params(ct):
                pe.wait_ge(S("s5_f"), ct + 1)
                for nm, src in (("er", F_r), ("ei", F_i)):
                    b = start_job(f"{nm}{ct}")
                    for q in range(PAIRS):
                        last = nc.tensor.transpose(b[:, q * P:(q + 1) * P], src[:, q, :], ident)
                    end_job(last, f"{nm}{ct}")
                b = start_job(f"kk{ct}")
                for q in range(PAIRS):
                    mm(b[:, 32 * q:32 * q + 32], F_r[:, q, :], cbd_r[:, PAIRS * ct + q, :], start=True, stop=False)
                    last = mm(b[:, 32 * q:32 * q + 32], F_i[:, q, :], cbd_i[:, PAIRS * ct + q, :], start=False, stop=True)
                end_job(last, f"kk{ct}")

            def s5_block(ct):
                pe.wait_ge(S("uwin"), ct + 1)
                uwin = uwins[ct % 2]
                stored(pe, f"ei{ct}")
                b = start_job(f"ve{ct}")
                for q in range(PAIRS):
                    for g in range(2):
                        for ri, e in ((0, E_r), (1, E_i)):
                            at = (ri * PAIRS + q) * NBL
                            last = mm(b[64 * g:64 * g + 64, at:at + NBL], e[:, q, 64 * g:64 * g + 64],
                                      uwin[:, 2 * q + g, BL - 1::BL], start=True, stop=True)
                end_job(last, f"ve{ct}")
                stored(pe, f"kk{ct}")
                b = start_job(f"loc{ct}")
                for g in range(2):
                    for q in range(PAIRS):
                        last = mm(b[32 * q:32 * q + 32, 0:T], kkz[:, 2 * q + g, :], uwin[:, 2 * q + g, :],
                                  start=(g == 0), stop=(g == 1))
                end_job(last, f"loc{ct}")

            def s5_out(ct):
                pe.wait_ge(S("s5_ca"), ct + 1)
                pe.wait_ge(S("s5_x0"), ct + 1)
                b = start_job(f"st{ct}")
                for j in range(BL):
                    for ri, c in ((0, ca_r), (1, ca_i)):
                        for q in range(PAIRS):
                            last = mm(b[32 * q:32 * q + 32, j * NBL:(j + 1) * NBL], c[:, q, BL - 1 - j, :], x0[:, ri, q, :],
                                      start=(ri == 0), stop=(ri == 1))
                end_job(last, f"st{ct}")

            def mem_k(i):
                pe.wait_ge(S("nmem"), KT)
                dense_stream(FIRST["memk"], i, f"mk{i}", memT, NM)

            def mem_v(job, k):
                q, t = int(job[2]), int(job[3])
                b = start_job(job) if k == 0 else ps[JOB[job][0]]
                ins = mm(b[:, 0:256], memT[:, k, t * P:(t + 1) * P], chunk(FIRST["memv"] + q, KT, 256)[:, k, :],
                         start=(k == 0), stop=(k == KT - 1))
                if k == KT - 1:
                    end_job(ins, job)

            def lora_up():
                pe.wait_ge(S("smw_in"), 16)
                pe.wait_ge(S("z_mixed"), 12)
                for job, w, n, src in (("lw", smw("w1", CT, 64), 64, R[4]), ("la", smw("a1", CT, 64), 64, R[5]),
                                       ("lg", smw("g1", CT, P), P, R[6])):
                    b = start_job(job)
                    for k in range(CT):
                        last = mm(b[0:n, 0:T], w[:, k, :], src[:, k, :], start=(k == 0), stop=(k == CT - 1))
                    end_job(last, job)

            def lora_down():
                for nm, up, w, n in (("dw", "lw", "w2", 64), ("da", "la", "a2", 64), ("dg", "lg", "g2", P)):
                    stored(pe, up)
                    for i in TILES4:
                        b = start_job(f"{nm}{i}")
                        end_job(mm(b[:, 0:T], smw(w, CT, P)[0:n, i, :], hidden[nm][0:n, :], start=True, stop=True), f"{nm}{i}")

            def head_sums(nm, src, ready=None, each=0):
                for i in TILES4:
                    if ready:
                        pe.wait_ge(S(ready), 1 + i * each)
                    b = start_job(f"{nm}{i}")
                    end_job(mm(b[:, 0:T], headones, src[:, i, :], start=True, stop=True), f"{nm}{i}")

            for kind, n in MIX_ORDER:
                if kind == "in":
                    dense_stream(FIRST["in"] + 2 + 2 * IN_ORDER.index(n[0]), int(n[1]), n, n1, T)
                elif kind == "par":
                    s5_params(n)
                elif kind == "blk":
                    s5_block(n)
                elif kind == "out":
                    s5_out(n)
                elif kind == "lora_up":
                    lora_up()
                elif kind == "lora_down":
                    lora_down()
                elif kind == "memk":
                    mem_k(n)
                elif kind == "knorm":
                    head_sums("kn", R[6], "kk_squares")
                elif kind == "glu":
                    pe.wait_ge(S("s5_gelu"), CT)
                    w = chunk(FIRST["glu"], CT, CT, P)
                    for i in TILES4:
                        dense(f"gl{i}", w[:, i], mix, T, kt=CT)

            halves = [(0, slice(0, 64)), (1, slice(64, 128))]
            head_sums("bo", R[8], "rkr")
            pe.wait_ge(S("rw_keys"), 4)
            for i in TILES4:
                for nm, src in (("b", Rc[6]), ("v", Rc[2]), ("k", Rc[7]), ("a", ar[:, :, :, 0, :])):
                    b = start_job(f"t{nm}{i}")
                    for c in range(NC):
                        for _, h in halves:
                            last = mm(b[h, c * CH:(c + 1) * CH], src[h, i, c, :], con("ident64")[h, :], start=True, stop=True)
                    end_job(last, f"t{nm}{i}")
            for i in range(5):
                for nm, src in (("b", Rc[6]), ("k", Rc[7])):
                    b = start_job(f"g{nm}{i}")
                    for n in range(4):
                        t, c = (i, n) if i < 4 else (n, PC)
                        for _, h in halves:
                            last = mm(b[h, n * P:(n + 1) * P], src[h, t, c, :],
                                      ar[h, t, c, :, :].rearrange("p a b -> p (a b)"), start=True, stop=True)
                    end_job(last, f"g{nm}{i}")
            for i in TILES4:
                pe.wait_ge(S("a_level"), i + 1)
                b = start_job(f"y0_{i}")
                for c in range(NC):
                    for _, h in halves:
                        last = mm(b[h, c * CH:(c + 1) * CH], al[h, i, c, :], con("ident64")[h, :], start=True, stop=True)
                end_job(last, f"y0_{i}")
            for lv in range(1, 6):
                n = NC if lv < 3 else PC
                for i in TILES4:
                    pe.wait_ge(S("a_level"), 4 * lv + i + 1)
                    b = start_job(f"y{lv}_{i}")
                    for c in range(n):
                        for _, h in halves:
                            last = mm(b[h, c * CH:(c + 1) * CH], al[h, i, c, :], X[h, i, c, :], start=True, stop=True)
                    end_job(last, f"y{lv}_{i}")
                for i in TILES4:
                    stored(pe, f"y{lv}_{i}")
                    for job, lhs, rhs in ((f"dt{lv}_{i}", Y, XI), (f"dx{lv}_{i}", XI, Y))[:2 if lv < 5 else 1]:
                        b = start_job(job)
                        for c in range(n):
                            for _, h in halves:
                                last = mm(b[h, c * CH:(c + 1) * CH], lhs[h, i, c, :], rhs[h, i, c, :], start=True, stop=True)
                        end_job(last, job)
            for i in TILES4:
                stored(pe, f"dt5_{i}")
                for job, lhs, rhs in ((f"gt{i}", aT, XI), (f"bv{i}", BT, vT)):
                    b = start_job(job)
                    for c in range(NC):
                        for _, h in halves:
                            last = mm(b[h, c * CH:(c + 1) * CH], lhs[h, i, c, :], rhs[h, i, c, :], start=True, stop=True)
                    end_job(last, job)
            for i in TILES4:
                stored(pe, f"bv{i}")
                b = start_job(f"hh{i}")
                for c in range(NC):
                    for _, h in halves:
                        last = mm(b[h, c * CH:(c + 1) * CH], XI[h, i, c, :], BV[h, i, c, :], start=True, stop=True)
                end_job(last, f"hh{i}")
            pe.wait_ge(S("u_first"), 1)
            for c in range(PC):
                if c:
                    stored(pe, f"m_{c - 1}")
                    if c > 1:
                        pe.wait_ge(S("m_ready"), c - 1)
                    b = start_job(f"u_{c}")
                    for i in TILES4:
                        for _, h in halves:
                            last = mm(b[h, i * HN:(i + 1) * HN], GT[h, i, c, :], M[h, c - 1, i, :], start=True, stop=True)
                    end_job(last, f"u_{c}")
                    stored(pe, f"u_{c}")
                b = start_job(f"m_{c}")
                for i in TILES4:
                    for _, h in halves:
                        mm(b[h, i * HN:(i + 1) * HN], kT[h, i, c, :], vT[h, i, c, :], start=True, stop=False)
                        last = mm(b[h, i * HN:(i + 1) * HN], bT[h, i, c, :], U[h, i, c, :], start=False, stop=True)
                end_job(last, f"m_{c}")
                b = start_job(f"yy{c}")
                for i in TILES4:
                    for _, h in halves:
                        mm(b[h, i * CH:(i + 1) * CH], vT[h, i, c, :], C2[h, i, c, :], start=True, stop=False)
                        last = mm(b[h, i * CH:(i + 1) * CH], U[h, i, c, :], C1[h, i, c, :], start=False, stop=(c == 0))
                        if c:
                            last = mm(b[h, i * CH:(i + 1) * CH], M[h, c - 1, i, :], ar[h, i, c, 1, :], start=False, stop=True)
                end_job(last, f"yy{c}")
            pe.wait_ge(S("m0_in"), 16)
            for i in TILES4:
                b = start_job(f"us{i}")
                for _, h in halves:
                    last = mm(b[h, :], GT[h, i, PC, :], m0[h, i].rearrange("p a b -> p (a b)"), start=True, stop=True)
                end_job(last, f"us{i}")
            for i in TILES4:
                pe.wait_ge(S("u_sample"), i + 1)
                b = start_job(f"ys{i}")
                for _, h in halves:
                    mm(b[h, 0:CH], vT[h, i, PC, :], C2[h, i, PC, :], start=True, stop=False)
                    mm(b[h, 0:CH], U[h, i, PC, :], C1[h, i, PC, :], start=False, stop=False)
                    for s in range(NB):
                        last = mm(b[h, s * TS:(s + 1) * TS], m0[h, i, s, :], ar[h, i, PC, 1, s * TS:(s + 1) * TS],
                                  start=False, stop=(s == NB - 1))
                end_job(last, f"ys{i}")
            for i in TILES4:
                pe.wait_ge(S("uv_masked"), i + 1)
                b = start_job(f"sf{i}")
                for _, h in halves:
                    mm(b[h, :], kT[h, i, PC, :], vm[h, i % 2, :], start=True, stop=False)
                    last = mm(b[h, :], bT[h, i, PC, :], um[h, i % 2, :], start=False, stop=True)
                end_job(last, f"sf{i}")
            stored(pe, "ys3")
            head_sums("me", YT)
            head_sums("va", ysq, "y_squares", each=1)

            pe.wait_ge(S("mix_ready"), CT)
            for n in range(KT):
                dense_stream(FIRST["out"], n, f"o{n}", mix, T)

            pe.wait_ge(S("x1sq"), KT)
            sums("ss_c", qT, T, ones)
            pe.wait_ge(S("nca"), KT)
            for n in range(KT):
                dense_stream(FIRST["cq"], n, f"q{n}", nT, T)
            stored(pe, "q7")
            stored(pe, "mk7")
            for job in MEM_V[-2:]:
                stored(pe, job)
            for h in range(MH):
                b = start_job(f"sp{h}")
                for t in range(2):
                    for i in range(2):
                        last = mm(b[:, t * NM:(t + 1) * NM], qT[:, 2 * h + i, t * P:(t + 1) * P], mkT[:, 2 * h + i, :],
                                  start=(i == 0), stop=(i == 1))
                end_job(last, f"sp{h}")
            pe.wait_ge(S("qblk"), MH)
            for g in range(2):
                b = start_job(f"sb{g}")
                for n in range(KT):
                    for i in range(4):
                        s = 4 * g + i
                        w = chunk(FIRST["kcache"] + s, KT, NM)
                        last = mm(b[32 * i:32 * i + 32, 0:NM], qblk[:, n, s, :], w[:, n, :], start=(n == 0), stop=(n == KT - 1))
                end_job(last, f"sb{g}")
            for h in range(MH):
                pe.wait_ge(S("prob"), h + 1)
                b = start_job(f"tp{h}")
                for m in range(2):
                    for t in range(2):
                        last = nc.tensor.transpose(b[:, (2 * m + t) * P:(2 * m + t + 1) * P], prob[:, h, t, m * P:(m + 1) * P], ident)
                end_job(last, f"tp{h}")
            pe.wait_ge(S("prob"), MH + 2)
            b = start_job("tb")
            for g in range(2):
                for m in range(2):
                    last = nc.tensor.transpose(b[:, (2 * g + m) * P:(2 * g + m + 1) * P], sprob[:, g, m * P:(m + 1) * P], ident)
            end_job(last, "tb")
            for n in range(KT):
                stored(pe, f"tp{n // 2}")
                b = start_job(f"op{n}")
                for m in range(2):
                    last = mm(b[:, 0:TP], mv[:, m, n * P:(n + 1) * P], pT[:, n // 2, m, :], start=(m == 0), stop=(m == 1))
                end_job(last, f"op{n}")
            stored(pe, "tb")
            for g in range(2):
                b = start_job(f"ob{g}")
                for i in range(4):
                    w = chunk(FIRST["vcache"] + 4 * g + i, 2, D)
                    for n in range(KT):
                        at, col = n * 32 + i * TS, i * 32 + (n // 2) * TS
                        for m in range(2):
                            last = mm(b[:, at:at + TS], w[:, m, n * P:(n + 1) * P], spT[:, g, m, col:col + TS], start=(m == 0), stop=(m == 1))
                end_job(last, f"ob{g}")
            stored(pe, "ob1")
            for n in range(KT):
                dense_stream(FIRST["co"], n, f"co{n}", oT, T)

            pe.wait_ge(S("x2sq"), KT)
            sums("ss_f", nT, T, ones)
            pe.wait_ge(S("nff"), KT)
            for nm, src in (("th", hT), ("tx", xT)):
                for t in range(TT):
                    for h in range(2):
                        b = start_job(f"{nm}{t}{h}")
                        for i in range(4):
                            last = nc.tensor.transpose(b[0:tile_rows[t], i * P:(i + 1) * P], src[:, 4 * h + i, t * P:t * P + tile_rows[t]], ident)
                        end_job(last, f"{nm}{t}{h}")
            b = start_job("lgt")
            for t in range(TT):
                for k in range(KT):
                    last = mm(b[0:tile_rows[t], t * NE:(t + 1) * NE], hT[:, k, t * P:t * P + tile_rows[t]], smw("router_w", KT, NE)[:, k, :],
                              start=(k == 0), stop=(k == KT - 1))
            end_job(last, "lgt")
            pe.wait_ge(S("mask"), 1)
            b = start_job("pos")
            for t in range(TT):
                for s in range(t + 1):
                    last = mm(b[:, t * NE:(t + 1) * NE], con("earlier") if s == t else ones, mask[:, s, :], start=(s == 0), stop=(s == t))
            end_job(last, "pos")
            b = start_job("cnt")
            for s in range(TT):
                last = mm(b[:, 0:NE], ones, mask[:, s, :], start=(s == 0), stop=(s == TT - 1))
            end_job(last, "cnt")
            pe.wait_ge(S("gates"), 1)
            b = start_job("gtr")
            for t in range(TT):
                last = nc.tensor.transpose(b[0:NE, t * P:(t + 1) * P], gate[:, t, :], ident)
            end_job(last, "gtr")
            stored(pe, "gtr")
            pe.wait_ge(S("bdown_in"), 16)
            for t in range(TT):
                for h in range(2):
                    b = start_job(f"bd{t}{h}")
                    end_job(mm(b[:, :], gtr[:, t * P:(t + 1) * P], bdown[:, h * 512:h * 512 + 512], start=True, stop=True), f"bd{t}{h}")

            def gather():
                for k in range(KT):
                    for t in range(TT):
                        last = mm(ps[2][:, k * CAP:(k + 1) * CAP], htok[:, t, k * P:(k + 1) * P], sel[:, t, :],
                                  start=(t == 0), stop=(t == TT - 1))
                last.then_inc(psum_full[2], 1)

            sides = [(0, slice(0, CAP)), (1, slice(CAP, 2 * CAP))]
            pe.wait_ge(psum_free[2], BANK_USES[2])
            pe.wait_ge(S("selected"), 1)
            stored(pe, "th21")
            gather()

            def expert(it, e):
                for bank in (0, 1):
                    pe.wait_ge(psum_free[bank], it + BANK_USES[bank])
                pe.wait_ge(S("bias_in"), it * 16 + 16)
                for bank in (0, 1):
                    for s, part in sides:
                        last = mm(ps[bank][part, :], con("onerow"), bias[:, bank * FF + s * 512:bank * FF + s * 512 + 512], start=True, stop=False)
                last.then_inc(S("bias_used"), 1)
                pe.wait_ge(psum_free[2], it + (BANK_USES[2] + 1))
                for k in range(KT):
                    slot = EXPERT_SLOT[k]
                    pe.wait_ge(ring_full[slot], it * 16 + 16 * (USES[slot] + 1))
                    w = view(slot * CHUNK, CHUNK)
                    for bank in (0, 1):
                        for s, part in sides:
                            at = bank * FF + s * 512
                            last = mm(ps[bank][part, :], xte[:, k, :], w[:, at:at + 512], start=False, stop=(k == KT - 1))
                        if k == KT - 1:
                            last.then_inc(psum_full[bank], 1)
                    if k < KT - 1:
                        last.then_inc(S("chunk_used"), 1)
                pe.wait_ge(psum_free[5], it + BANK_USES[5])
                pe.wait_ge(S("weighted"), it + 1)
                for t in range(TT):
                    last = nc.tensor.transpose(ps[5][:, t * P:(t + 1) * P], selg[:, t, :], ident)
                last.then_inc(psum_full[5], 1)
                pe.wait_ge(S("selected"), it + 2)
                gather()
                pe.wait_ge(psum_free[3], it * 2 + BANK_USES[3])
                pe.wait_ge(S("activated"), it + 1)
                for k in range(4):
                    last = nc.tensor.transpose(ps[3][:, k * P:(k + 1) * P], hact[:, k * P:(k + 1) * P], ident)
                last.then_inc(psum_full[3], 1)
                pe.wait_ge(psum_free[3], it * 2 + (BANK_USES[3] + 1))
                pe.wait_ge(psum_free[4], it * 2 + BANK_USES[4])
                for k in range(KT):
                    slot = EXPERT_SLOT[8 + k // 2]
                    if k % 2 == 0:
                        pe.wait_ge(ring_full[slot], it * 16 + 16 * (USES[slot] + 1))
                    w = view(slot * CHUNK, 2, D)
                    for s, part in sides:
                        last = mm(ps[4][part, :], actT[:, k % 4, (k // 4) * CAP:(k // 4 + 1) * CAP], w[:, k % 2, s * 512:s * 512 + 512],
                                  start=(k == 0), stop=(k == KT - 1))
                    if k == KT - 1:
                        last.then_inc(psum_full[4], 1)
                    elif k % 2:
                        last.then_inc(S("chunk_used"), 1)
                pe.wait_ge(psum_free[4], it * 2 + (BANK_USES[4] + 1))
                pe.wait_ge(psum_free[5], it + (BANK_USES[5] + 1))
                for t, banks, at in ((0, (6, 7), 0), (1, (3, 4), 1), (2, (6, 7), 1)):
                    for bank in banks:
                        pe.wait_ge(psum_free[bank], it * 2 + (BANK_USES[bank] + at))
                    for s, part in sides:
                        mm(ps[banks[s]][:, :], gtt[part, t, :], yb[part, :], start=True, stop=True).then_inc(psum_full[banks[s]], 1)

            all_passes(pe, expert)

        @block.scalar
        def _(act):
            step = Steps(act, "act_steps")
            af = nc.scalar.activation
            act.wait_ge(S("x_in"), 16)
            for k in range(KT):
                step(af(xsq[:, k, :], xT[:, k, :], ACT.Square), "xsq")
            stored(act, "ss_x")
            step(af(view(YL, T), view(YL, T), ACT.Sqrt), "rx_sqrt")
            stored(act, "ss_m")
            step(af(view(KKO, NM), view(KKO, NM), ACT.Sqrt), "rm_sqrt")
            act.wait_ge(S("s5p_in"), 16)
            step(af(s5p("dt", 16), s5p("dt", 16), ACT.Exp), "s5_dt")
            act.wait_ge(S("s5_mag_arg"), 1)
            step(af(view(SCAN, 16), view(SCAN, 16), ACT.Exp), "s5_mag")
            act.wait_ge(S("s5_angles"), 1)
            step(af(view(SCAN + 32, 32), view(SCAN + 32, 32), ACT.Sin), "s5_sincos")

            def copy(dst, job, src=None):
                b = computed(act, job)
                step.read_out(af(dst, b[:, 0:T] if src is None else src(b), ACT.Identity), job)

            for i in TILES4:
                copy(uT[:, i, 7:], f"u{i}")
            act.wait_ge(S("u_pad"), 1)
            act.dma_start(u_dram.ap().rearrange("(c p) t -> p c t", p=P), uT).then_inc(S("u_stored"), 16)

            def s5_params(ct):
                copy(E_r, f"er{ct}", lambda b: b[:, :].rearrange("p (q n) -> p q n", q=PAIRS))
                copy(E_i, f"ei{ct}", lambda b: b[:, :].rearrange("p (q n) -> p q n", q=PAIRS))
                if ct == 0:
                    act.wait_ge(S("kk_zero"), 1)
                b = computed(act, f"kk{ct}")[:, 0:128].rearrange("p (q n) -> p q n", q=PAIRS)
                dst = view(KKO, PAIRS, 2, 32)
                step(af(dst[:, :, 0, 0:16], b[:, :, 0:16], ACT.Identity))
                step.read_out(af(dst[:, :, 1, 16:32], b[:, :, 16:32], ACT.Identity), f"kk{ct}")

            def load_windows(ct):
                if ct >= 2:
                    computed(act, f"loc{ct - 2}")
                for tap in range(BL):
                    src = bass.AP(u_dram, ct * P * (T + 7) + tap, [[T + 7, GC], [GC * (T + 7), 8], [1, T]])
                    act.dma_start(uwins[ct % 2][tap * GC:(tap + 1) * GC], src).then_inc(S(f"uwin_in{ct % 2}"), 16)

            act.wait_ge(S("u_stored"), 16)
            for kind, n in MIX_ORDER:
                if kind == "in":
                    copy(prj[n[0]][:, int(n[1]), :], n)
                elif kind == "par":
                    s5_params(n)
                elif kind == "load":
                    load_windows(n)
                elif kind == "blk":
                    if n >= 2:
                        act.wait_ge(S("s5_x0"), n - 1)
                    copy(xes[n % 2], f"ve{n}", lambda b: b[:, 0:2 * PAIRS * NBL].rearrange("p (r q n) -> p r q n", r=2, q=PAIRS))
                elif kind == "out":
                    act.wait_ge(S("gelu_arg"), n + 1)
                    step(af(mix[:, n, :], mix[:, n, :], ACT.Tanh, scale=float(np.sqrt(2 / np.pi))), "gelu_tanh")
                elif kind == "lora_up":
                    for job, dst, rows, fn in (("lw", hidden["dw"], 64, ACT.Tanh), ("la", hidden["da"], 64, ACT.Identity),
                                               ("lg", hidden["dg"], P, ACT.Sigmoid)):
                        b = computed(act, job)
                        step.read_out(af(dst[0:rows, :], b[0:rows, 0:T], fn), job)
                elif kind == "lora_down":
                    for i in TILES4:
                        b = computed(act, f"dw{i}")
                        step.read_out(af(R[3][:, i, :], b[:, 0:T], ACT.Sigmoid, bias=vec("rwkv_w0", i)), f"dw{i}")
                    act.wait_ge(S("delta_free"), 1)
                    for i in TILES4:
                        b = computed(act, f"da{i}")
                        step.read_out(af(R[7][:, i, :], b[:, 0:T], ACT.Sigmoid, bias=vec("rwkv_a0", i)), f"da{i}")
                    for i in TILES4:
                        copy(R[5][:, i, :], f"dg{i}")
                    step(af(R[3], R[3], ACT.Exp, scale=-DECAY), "decay")
                elif kind == "memk":
                    copy(mkT[:, n, :], f"mk{n}", lambda b: b[:, 0:NM])
                elif kind == "knorm":
                    stored(act, "kn3")
                    step(af(R[9], R[9], ACT.Sqrt), "kk_norm")
                elif kind == "glu":
                    for i in TILES4:
                        b = computed(act, f"gl{i}")
                        step.read_out(af(view(UWIN, CT, T)[:, i, :], b[:, 0:T], ACT.Sigmoid, bias=vec("s5_glu_b", i)), f"gl{i}")
            act.dma_start(o["mem_k"], mkT).then_inc(S("stores"), 16)
            act.wait_ge(S("s5_final"), CT)
            act.dma_start(o["s5"], s5fin).then_inc(S("s5_stored"), 16)
            act.wait_ge(S("shifts"), 4)
            act.dma_start(o["shift"], shift).then_inc(S("stores"), 16)
            reached = [0]

            def rwkv_copy(dst, job, n):
                while reached[0] <= RWKV_JOBS.index(job):
                    for f in FILL_DONE[RWKV_JOBS[reached[0]]]:
                        copy(mv[:, int(f[3]), int(f[2]) * 256:int(f[2]) * 256 + 256], f, lambda b: b[:, 0:256])
                    reached[0] += 1
                copy(dst, job, lambda b: b[:, 0:n * CH].rearrange("p (c n) -> p c n", c=n))

            for i in TILES4:
                for nm, dst in (("b", bT), ("v", vT), ("k", kT), ("a", aT)):
                    rwkv_copy(dst[:, i], f"t{nm}{i}", NC)
            act.wait_ge(S("s5_gated"), CT)
            for lv in range(1, 6):
                n = NC if lv < 3 else PC
                for i in TILES4:
                    rwkv_copy(Y[:, i, 0:n], f"y{lv}_{i}", n)
            for i in TILES4:
                rwkv_copy(GT[:, i], f"gt{i}", NC)
                rwkv_copy(BV[:, i], f"bv{i}", NC)
            for job in RWKV_JOBS[reached[0]:]:
                for f in FILL_DONE[job]:
                    copy(mv[:, int(f[3]), int(f[2]) * 256:int(f[2]) * 256 + 256], f, lambda b: b[:, 0:256])
            act.dma_start(o["mem_v"], mv).then_inc(S("stores"), 16)
            for c in range(PC):
                copy(YT[:, :, c * CH:(c + 1) * CH], f"yy{c}", lambda b: b[:, 0:CT * CH].rearrange("p (i n) -> p i n", i=CT))
            act.wait_ge(S("m_ready"), PC - 1)
            act.dma_start(o["wkv_p"], M[:, PC - 1]).then_inc(S("wkv_p_stored"), 16)
            for i in TILES4:
                copy(YT[:, i, TP:T], f"ys{i}", lambda b: b[:, 0:CH])
            for i in TILES4:
                stored(act, f"me{i}")
                step(af(ysq[:, i, :], YT[:, i, :], ACT.Square), "y_squares")
            act.wait_ge(S("m0_done"), CT)
            act.dma_start(o["wkv_s"], m0).then_inc(S("wkv_stored"), 16)
            stored(act, "va3")
            step(af(gn, gn, ACT.Sqrt), "gn_sqrt")

            for n in range(KT):
                stored(act, f"o{n}")
                step(af(qT[:, n, :], xT[:, n, :], ACT.Square), "x1sq")
            stored(act, "ss_c")
            step(af(rx2, rx2, ACT.Sqrt), "rc_sqrt")
            for n in range(KT):
                copy(qT[:, n, :], f"q{n}")
            act.wait_ge(S("wkv_p_stored"), 16)
            mx, sm = view(STAT, 16), view(STAT + 16, 16)
            for h in range(MH):
                act.wait_ge(S("neg_max"), h + 1)
                b = computed(act, f"sp{h}")
                for t in range(2):
                    i = 2 * h + t
                    ins = af(prob[:, h, t, :], b[:, t * NM:(t + 1) * NM], ACT.Exp, bias=mx[:, i:i + 1], scale=SCALE, accum_out=sm[:, i:i + 1])
                    step.read_out(ins, f"sp{h}") if t else step(ins)
            for g in range(2):
                act.wait_ge(S("neg_max"), MH + g + 1)
                b, i = computed(act, f"sb{g}"), 8 + g
                step.read_out(af(sprob[:, g, :], b[:, 0:NM], ACT.Exp, bias=mx[:, i:i + 1], scale=SCALE, accum_out=sm[:, i:i + 1]), f"sb{g}")
            for h in range(MH):
                copy(pT[:, h], f"tp{h}", lambda b: b[:, :].rearrange("p (m t) -> p m t", m=2))
            copy(spT, "tb", lambda b: b[:, :].rearrange("p (g m t) -> p g m t", g=2, m=2))
            for n in range(KT):
                copy(oT[:, n, 0:TP], f"op{n}", lambda b: b[:, 0:TP])
            for g in range(2):
                copy(oT[:, :, TP + 32 * g:TP + 32 * g + 32], f"ob{g}", lambda b: b[:, 0:256].rearrange("p (n t) -> p n t", n=KT))
            computed(act, "co7")
            act.dma_start(gfin, bass.AP(a["final_g"].tensor, 0, [[0, P], [1, D]])).then_inc(S("gfin_in"), 16)
            act.dma_start(rbias, bass.AP(a["router_b"].tensor, 0, [[0, P], [1, NE]])).then_inc(S("rbias_in"), 16)
            act.dma_start(bdown, a["b_down"]).then_inc(S("bdown_in"), 16)
            for n in range(KT):
                stored(act, f"co{n}")
                step(af(nT[:, n, :], xT[:, n, :], ACT.Square), "x2sq")
            stored(act, "ss_f")
            step(af(rx2, rx2, ACT.Sqrt), "rf_sqrt")
            act.wait_ge(S("stores"), 16 * 3)
            act.wait_ge(S("tok_zero"), 2)
            for dst, nm in ((htok, "th"), (yacc, "tx")):
                for t in range(TT):
                    for h in range(2):
                        copy(dst[0:tile_rows[t], t, h * 512:h * 512 + 512], f"{nm}{t}{h}", lambda b: b[0:tile_rows[t], :])
            act.wait_ge(S("top_shifted"), 1)
            step(af(g4, g4, ACT.Exp), "top_exp")
            copy(gtr, "gtr", lambda b: b[0:NE, 0:TT * P])

            b = ps[2]
            act.wait_ge(psum_full[2], BANK_USES[2] + 1)
            ins = af(xte, b[:, :].rearrange("p (k c) -> p k c", k=KT), ACT.Identity)
            ins.then_inc(psum_free[2], 1)

            def expert(it, e):
                act.wait_ge(psum_free[0], it + (BANK_USES[0] + 1))
                af(sig, hg, ACT.Sigmoid, scale=ALPHA).then_inc(S("sigmoid"), 1)
                act.wait_ge(psum_full[5], it + (BANK_USES[5] + 1))
                af(gtt, ps[5][:, 0:TT * P].rearrange("p (t n) -> p t n", t=TT), ACT.Identity).then_inc(psum_free[5], 1)
                act.wait_ge(psum_full[2], it + (BANK_USES[2] + 2))
                af(xte, ps[2][:, :].rearrange("p (k c) -> p k c", k=KT), ACT.Identity).then_inc(psum_free[2], 1)
                act.wait_ge(psum_full[3], it * 2 + (BANK_USES[3] + 1))
                af(actT, ps[3][:, :].rearrange("p (k c) -> p k c", k=4), ACT.Identity).then_inc(psum_free[3], 1)
                act.wait_ge(psum_full[4], it * 2 + (BANK_USES[4] + 1))
                af(yb, ps[4][:, :], ACT.Identity).then_inc(psum_free[4], 1)

            all_passes(act, expert)
            sm = view(SCR + 1100, 16)
            act.wait_ge(S("experts_done"), 1)
            for t in range(TT):
                step(af(view(BIAS, D), yacc[:, t, :], ACT.Square, accum_out=sm[:, t:t + 1]), "y_sq")
            act.wait_ge(S("y_var"), 1)
            step(af(sm[:, 0:TT], sm[:, 0:TT], ACT.Sqrt), "y_sqrt")

        @block.gpsimd
        def _(pool):
            step = Steps(pool, "pool_steps")
            tt, ts = nc.gpsimd.tensor_tensor, nc.gpsimd.tensor_scalar
            pool.wait_ge(S("mem_in"), 16)
            step(tt(memsq, memT, memT, ALU.mult), "memsq")
            step(nc.gpsimd.memset(uT[:, :, 0:7], 0.0), "u_pad")
            pool.wait_ge(S("nmem"), KT)
            step(nc.gpsimd.memset(view(KKO, 256), 0.0), "kk_zero")
            pool.wait_ge(S("consts_in"), 16)

            def advance(dst, src, lr, li, n):
                a_r = over(lr, 2, n)
                a_i = over(li, 2, n)
                u, v = w1[:, :, :, 0:n], w2[:, :, :, 0:n]
                step(tt(u, src, over(a_r, 1, 2), ALU.mult))
                step(tt(v[:, 0], src[:, 1], a_i, ALU.mult))
                step(tt(v[:, 1], src[:, 0], a_i, ALU.mult))
                step(tt(u[:, 0], u[:, 0], v[:, 0], ALU.subtract))
                step(tt(u[:, 1], u[:, 1], v[:, 1], ALU.add))
                step(tt(dst, dst, u, ALU.add))

            def scan(ct):
                qs = slice(PAIRS * ct, PAIRS * ct + PAIRS)
                h0 = s5p("h0", 2, 16, NB)[:, :, qs, :]
                stored(pool, f"ve{ct}")
                xe = xes[ct % 2]
                advance(xe[:, :, :, PBL:NBL], h0, pw_r[:, 0, qs], pw_i[:, 0, qs], NB)
                for lv in range(5):
                    d = 1 << lv
                    lr, li = (view(PWO + 288 + 80 * i, 5, 16)[:, lv, qs] for i in range(2))
                    advance(xe[:, :, :, d:PBL], xe[:, :, :, 0:PBL - d], lr, li, PBL - d)
                step(nc.gpsimd.tensor_copy(s5fin[:, :, qs, :], xe[:, :, :, PBL - 1:NBL]), "s5_final")

            def starts(ct):
                h0 = s5p("h0", 2, 16, NB)[:, :, PAIRS * ct:PAIRS * ct + PAIRS, :]
                if ct:
                    computed(pool, f"st{ct - 1}")
                else:
                    step(nc.gpsimd.memset(x0[:, :, :, 0:1], 0.0))
                step(nc.gpsimd.tensor_copy(x0[:, :, :, PBL:NBL], h0))
                step(nc.gpsimd.tensor_copy(x0[:, :, :, 1:PBL], xes[ct % 2][:, :, :, 0:PBL - 1]), "s5_x0")

            def c_matrices(ct):
                if ct:
                    computed(pool, f"st{ct - 1}")
                qs = slice(PAIRS * ct, PAIRS * ct + PAIRS)
                pr, pi = (over(p[:, 0:BL, qs].rearrange("p j q -> p q j"), 3, 32) for p in (pw_r, pw_i))
                cr, ci = (over(c[:, qs, :], 2, BL) for c in (cbd_r, cbd_i))
                half = [slice(0, 2), slice(2, 4)]
                tmp = view(CAO + 2048, 2, BL, 32)
                for hq in half:
                    step(tt(ca_r[:, hq], pr[:, hq], cr[:, hq], ALU.mult))
                    step(tt(tmp, pi[:, hq], ci[:, hq], ALU.mult))
                    step(tt(ca_r[:, hq], ca_r[:, hq], tmp, ALU.add))
                    step(tt(ca_i[:, hq], pr[:, hq], ci[:, hq], ALU.mult))
                    step(tt(tmp, pi[:, hq], cr[:, hq], ALU.mult))
                    last = tt(ca_i[:, hq], ca_i[:, hq], tmp, ALU.subtract)
                    step(last, "s5_ca" if hq is half[1] else None)

            pool.wait_ge(S("s5_ready"), 1)
            c_matrices(0)
            for ct in range(CT):
                scan(ct)
                if ct:
                    c_matrices(ct)
                starts(ct)

        @block.vector
        def _(dve):
            step = Steps(dve, "dve_steps")
            v = nc.vector
            tt, ts, stt, cp = v.tensor_tensor, v.tensor_scalar, v.scalar_tensor_tensor, v.tensor_copy
            add, sub, mul = ALU.add, ALU.subtract, ALU.mult
            dve.wait_ge(S("consts_in"), 16)
            dve.wait_ge(S("vecs_in"), 16)
            dve.wait_ge(S("x_in"), 16)

            dve.wait_ge(S("s5p_in"), 16)
            t = [view(SCAN + 16 * i, 16) for i in range(16)]
            rx, rm = view(YL, T), view(KKO, NM)
            b = computed(dve, "ss_x")
            step.read_out(ts(rx, b[:, 0:T], 1.0 / D, RMS_EPS, mul, add), "ss_x")
            b = computed(dve, "ss_m")
            step.read_out(ts(rm, b[:, 0:NM], 1.0 / D, RMS_EPS, mul, add), "ss_m")
            dve.wait_ge(S("rx_sqrt"), 1)
            step(v.reciprocal(rx, rx))
            for k in range(KT):
                step(stt(n1[:, k, :], xT[:, k, :], vec("norm_mix_g", k), rx, mul, mul), "n1")
            dve.wait_ge(S("rm_sqrt"), 1)
            step(v.reciprocal(rm, rm))
            dve.wait_ge(S("mem_in"), 16)
            dve.wait_ge(S("memsq"), 1)
            for k in range(KT):
                step(stt(memT[:, k, :], memT[:, k, :], vec("norm_mem_g", k), rm, mul, mul), "nmem")

            lr, li, dt = s5p("lr", 16), s5p("li", 16), s5p("dt", 16)
            dve.wait_ge(S("s5_dt"), 1)
            step(tt(t[0], lr, dt, mul), "s5_mag_arg")
            step(tt(t[1], li, dt, mul))
            for n, quarter in ((2, 0.0), (3, float(np.pi / 2))):
                step(ts(t[4], t[1], quarter, 1.0 / (2 * np.pi), add, mul))
                step(ts(t[4], t[4], ROUND, None, add))
                step(ts(t[4], t[4], ROUND, None, sub))
                step(stt(t[5], t[4], -TWO_PI_HI, t[1], mul, add))
                step(stt(t[5], t[4], -TWO_PI_LO, t[5], mul, add))
                step(ts(t[5], t[5], quarter, 3.1415925, add, ALU.min))
                step(ts(t[n], t[5], -3.1415925, None, ALU.max), "s5_angles" if n == 3 else None)
            dve.wait_ge(S("s5_mag"), 1)
            dve.wait_ge(S("s5_sincos"), 1)
            one_r, one_i = pw_r[:, BL - 1, :], pw_i[:, BL - 1, :]
            step(tt(one_r, t[0], t[3], mul))
            step(tt(one_i, t[0], t[2], mul))
            step(v.memset(pw_r[:, BL, :], 1.0))
            step(v.memset(pw_i[:, BL, :], 0.0))
            step(tt(t[6], lr, lr, mul))
            step(tt(t[7], li, li, mul))
            step(tt(t[6], t[6], t[7], add))
            step(v.reciprocal(t[6], t[6]))
            step(ts(t[7], one_r, 1.0, None, sub))
            step(tt(t[8], t[7], lr, mul))
            step(tt(t[9], one_i, li, mul))
            step(tt(t[8], t[8], t[9], add))
            step(tt(t[8], t[8], t[6], mul))
            step(tt(t[9], one_i, lr, mul))
            step(tt(t[10], t[7], li, mul))
            step(tt(t[9], t[9], t[10], sub))
            step(tt(t[9], t[9], t[6], mul))
            br, bi = s5p("br", 16, GC), s5p("bi", 16, GC)
            cr, ci = over(t[8], 2, GC), over(t[9], 2, GC)
            m = [view(SCAN + 256 + 256 * i, 16, GC) for i in range(3)]
            step(tt(m[0], br, cr, mul))
            step(tt(m[1], bi, ci, mul))
            step(tt(m[0], m[0], m[1], sub))
            step(tt(m[1], bi, cr, mul))
            step(tt(m[2], br, ci, mul))
            step(tt(bi, m[1], m[2], add))
            step(cp(br, m[0]))
            step(ts(view(S5O + S5P["ci"][0], 512), view(S5O + S5P["ci"][0], 512), -1.0, None, mul))

            def cmul(dst, src, by, n, signal=None):
                (dr, di), (sr, si), (qr, qi) = dst, src, by
                qr, qi = over(qr, 1, n), over(qi, 1, n)
                p, q = (view(SCAN + 256 + 64 * i, n, 16) for i in range(2))
                step(tt(p, si, qi, mul))
                step(tt(dr, sr, qr, mul))
                step(tt(dr, dr, p, sub))
                step(tt(q, si, qr, mul))
                step(tt(di, sr, qi, mul))
                step(tt(di, di, q, add), signal)

            def rows(lo, hi):
                return pw_r[:, lo:hi, :], pw_i[:, lo:hi, :]

            for lo, n in ((6, 1), (4, 2), (0, 4)):
                cmul(rows(lo, lo + n), rows(lo + n, lo + 2 * n), (pw_r[:, lo + n, :], pw_i[:, lo + n, :]), n)
            lvl_r, lvl_i = (view(PWO + 288 + 80 * i, 5, 16) for i in range(2))
            step(cp(lvl_r[:, 0, :], pw_r[:, 0, :]))
            step(cp(lvl_i[:, 0, :], pw_i[:, 0, :]))
            for i in range(1, 5):
                one = (lvl_r[:, i - 1, :], lvl_i[:, i - 1, :])
                cmul((lvl_r[:, i:i + 1, :], lvl_i[:, i:i + 1, :]), (lvl_r[:, i - 1:i, :], lvl_i[:, i - 1:i, :]), one, 1,
                     signal="s5_ready" if i == 4 else None)

            prev = view(VECO + VEC["prev"][0], 4, CT, NB)
            DELTA = R[7]

            def mixes(c):
                p, n = prj[c], PRJ_ORDER.index(c)
                stored(dve, f"{c}3")
                step(cp(shift[:, n], p[:, :, TP - 1::TS]), "shifts")
                ps_, ds_ = (x[:, :, TP:T].rearrange("p i (s t) -> p i s t", s=NB) for x in (p, DELTA))
                step(tt(DELTA[:, :, 1:TP], p[:, :, 0:TP - 1], p[:, :, 1:TP], sub))
                step(ts(DELTA[:, :, 0:1], p[:, :, 0:1], -1.0, None, mul))
                step(tt(ds_[:, :, :, 1:TS], ps_[:, :, :, 0:TS - 1], ps_[:, :, :, 1:TS], sub))
                step(tt(ds_[:, :, :, 0], prev[:, n], ps_[:, :, :, 0], sub))
                outs = [(R[4], 3), (R[5], 4), (R[6], 5)] if c == "z" else [(p, "rkv".index(c))]
                for dst, mu in outs:
                    for i in TILES4:
                        last = stt(dst[:, i, :], DELTA[:, i, :], vec("rwkv_mu", 4 * mu + i), p[:, i, :], mul, add)
                        step(last, "z_mixed" if c == "z" else ("delta_free" if (c, i) == ("v", 3) else None))

            def f_matrices(ct):
                if ct:
                    computed(dve, f"kk{ct - 1}")
                qs = slice(PAIRS * ct, PAIRS * ct + PAIRS)
                shape = "p q (j c) -> p q j c"
                fr, fi = F_r.rearrange(shape, j=BL), F_i.rearrange(shape, j=BL)
                tmp = view(RW[7], PAIRS, BL, GC)
                pr, pi = (over(p[:, 1:BL + 1, qs].rearrange("p j q -> p q j"), 3, GC) for p in (pw_r, pw_i))
                br, bi = (over(s5p(nm, 16, GC)[:, qs, :], 2, BL) for nm in ("br", "bi"))
                step(tt(fr, pr, br, mul))
                step(tt(tmp, pi, bi, mul))
                step(tt(fr, fr, tmp, sub))
                step(tt(fi, pr, bi, mul))
                step(tt(tmp, pi, br, mul))
                step(tt(fi, fi, tmp, add), "s5_f")

            def mask_windows(ct):
                dve.wait_ge(S(f"uwin_in{ct % 2}"), 16 * BL * (ct // 2 + 1))
                step(tt(uwins[ct % 2], uwins[ct % 2], over(con("window"), 1, 8), mul), "uwin")

            def s5_local(ct):
                b = computed(dve, f"loc{ct}")
                step.read_out(stt(yl[ct], uT[:, ct, 7:], vec("s5_d", ct), b[:, 0:T], mul, add), f"loc{ct}")

            def s5_gelu(ct):
                b = computed(dve, f"st{ct}")
                y = yl[ct].rearrange("p (c j) -> p j c", j=BL)
                step.read_out(tt(y, y, b[:, 0:T].rearrange("p (j c) -> p j c", j=BL), add), f"st{ct}")
                z = mix[:, ct, :]
                step(tt(z, yl[ct], yl[ct], mul))
                step(ts(z, z, 0.044715, 1.0, mul, add))
                step(tt(z, z, yl[ct], mul), "gelu_arg")
                dve.wait_ge(S("gelu_tanh"), ct + 1)
                step(stt(z, z, 1.0, yl[ct], add, mul))
                step(ts(z, z, 0.5, None, mul), "s5_gelu")

            def k_norm():
                computed(dve, "lg")
                kk = R[4]
                for i in TILES4:
                    step(ts(kk[:, i, :], R[1][:, i, :], vec("rwkv_k_k", i), None, mul))
                step(tt(R[6], kk, kk, mul), "kk_squares")
                for i in TILES4:
                    b = computed(dve, f"kn{i}")
                    step.read_out(ts(R[9][:, i, :], b[:, 0:T], 1e-24, None, ALU.max), f"kn{i}")
                dve.wait_ge(S("kk_norm"), 1)
                step(v.reciprocal(R[9], R[9]))
                step(tt(kk, kk, R[9], mul))

            def keys():
                kk, w, a_, k, r = R[4], R[3], R[7], R[1], R[0]
                dve.wait_ge(S("decay"), 1)
                computed(dve, "dg3")
                computed(dve, "v3")
                step(tt(R[9], w, over(con("carry"), 1, CT), mul))
                step(tt(R[8], w, R[9], sub))
                flat = [view(RW[i], ROW) for i in (9, 8, 12)]
                step(v.tensor_tensor_scan(flat[2], flat[0], flat[1], 0.0, mul, add))
                prod = Rc[12]
                step(cp(pend[:, :, 0:PC], prod[:, :, 0:PC, CH - 1]))
                step(cp(pend[:, :, PC:], prod[:, :, PC, TS - 1::TS]))
                step(v.reciprocal(R[9], R[12]))
                stored(dve, "da3")
                computed(dve, "kn3")
                for i in TILES4:
                    ka, one = vec("rwkv_k_a", i), view(SCAN + 700, 1)
                    step(ts(one, ka, -1.0, 1.0, mul, add))
                    step(ts(R[6][:, i, :], a_[:, i, :], ka, one, mul, add))
                step(tt(k, k, R[6], mul))
                step(tt(R[6], kk, a_, mul))
                flatc = [x.rearrange("p i c n -> p (i c) n") for x in (Rc[4], prod, Rc[0])]
                arf = ar.rearrange("p i c a n -> p (i c) a n")
                computed(dve, "st3")
                step(stt(arf[:, :, 0, 1:], flatc[0][:, :, 1:], -1.0, flatc[1][:, :, 0:CH - 1], mul, mul))
                step(ts(arf[:, :, 0, 0:1], flatc[0][:, :, 0:1], -1.0, None, mul))
                step(ts(ar[:, :, PC, 0, TS::TS], Rc[4][:, :, PC, TS::TS], -1.0, None, mul), "rw_keys")
                step(tt(arf[:, :, 1, :], flatc[2], flatc[1], mul), "rw_keys")
                for i in TILES4:
                    step(stt(R[8][:, i, :], r[:, i, :], vec("rwkv_r_k", i), k[:, i, :], mul, mul), "rkr" if i == 3 else None)
                step(tt(R[6], R[6], R[9], mul), "rw_keys")
                step(tt(R[7], k, R[9], mul), "rw_keys")
                for i in TILES4:
                    b = computed(dve, f"bo{i}")
                    step.read_out(tt(R[1][:, i, :], b[:, 0:T], R[2][:, i, :], mul), f"bo{i}")

            def glu():
                for i in TILES4:
                    stored(dve, f"gl{i}")
                for i in TILES4:
                    step(tt(mix[:, i, :], mix[:, i, :], view(UWIN, CT, T)[:, i, :], mul), "s5_gated")

            for kind, n in MIX_ORDER:
                if kind == "mix":
                    mixes(n)
                elif kind == "f":
                    f_matrices(n)
                elif kind == "win":
                    mask_windows(n)
                elif kind == "y":
                    s5_local(n)
                elif kind == "out":
                    s5_gelu(n)
                elif kind == "knorm":
                    k_norm()
            keys()
            glu()

            strict, incl = (con(nm).rearrange("p (a n) -> p a n", a=2) for nm in ("strict", "incl"))
            level = con("level").rearrange("p (l n) -> p l n", l=6)
            for i in range(5):
                kind, blocks = (0, lambda x: x[:, i, 0:PC]) if i < 4 else (1, lambda x: x[:, :, PC])
                for nm, first, second in (("b", AT, C1), ("k", BT, C2)):
                    b = computed(dve, f"g{nm}{i}")[:, :].rearrange("p (c a n) -> p c a n", c=4, a=2)
                    if nm == "b":
                        step(cp(blocks(first), b[:, :, 0, :]))
                    else:
                        step(tt(blocks(first), b[:, :, 0, :], over(strict[:, kind], 1, 4), mul))
                    step.read_out(tt(blocks(second), b[:, :, 1, :], over(incl[:, kind], 1, 4), mul), f"g{nm}{i}")

            def a_level(lv, i):
                n = NC if lv < 3 else PC
                step(tt(al[:, i, 0:n], AT[:, i, 0:n], over(level[:, lv], 1, n), mul), "a_level")

            for i in TILES4:
                a_level(0, i)
            for i in TILES4:
                b = computed(dve, f"y0_{i}")[:, 0:T].rearrange("p (c n) -> p c n", c=NC)
                step.read_out(tt(X[:, i], b, over(con("ident64"), 1, NC), add), f"y0_{i}")
                step(tt(XI[:, i], al[:, i], over(con("ident64"), 1, NC), add))
                a_level(1, i)
            for lv in range(1, 6):
                n = NC if lv < 3 else PC
                for i in TILES4:
                    if lv < 5:
                        b = computed(dve, f"dx{lv}_{i}")[:, 0:n * CH].rearrange("p (c n) -> p c n", c=n)
                        step.read_out(tt(X[:, i, 0:n], X[:, i, 0:n], b, add), f"dx{lv}_{i}")
                    b = computed(dve, f"dt{lv}_{i}")[:, 0:n * CH].rearrange("p (c n) -> p c n", c=n)
                    step.read_out(tt(XI[:, i, 0:n], XI[:, i, 0:n], b, add), f"dt{lv}_{i}")
                    if lv < 5:
                        a_level(lv + 1, i)
            for i in TILES4:
                b = computed(dve, f"hh{i}")[:, 0:T].rearrange("p (c n) -> p c n", c=NC)
                step.read_out(cp(H[:, i], b), f"hh{i}")
            step(cp(U[:, :, 0], H[:, :, 0]), "u_first")
            for c in range(PC):
                if c:
                    b = computed(dve, f"u_{c}")[:, 0:CT * HN].rearrange("p (i n) -> p i n", i=CT)
                    step.read_out(tt(U[:, :, c], b, H[:, :, c], add), f"u_{c}")
                b = computed(dve, f"m_{c}")[:, 0:CT * HN].rearrange("p (i n) -> p i n", i=CT)
                scale = over(pend[:, :, c], 2, HN)
                if c:
                    step.read_out(tt(M[:, c], b, M[:, c - 1], add), f"m_{c}")
                    step(tt(M[:, c], M[:, c], scale, mul), "m_ready")
                else:
                    step.read_out(tt(M[:, 0], b, scale, mul), "m_0")
            seq = con("seqmask")
            for i in TILES4:
                tmp, t2 = view(RW[8], NB, HN), view(RW[8] + 512, HN)
                b = computed(dve, f"us{i}")[:, :].rearrange("p (s n) -> p s n", s=NB)
                step.read_out(tt(tmp, b, over(seq, 2, HN), mul), f"us{i}")
                step(v.reduce_sum(t2, tmp.rearrange("p s n -> p n s"), AX.X))
                step(tt(U[:, i, PC], t2, H[:, i, PC], add), "u_sample")
            for i in TILES4:
                if i >= 2:
                    computed(dve, f"sf{i - 2}")
                for src, dst, signal in ((U, um, None), (vT, vm, "uv_masked")):
                    step(tt(dst[:, i % 2].rearrange("p (s n) -> p s n", s=NB), over(src[:, i, PC], 1, NB), over(seq, 2, HN), mul), signal)
            for i in TILES4:
                b = computed(dve, f"sf{i}")[:, :].rearrange("p (s n) -> p s n", s=NB)
                step.read_out(tt(m0[:, i], m0[:, i], b, add), f"sf{i}")
                step(tt(m0[:, i], m0[:, i], over(pend[:, i, PC:], 2, HN), mul), "m0_done")
            for i in TILES4:
                b = computed(dve, f"me{i}")
                step.read_out(stt(YT[:, i, :], b[:, 0:T], -1.0 / HN, YT[:, i, :], mul, add), f"me{i}")
            for i in TILES4:
                b = computed(dve, f"va{i}")
                step.read_out(ts(gn[:, i, :], b[:, 0:T], 1.0 / HN, GN_EPS, mul, add), f"va{i}")
            dve.wait_ge(S("gn_sqrt"), 1)
            step(v.reciprocal(gn, gn))
            dve.wait_ge(S("s5_stored"), 16)
            for i in TILES4:
                y = YT[:, i, :]
                step(stt(y, y, vec("rwkv_ln_w", i), gn[:, i, :], mul, mul))
                step(stt(y, y, vec("rwkv_ln_b", i), R[1][:, i, :], add, add))
                step(tt(mix[:, CT + i, :], y, R[5][:, i, :], mul), "mix_ready")

            def norm(sumsq, sqrt, g, dst, signal):
                b = computed(dve, sumsq)
                step.read_out(ts(rx2, b[:, 0:T], 1.0 / D, RMS_EPS, mul, add), sumsq)
                dve.wait_ge(S(sqrt), 1)
                step(v.reciprocal(rx2, rx2))
                for k in range(KT):
                    step(stt(dst[:, k, :], xT[:, k, :], vec(g, k), rx2, mul, mul), signal)

            for n in range(KT):
                b = computed(dve, f"o{n}")
                step.read_out(tt(xT[:, n, :], xT[:, n, :], b[:, 0:T], add), f"o{n}")
            norm("ss_c", "rc_sqrt", "norm_ca_g", nT, "nca")
            dve.wait_ge(S("wkv_stored"), 16)
            step(v.memset(view(QBLK, 2048), 0.0))
            stored(dve, "q7")
            for h in range(MH):
                step(cp(qblk[:, 2 * h:2 * h + 2, :, h * TS:(h + 1) * TS],
                        qT[:, 2 * h:2 * h + 2, TP:T].rearrange("p n (s t) -> p n s t", s=NB)), "qblk")
            mx, sm = view(STAT, 16), view(STAT + 16, 16)
            for h in range(MH):
                b = computed(dve, f"sp{h}")
                step(v.reduce_max(mx[:, 2 * h:2 * h + 2], b[:, :].rearrange("p (t m) -> p t m", t=2), AX.X))
                step(ts(mx[:, 2 * h:2 * h + 2], mx[:, 2 * h:2 * h + 2], -SCALE, None, mul), "neg_max")
            for g in range(2):
                b = computed(dve, f"sb{g}")
                step(v.reduce_max(mx[:, 8 + g:9 + g], b[:, 0:NM], AX.X))
                step(ts(mx[:, 8 + g:9 + g], mx[:, 8 + g:9 + g], -SCALE, None, mul), "neg_max")
            for h in range(MH):
                stored(dve, f"sp{h}")
                step(v.reciprocal(sm[:, 2 * h:2 * h + 2], sm[:, 2 * h:2 * h + 2]))
                step(tt(prob[:, h], prob[:, h], over(sm[:, 2 * h:2 * h + 2], 2, NM), mul), "prob")
            for g in range(2):
                stored(dve, f"sb{g}")
                step(v.reciprocal(sm[:, 8 + g:9 + g], sm[:, 8 + g:9 + g]))
                step(ts(sprob[:, g, :], sprob[:, g, :], sm[:, 8 + g:9 + g], None, mul), "prob")
            for n in range(KT):
                b = computed(dve, f"co{n}")
                step.read_out(tt(xT[:, n, :], xT[:, n, :], b[:, 0:T], add), f"co{n}")
            step(v.memset(bias, 0.0), "bias_zero")
            norm("ss_f", "rf_sqrt", "norm_ffn_g", hT, "nff")

            dve.wait_ge(S("stores"), 16 * 3)
            step(v.memset(htok[CAP:, TT - 1, :], 0.0), "tok_zero")
            step(v.memset(yacc[CAP:, TT - 1, :], 0.0), "tok_zero")
            step(v.memset(logit, 0.0))
            dve.wait_ge(S("rbias_in"), 16)
            b = computed(dve, "lgt")
            step(tt(logit[:, 0:2], b[:, 0:2 * NE].rearrange("p (t e) -> p t e", t=2), over(rbias, 1, 2), add))
            step.read_out(tt(logit[0:tile_rows[2], 2], b[0:tile_rows[2], 2 * NE:3 * NE], rbias[0:tile_rows[2], :], add), "lgt")
            for t in range(TT):
                step(v.max(top[:, t], logit[:, t]))
                step(v.max_index(idx_u[:, t], top[:, t], logit[:, t]))
            step(cp(idxf, idx_u))
            step(tt(g4, top[:, :, 0:TOPK], over(top[:, :, 0], 2, TOPK), sub), "top_shifted")
            expert_no = over(con("iota")[:, 0:NE], 1, TT)
            step(tt(mask, expert_no, over(idxf[:, :, 0], 2, NE), ALU.is_equal))
            for j in range(1, TOPK):
                step(tt(eq, expert_no, over(idxf[:, :, j], 2, NE), ALU.is_equal))
                step(tt(mask, mask, eq, add))
            step(v.memset(mask[CAP:, TT - 1, :], 0.0), "mask")
            dve.wait_ge(S("top_exp"), 1)
            step(v.reduce_sum(gsum, g4, AX.X))
            step(v.reciprocal(gsum, gsum))
            step(tt(g4, g4, over(gsum, 2, TOPK), mul))
            step(tt(gate, expert_no, over(idxf[:, :, 0], 2, NE), ALU.is_equal))
            step(tt(gate, gate, over(g4[:, :, 0], 2, NE), mul))
            for j in range(1, TOPK):
                step(tt(eq, expert_no, over(idxf[:, :, j], 2, NE), ALU.is_equal))
                step(tt(eq, eq, over(g4[:, :, j], 2, NE), mul))
                step(tt(gate, gate, eq, add))
            step(v.memset(gate[CAP:, TT - 1, :], 0.0), "gates")
            tabt = tab.rearrange("p e s -> p s e")
            b = computed(dve, "pos")[:, 0:TT * NE].rearrange("p (t e) -> p t e", t=TT)
            step.read_out(stt(eg, b, 1.0, mask, add, mul), "pos")
            step(ts(tabt[:, 0:TT, 0:NE], eg, -1.0, None, add))
            step(cp(tabt[:, TT:, 0:NE], gate))
            step(ts(tab[:, NE, 0:TT], tab[:, 0, 0:TT], -float(CAP), None, add))
            step(cp(tab[:, NE, TT:], tab[:, 0, TT:]))
            b = computed(dve, "cnt")
            step.read_out(v.reduce_max(gsum[:, 0:1], b[:, 0:NE], AX.X), "cnt")
            step(cp(most_i32[:, :], gsum[:, 0:1]), "counts")
            step(cp(cur[:, 0:6], tab[:, 0]))
            step(tt(sel, over(con("iota")[:, 0:CAP], 1, TT), over(cur[:, 0:TT], 2, CAP), ALU.is_equal), "selected")
            stored(dve, "tx21")
            for t in range(TT):
                for h in range(2):
                    part = slice(h * 512, h * 512 + 512)
                    b = computed(dve, f"bd{t}{h}")
                    step.read_out(tt(yacc[:, t, part], yacc[:, t, part], b[:, :], add), f"bd{t}{h}")

            def next_pass(p):
                ts(tab[:, :, 0:TT], tab[:, :, 0:TT], -float(CAP), None, add).then_inc(S("ranks_moved"), 1)
                dve.wait_ge(S("ranks_moved"), p)
                cp(cur[:, 7:8], tab[:, 0, 0:1])

            CHAIN = 2

            def expert(it, e):
                n = [0]

                def chain(ins):
                    n[0] += 1
                    ins.then_inc(S("expert_steps"), 1)
                    dve.wait_ge(S("expert_steps"), it * CHAIN + n[0])

                dve.wait_ge(psum_full[5], it + BANK_USES[5])
                for t in range(TT):
                    ins = ts(selg[:, t, :], con("iota"), cur[:, t:t + 1], cur[:, TT + t:TT + t + 1], ALU.is_equal, mul)
                ins.then_inc(S("weighted"), 1)
                dve.wait_ge(S("weighted"), it + 1)
                chain(cp(cur[:, 0:6], tab.rearrange("p e s -> p (e s)")[:, bass.ds(e * 6 + 6, 6)]))
                dve.wait_ge(psum_full[2], it + (BANK_USES[2] + 1))
                tt(sel, over(con("iota")[:, 0:CAP], 1, TT), over(cur[:, 0:TT], 2, CAP), ALU.is_equal).then_inc(S("selected"), 1)
                dve.wait_ge(psum_full[0], it + (BANK_USES[0] + 1))
                dve.wait_ge(S("selected"), it + 2)
                ts(hg, ps[0][:, :], LIMIT, None, ALU.min).then_inc(psum_free[0], 1)
                dve.wait_ge(psum_full[1], it + (BANK_USES[1] + 1))
                ts(hu, ps[1][:, :], LIMIT, -LIMIT, ALU.min, ALU.max).then_inc(psum_free[1], 1)
                dve.wait_ge(psum_free[0], it + (BANK_USES[0] + 1))
                dve.wait_ge(psum_free[1], it + (BANK_USES[1] + 1))
                chain(stt(hu, hu, 1.0, hg, add, mul))
                dve.wait_ge(S("sigmoid"), it + 1)
                tt(hact, hu, sig, mul).then_inc(S("activated"), 1)
                dve.wait_ge(S("activated"), it + 1)
                for t, banks, at in ((0, (6, 7), 1), (1, (3, 4), 2), (2, (6, 7), 2)):
                    for s, bank in enumerate(banks):
                        dve.wait_ge(psum_full[bank], it * 2 + (BANK_USES[bank] + at))
                        part = yacc[:, t, s * 512:s * 512 + 512]
                        tt(part, part, ps[bank][:, :], add).then_inc(psum_free[bank], 1)
                for bank in (3, 4, 6, 7):
                    dve.wait_ge(psum_free[bank], it * 2 + (BANK_USES[bank] + 2))
                assert n[0] == CHAIN

            all_passes(dve, expert, next_pass)
            step(cp(cur[:, 6:7], cur[:, 0:1]), "experts_done")
            sm = view(SCR + 1100, 16)
            dve.wait_ge(S("y_sq"), TT)
            step(ts(sm[:, 0:TT], sm[:, 0:TT], 1.0 / D, RMS_EPS, mul, add), "y_var")
            dve.wait_ge(S("y_sqrt"), 1)
            step(v.reciprocal(sm[:, 0:TT], sm[:, 0:TT]))
            dve.wait_ge(S("gfin_in"), 16)
            for t in range(TT):
                step(stt(htok[:, t, :], yacc[:, t, :], sm[:, t:t + 1], gfin, mul, mul), "final")


def _stationary(w, np_):
    k, n = w.shape
    return np_.ascontiguousarray(w.reshape(k // 128, 128, n // 256, 2, 128).transpose(2, 1, 3, 0, 4)).reshape(n // 256, 128, -1)


def _columns(v):
    return v.reshape(-1, 128).T


def _constants(np_):
    c = {n: np_.zeros((128, w), np_.float32) for n, (_, w) in CON.items()}
    p = np_.arange(128)
    s, t = p[:, None] % 64, np_.arange(64)[None, :]
    c["ident"][p, p] = 1
    c["headones"][:] = p[:, None] // 64 == p[None, :] // 64
    c["ones"][:] = 1
    for lv in range(6):
        b = 1 << lv
        c["level"][:, 64 * lv:64 * lv + 64] = (t // (2 * b) == s // (2 * b)) & (t // b % 2 == 1) & (s // b % 2 == 0)
    c["strict"][:, :64], c["strict"][:, 64:] = s < t, (s < t) & (s // TS == t // TS)
    c["incl"][:, :64], c["incl"][:, 64:] = s <= t, (s <= t) & (s // TS == t // TS)
    c["seqmask"][:] = s // TS == np_.arange(NB)[None, :]
    tok = np_.arange(T)
    c["carry"][:] = np_.where(tok < TP, tok % CH != 0, tok % TS != 0)[None, :]
    c["window"][:] = tok[None, :] % BL >= BL - 1 - p[:, None] // GC
    c["iota"][:] = (np_.arange(128) % CAP)[None, :]
    c["earlier"][:] = p[:, None] < p[None, :]
    c["ident64"][:] = s == t
    c["onerow"][0, :] = 1
    return np_.concatenate([c[n] for n in CON], axis=1)


def _pack(table, parts, rows, np_):
    out = np_.zeros((rows, sum(n for _, n in table.values())), np_.float32)
    for name, part in parts.items():
        at, n = table[name]
        part = np_.asarray(part)
        out[:part.shape[0], at:at + n] = part.reshape(part.shape[0], n)
    return out


def _layout(x, np_):
    w_in = x["w_in"][0]
    u, r, k, v, z = (w_in[:, i * 512:(i + 1) * 512] for i in range(5))
    kc = x["cache_mem_k"][0].reshape(NB, NM, KT, P).transpose(0, 3, 2, 1).reshape(NB, P, -1)
    vc = x["cache_mem_v"][0].reshape(NB, 2, P, D).transpose(0, 2, 1, 3).reshape(NB, P, -1)
    w_v = x["w_mem_kv"][0][:, D:].reshape(KT, P, 4, 256).transpose(2, 1, 0, 3).reshape(4, P, -1)
    glu = x["s5_glu_w"][0].reshape(4, P, 4, P).transpose(1, 2, 0, 3).reshape(1, P, -1)
    dense = np_.concatenate([_stationary(w, np_) for w in (u, k, z, r, v)]
                            + [glu, _stationary(x["w_mem_kv"][0][:, :D], np_), w_v, _stationary(x["w_out"][0], np_), _stationary(x["w_cq"][0], np_), kc, vc,
                               _stationary(x["w_co"][0], np_)])
    tokens = np_.concatenate([x["x_prompt"].reshape(-1, D), x["x_sample"].reshape(-1, D)])
    prev = x["state_rwkv_shift"][0].reshape(NB, 4, CT, P).transpose(3, 1, 2, 0).reshape(P, -1)
    vecs = {n: _columns(x[n]) for n in VEC if n != "prev"}
    vecs["prev"] = prev
    per_state = lambda w: w.reshape(16, 2, NS, -1).transpose(1, 2, 0, 3).reshape(P, -1)
    cpad = {}
    for n in ("s5_c_re", "s5_c_im"):
        c = x[n][0].reshape(16, 2, GC, NS).transpose(1, 3, 0, 2)
        out = np_.zeros((2, NS, 16, 2, GC), np_.float32)
        for g in range(2):
            out[g, :, :, g, :] = c[g]
        cpad[n] = out.reshape(P, -1)
    h0 = np_.stack([x[n][0].reshape(NB, 16, 2, NS).transpose(2, 3, 1, 0) for n in ("state_s5_re", "state_s5_im")], axis=2)
    s5p = {"lr": per_state(x["s5_lambda_re"][0]), "li": per_state(x["s5_lambda_im"][0]),
           "dt": per_state(np_.broadcast_to(x["s5_log_dt"][0][:, None], (32, NS))),
           "br": per_state(x["s5_b_re"][0]), "bi": per_state(x["s5_b_im"][0]),
           "cr": cpad["s5_c_re"], "ci": cpad["s5_c_im"], "h0": h0.reshape(P, -1)}
    up = lambda w: w[0].reshape(CT, P, -1).transpose(1, 0, 2).reshape(P, -1)
    smw = {"w1": up(x["rwkv_w1"]), "a1": up(x["rwkv_a1"]), "g1": up(x["rwkv_g1"]), "w2": x["rwkv_w2"][0], "a2": x["rwkv_a2"][0],
           "g2": x["rwkv_g2"][0], "router_w": x["router_w"][0].reshape(KT, P, NE).transpose(1, 0, 2).reshape(P, -1)}
    m0 = x["state_rwkv_wkv"][0].reshape(NB, CT, 2, HN, HN).transpose(2, 4, 1, 0, 3).reshape(P, CT, NB, HN)
    return {
        "xT": tokens.T.reshape(KT, P, T).transpose(1, 0, 2), "memT": x["mem_prompt"][0].T.reshape(KT, P, NM).transpose(1, 0, 2),
        "dense": dense, "vecs": _pack(VEC, vecs, P, np_), "consts": _constants(np_), "smw": _pack(SMW, smw, P, np_),
        "s5p": _pack(S5P, s5p, P, np_), "m0": m0, "w_gu": x["ex_w_gu"][0], "w_down": x["ex_w_down"][0], "b_gu": x["ex_b_gu"][0],
        "b_down": x["ex_b_down"][0], "router_b": x["router_b"][0].reshape(1, NE), "final_g": x["norm_final_g"].reshape(1, D),
    }


_OUTS = {"y": (P, TT, D), "s5": (P, 2, 16, NB + 1), "shift": (P, 4, CT, NB + 1), "wkv_p": (P, CT, HN), "wkv_s": (P, CT, NB, HN),
         "mem_k": (P, KT, NM), "mem_v": (P, 2, D)}


def kernel(**inputs):
    import numpy as _np
    import concourse.bacc as _bacc
    from concourse import mybir as _mybir
    from concourse.bass_utils import run_bass_kernel_spmd as _run

    nc = _bacc.Bacc("TRN2", target_bir_lowering=False, num_devices=1)
    arrays, a = {}, {}
    for name, arr in _layout({k: _np.asarray(v) for k, v in inputs.items()}, _np).items():
        arr = _np.ascontiguousarray(arr)
        arrays[f"in_{name}"] = arr
        a[name] = nc.dram_tensor(f"in_{name}", arr.shape, _mybir.dt.from_np(arr.dtype), kind="ExternalInput").ap()
    o = {name: nc.dram_tensor(f"out_{name}", shape, _mybir.dt.float32, kind="ExternalOutput").ap() for name, shape in _OUTS.items()}
    build(nc, a, o)
    r = _run(nc, [arrays], core_ids=[0])
    g = {name: r.results[0][f"out_{name}"] for name in _OUTS}
    y = g["y"].transpose(1, 0, 2).reshape(TT * P, D)
    s5 = g["s5"].reshape(2, NS, 2, 16, NB + 1).transpose(2, 4, 3, 0, 1).reshape(2, NB + 1, 32, NS)
    shift = g["shift"].transpose(3, 1, 2, 0).reshape(NB + 1, 4 * W5)
    wkv = lambda w: w.transpose(3, 2, 0, 4, 1).reshape(-1, 8, HN, HN)
    wkv_p = wkv(g["wkv_p"].reshape(2, HN, CT, 1, HN))
    wkv_s = wkv(g["wkv_s"].reshape(2, HN, CT, NB, HN))
    mk = g["mem_k"].transpose(2, 1, 0).reshape(1, 1, NM, MH, MD)
    mv = g["mem_v"].transpose(1, 0, 2).reshape(1, 1, NM, MH, MD)
    c = _np.ascontiguousarray
    return (c(y[:TP].reshape(1, TP, D)), c(y[TP:T].reshape(NB, TS, D)), c(s5[0, None, :1]), c(s5[1, None, :1]), c(shift[None, :1]),
            c(wkv_p[None]), c(mk), c(mv), c(s5[0, None, 1:]), c(s5[1, None, 1:]), c(shift[None, 1:]), c(wkv_s[None]))
```

```python
from contextlib import ExitStack

import numpy as np

import concourse.bass as bass
from concourse import mybir

F32 = mybir.dt.float32
U32 = mybir.dt.uint32
I32 = mybir.dt.int32
ALU = mybir.AluOpType
ACT = mybir.ActivationFunctionType
AX = mybir.AxisListType

P = 128
D = 1024
KT = D // P
TP, NB, TS = 256, 8, 8
T = TP + NB * TS
NM = 256
W5 = 512
CT = W5 // P
GC, NS = 16, 64
BL = 8
NBL = T // BL
PBL = TP // BL
PAIRS = 4
HN = 64
CH = 64
NC = T // CH
PC = TP // CH
MH, MD = 4, 256
NE, TOPK, FF = 32, 4, 1024
CAP = 64
PASSES = T // CAP
TT = 3
SCALE = MD ** -0.5
LIMIT, ALPHA = 7.0, 1.702
DECAY = 0.6065306597
RMS_EPS, GN_EPS = 1e-5, 64e-5
TWO_PI_HI, TWO_PI_LO = 6.28125, float(2 * np.pi - 6.28125)
ROUND = 12582912.0

VEC = {}
for _name, _n in (("norm_mix_g", 8), ("norm_ca_g", 8), ("norm_mem_g", 8), ("norm_ffn_g", 8), ("s5_d", 4), ("s5_glu_b", 4),
                  ("rwkv_mu", 24), ("rwkv_w0", 4), ("rwkv_a0", 4), ("rwkv_k_k", 4), ("rwkv_k_a", 4), ("rwkv_r_k", 4),
                  ("rwkv_ln_w", 4), ("rwkv_ln_b", 4), ("prev", 128)):
    VEC[_name] = (sum(n for _, n in VEC.values()), _n)
NVEC = sum(n for _, n in VEC.values())

CON = {}
for _name, _n in (("ident", 128), ("headones", 128), ("ones", 128), ("level", 6 * 64), ("strict", 128), ("incl", 128),
                  ("seqmask", 8), ("carry", T), ("window", T), ("iota", 128), ("earlier", 128), ("sign", 1),
                  ("ident64", 64), ("onerow", 64)):
    CON[_name] = (sum(n for _, n in CON.values()), _n)
NCON = sum(n for _, n in CON.values())

SMW = {}
for _name, _n in (("w1", 256), ("a1", 256), ("g1", 512), ("w2", 512), ("a2", 512), ("g2", 512), ("router_w", 256)):
    SMW[_name] = (sum(n for _, n in SMW.values()), _n)
NSMW = sum(n for _, n in SMW.values())

S5P = {}
for _name, _n in (("lr", 16), ("li", 16), ("dt", 16), ("br", 256), ("bi", 256), ("cr", 512), ("ci", 512), ("h0", 256)):
    S5P[_name] = (sum(n for _, n in S5P.values()), _n)
NS5P = sum(n for _, n in S5P.values())

CHUNK = 2048
SLOTS = 12
EARLY = 3
PRE = (["in"] * 10 + ["memk"] * 4 + ["glu"] + ["memv"] * 4 + ["out"] * 4 + ["cq"] * 4
       + ["kcache"] * 8 + ["vcache"] * 8 + ["co"] * 4)
NPRE = len(PRE)
MIXER_CHUNKS = 23
FIRST = {k: PRE.index(k) for k in dict.fromkeys(PRE)}


def _slots():
    order = [c % EARLY for c in range(MIXER_CHUNKS)]
    free = [s for s in range(EARLY + 1, SLOTS)] + [EARLY] + [order[-EARLY + i] for i in range(EARLY)]
    while len(order) < NPRE:
        s = free.pop(0)
        order.append(s)
        free.append(s)
    return order, free


SLOT, EXPERT_SLOT = _slots()
PREV = [max([b for b in range(c) if SLOT[b] == SLOT[c]], default=None) for c in range(NPRE)]
USES = [SLOT.count(s) for s in range(SLOTS)]
NTH = [SLOT[:c].count(SLOT[c]) for c in range(NPRE)]
EXPERT_CHUNKS = 12


class Regions:

    def __init__(self, at):
        self.at = at

    def take(self, n):
        self.at += n
        return self.at - n


M0 = EARLY * CHUNK
LATE = M0 + CHUNK
ROW = CT * T
RW = [LATE + ROW * i for i in range(12)]
SCAN = LATE + 12 * ROW
_keep = Regions(SLOTS * CHUNK)
XT, VECO, CONO, SMWO = (_keep.take(n) for n in (KT * T, NVEC, NCON, NSMW))
MK, MV, MEMT = (_keep.take(2048) for _ in range(3))
WORK = _keep.at
_w = Regions(WORK)
N1, UWIN, FO, EO, S5O, PWO, UT = (_w.take(n) for n in (KT * T, 8 * T, 1024, 1024, NS5P, 448, CT * (T + 7)))
X0T, YL, KKO, MIX, PEND, SHIFT = (_w.take(n) for n in (T, T, 256, KT * T, 48, 144))
RW += [N1 + ROW * i for i in range(8)]
CAO = RW[10]
TOTAL = 53200
_w = Regions(WORK)
NT, QT, PROB, SPROB, PT, SPT, OT = (_w.take(n) for n in (KT * T, KT * T, 2048, 512, 2048, 512, KT * T))
QBLK = MEMT
RX, STAT = TOTAL - 400, TOTAL - 80
assert _w.at <= RX and SHIFT + 144 <= RX
HTOK, YACC = MK, MK + TT * D
_w = Regions(PROB)
(BIAS, XTE, HG, HU, SIG, HACT, ACTT, YB, SELG, SEL, GTT, TAB, CUR, GFIN, RB, SCR) = (
    _w.take(n) for n in (2 * FF, KT * CAP, 512, 512, 512, 512, 512, 512, TT * P, TT * CAP, TT * P, 6 * (NE + 1), 8, D, NE, 1200))
assert _w.at <= TOTAL
BDOWN = NT
assert SCAN + 1024 <= SLOTS * CHUNK and RW[19] + ROW <= X0T and _w.at <= TOTAL



def _tiles(kind, name, lo, hi):
    return [(kind, f"{name}{i}" if name else i) for i in range(lo, hi)]


IN_ORDER = "kzrv"
MIX_ORDER = ([("load", 0), ("load", 1), ("f", 0), ("memnorm", 0)] + _tiles("in", "k", 0, 4) + [("win", 0), ("par", 0), ("c", 0)] + _tiles("in", "z", 0, 2)
             + [("f", 1), ("blk", 0), ("y", 0), ("win", 1)] + _tiles("in", "z", 2, 4)
             + [("mix", "k"), ("par", 1), ("load", 2), ("blk", 1), ("f", 2), ("y", 1), ("win", 2)] + _tiles("in", "r", 0, 2)
             + [("mix", "z"), ("out", 0), ("c", 1)] + _tiles("in", "r", 2, 4)
             + [("load", 3), ("par", 2), ("blk", 2), ("f", 3), ("y", 2), ("win", 3), ("mix", "r")] + _tiles("in", "v", 0, 2)
             + [("out", 1), ("par", 3), ("blk", 3), ("y", 3), ("c", 2)] + _tiles("in", "v", 2, 4)
             + [("out", 2), ("mix", "v"), ("lora_up", 0), ("memk", 0), ("memk", 1), ("kk", 0), ("c", 3), ("knorm", 0), ("memk", 2),
                ("lora_down", 0), ("memk", 3), ("out", 3), ("decays", 0), ("memk", 4), ("memk", 5), ("glu", 0)])
TILES4 = range(4)


GRAM_ORDER = (4, 0, 1, 2, 3)


def rwkv_names():
    yield from [f"t{a}{i}" for i in TILES4 for a in "bvka"]
    yield from [f"g{a}{i}" for i in GRAM_ORDER for a in "bk"]
    yield from [f"y0_{i}" for i in TILES4]
    for lv in range(1, 6):
        for i in TILES4:
            yield f"y{lv}_{i}"
        for i in TILES4:
            yield f"dt{lv}_{i}"
            if lv < 5:
                yield f"dx{lv}_{i}"
    for i in TILES4:
        yield from [f"gt{i}", f"bv{i}"]
    yield from [f"us{i}" for i in TILES4]
    yield from [f"hh{i}" for i in TILES4]
    for c in range(PC):
        if c:
            yield f"u_{c}"
        yield from [f"m_{c}", f"yy{c}"]
    yield from [f"ys{i}" for i in TILES4]
    yield from [f"sf{i}" for i in TILES4]


MEM_V = [f"mv{q}{t}" for q in range(4) for t in range(2)]
FILLERS = ["mk6", "mk7"] + MEM_V


def job_names():
    yield from ["ss_x", "ss_m"] + [f"u{i}" for i in TILES4]
    for kind, n in MIX_ORDER:
        if kind == "par":
            yield from [f"er{n}", f"ei{n}", f"kk{n}"]
        elif kind == "in":
            yield n
        elif kind == "blk":
            yield from [f"ve{n}", f"loc{n}"]
        elif kind == "out":
            yield f"st{n}"
        elif kind == "lora_up":
            yield from ["lw", "la", "lg"]
        elif kind == "lora_down":
            yield from [f"{a}{i}" for a in ("dw", "da", "dg") for i in TILES4]
        elif kind == "memk":
            yield f"mk{n}"
        elif kind == "knorm":
            yield from [f"kn{i}" for i in TILES4]
        elif kind == "glu":
            yield from [f"gl{i}" for i in TILES4]
    yield from [f"bo{i}" for i in TILES4]
    yield from rwkv_names()
    yield from FILLERS
    yield from [f"me{i}" for i in TILES4]
    yield from [f"va{i}" for i in TILES4]
    yield from [f"o{n}" for n in range(8)]
    yield from ["q0", "q1", "ss_c"] + [f"q{n}" for n in range(2, 8)]
    yield from [f"sp{h}" for h in range(MH)]
    yield from [f"sb{i}" for i in range(2)]
    yield from [f"tp{i}" for i in range(4)]
    yield "tb"
    yield from [f"op{n}" for n in range(8)]
    yield from [f"{a}{g}{h}" for a in ("ob", "ox") for g in range(2) for h in range(2)]
    yield from [f"co{n}" for n in range(8)]
    yield from ["ss_f", "lgt"]
    yield from [f"tx{t}{h}" for t in range(TT) for h in range(2)]
    yield "lt"
    yield from [f"th{t}{h}" for t in range(TT) for h in range(2)]
    yield from ["pos", "cnt"]


RWKV_JOBS = list(rwkv_names())
_RATES = (("tb0", KT), ("t", 0.32), ("gb", 0.4), ("gk", 0.4), ("y0_0", 4), ("y0", 0.6), ("y1", 0.6), ("dt1", 0.5), ("dx1", 0.5),
          ("y2", 0.45), ("dt2", 0.45), ("dx2", 0.45), ("yy", 1), ("ys", 2), ("y", 0.36), ("d", 0.36), ("hh", 1), ("m_0", 3), ("m_", 2),
          ("u_", 1), ("us", 0), ("sf", 0), ("", 0.5))


def _fill():
    units, at, due, fill = [(job, k) for job in FILLERS for k in range(KT)], 0, 0.0, {}
    for job in RWKV_JOBS:
        due += next(rate for prefix, rate in _RATES if job.startswith(prefix))
        n = len(units) if job == RWKV_JOBS[-1] else int(due)
        fill[job] = units[at:n]
        at = max(at, n)
    return fill


FILL_AT = _fill()
FILL_DONE = {job: [f for f, k in units if k == KT - 1] for job, units in FILL_AT.items()}


def _banks():
    job, uses, at = {}, [0] * 8, 0
    for name in job_names():
        assert name not in job
        if name in FILLERS:
            bank = 6 + FILLERS.index(name) % 2
        elif name in RWKV_JOBS:
            bank = RWKV_JOBS.index(name) % 6
        else:
            bank, at = at % 8, at + 1
        job[name] = (bank, uses[bank])
        uses[bank] += 1
    return job, uses


JOB, _uses = _banks()
BANK_USES = list(_uses)


LAST_JOB = (["u1", "u3"] + [f"{c}{i}" for c in IN_ORDER for i in (1, 3)] + [f"mk{i}" for i in (1, 3, 5, 7)] + ["gl3"]
            + [f"mv{q}1" for q in range(4)]
            + [f"o{i}" for i in (1, 3, 5, 7)] + [f"q{i}" for i in (1, 3, 5, 7)] + ["sb0"] * 4 + ["sb1"] * 4
            + ["ob01"] * 4 + ["ob11"] * 4 + [f"co{i}" for i in (1, 3, 5, 7)])
assert len(LAST_JOB) == NPRE


def build(nc, a, o):
    with ExitStack() as ctx:
        BIG = ctx.enter_context(nc.sbuf_tensor("big", [P, TOTAL], F32))
        ps = [ctx.enter_context(nc.psum_tensor(f"bank{i}", [P, 512], F32)) for i in range(8)]
        u_dram = nc.dram_tensor("u_windows", [W5, T + 7], F32)
        sems = {}

        def S(name):
            if name not in sems:
                sems[name] = ctx.enter_context(nc.semaphore(name))
            return sems[name]

        psum_full = [S(f"psum_full{i}") for i in range(8)]
        psum_free = [S(f"psum_free{i}") for i in range(8)]
        ring_full = [S(f"ring_full{i}") for i in range(SLOTS)]

        def view(at, *shape, lo=0, hi=P):
            n = int(np.prod(shape))
            v = BIG[lo:hi, at:at + n]
            names = "abcd"[:len(shape)]
            if len(shape) == 1:
                return v
            return v.rearrange(f"p ({' '.join(names)}) -> p {' '.join(names)}", **dict(zip(names, shape)))

        def con(name, lo=0, hi=P):
            at, n = CON[name]
            return BIG[lo:hi, CONO + at:CONO + at + n]

        def vec(name, i=0):
            at, _ = VEC[name]
            return BIG[:, VECO + at + i:VECO + at + i + 1]

        def smw(name, *shape):
            return view(SMWO + SMW[name][0], *shape)

        def s5p(name, *shape):
            return view(S5O + S5P[name][0], *shape)

        def over(ap, axis, n):
            v = ap.unsqueeze(axis)
            shape = list(v.shape)
            shape[axis] = n
            return v.to_broadcast(shape)

        class Steps:

            def __init__(self, eng, own):
                self.eng, self.own, self.count = eng, S(own), {}

            def __call__(self, ins, signal=None):
                sem = self.own if signal is None else S(signal)
                key = signal or ""
                self.count[key] = self.count.get(key, 0) + 1
                ins.then_inc(sem, 1)
                self.eng.wait_ge(sem, self.count[key])

            def read_out(self, ins, job):
                bank, n = JOB[job]
                ins.then_inc(psum_free[bank], 1)
                self.eng.wait_ge(psum_free[bank], n + 1)

        def computed(eng, job):
            bank, n = JOB[job]
            eng.wait_ge(psum_full[bank], n + 1)
            return ps[bank]

        def stored(eng, job):
            bank, n = JOB[job]
            eng.wait_ge(psum_free[bank], n + 1)

        xT, n1 = view(XT, KT, T), view(N1, KT, T)
        memT = view(MEMT, KT, NM)
        m0 = view(M0, CT, NB, HN)
        mkT, mv = view(MK, KT, NM), view(MV, 2, D)
        mix = view(MIX, KT, T)
        uT = view(UT, CT, T + 7)
        uwins = [view(at, 8, T) for at in (UWIN, RW[8])]
        F_r, F_i = (view(FO + 512 * i, PAIRS, P) for i in range(2))
        E_r, E_i = (view(EO + 512 * i, PAIRS, P) for i in range(2))
        ca_r, ca_i = (view(CAO + 1024 * i, PAIRS, BL, 32) for i in range(2))
        pw_r, pw_i = (view(PWO + 144 * i, BL + 1, 16) for i in range(2))
        x0 = view(X0T, 2, PAIRS, NBL)
        kkz = view(KKO, 8, 32)
        R = [view(at, CT, T) for at in RW]
        Rc = [view(at, CT, NC, CH) for at in RW]
        xsq, memsq = view(UWIN, KT, T), view(RW[8], KT, NM)
        prj = {"r": R[0], "k": R[1], "v": R[2], "z": R[3]}
        dlt = {"r": R[4], "k": R[5], "v": R[6], "z": R[7]}
        PRJ_ORDER = ("r", "k", "v", "z")
        hidden = {nm: view(RW[8] + i * T, T) for i, nm in enumerate(("dw", "da", "dg"))}
        cbd_r, cbd_i = s5p("cr", 16, 32), s5p("ci", 16, 32)
        xes = [view(SCAN + 320 * i, 2, PAIRS, NBL) for i in range(2)]
        w1, w2 = (view(CAO + 2048 + 256 * i, 2, PAIRS, PBL) for i in range(2))
        yl = [mix[:, CT + 1 + ct % 3, :] for ct in range(CT)]
        s5fin = view(MIX + CT * T, 2, 16, NB + 1)
        pend = view(PEND, CT, PC + NB)
        shift = view(SHIFT, 4, CT, NB + 1)
        ar = view(RW[10], CT, NC, 2, CH)
        bT, vT, kT, aT = Rc[3], Rc[4], Rc[9], Rc[12]
        AT, BT, C1, C2 = Rc[8], Rc[13], Rc[14], Rc[15]
        X, XI, Y, al = Rc[16], Rc[17], Rc[18], Rc[19]
        GT, BV, H, U = Rc[6], Rc[7], Rc[18], Rc[19]
        M = view(RW[16], PC, CT, HN)
        um, vm = (view(at, 2, NB * HN) for at in (RW[0], RW[17]))
        YT, ysq, gn = R[13], R[14], R[15]

        most_i32 = ctx.enter_context(nc.sbuf_tensor("most_tokens", [P, 1], I32))

        def most_tokens(eng):
            eng.wait_ge(S("counts"), 1)
            return eng.value_load(most_i32[0:1, 0:1], min_val=0, max_val=T)

        def all_passes(eng, expert, next_pass=None):
            with eng.Fori(0, NE) as e:
                expert(e, e)
            most = most_tokens(eng)
            with eng.Fori(1, PASSES) as p:
                with eng.If(most > p * CAP):
                    if next_pass:
                        next_pass(p)
                    with eng.Fori(0, NE) as e:
                        expert(p * NE + e, e)

        nT, qT, oT, rx2 = view(NT, KT, T), view(QT, KT, T), view(OT, KT, T), view(RX, T)
        prob, sprob = view(PROB, MH, 2, NM), view(SPROB, 2, NM)
        pT, spT = view(PT, MH, 2, TP), view(SPT, 2, 2, P)
        srow = view(PROB, 2, D)
        qblk = view(QBLK, KT, NB, MH * TS)
        hT, htok, yacc = view(QT, KT, T), view(HTOK, TT, D), view(YACC, TT, D)
        bias, xte = view(BIAS, 2 * FF), view(XTE, KT, CAP)
        hg, hu, sig, hact = (view(x, 512) for x in (HG, HU, SIG, HACT))
        actT, yb = view(ACTT, 4, P), view(YB, 512)
        selg, sel, gtt = view(SELG, TT, P), view(SEL, TT, CAP), view(GTT, TT, P)
        tab, cur = view(TAB, NE + 1, 6), view(CUR, 8)
        hrow = view(SCR + 584, 512)
        gfin, rbias, bdown = view(GFIN, D), view(RB, NE), view(BDOWN, D)
        logit, mask, gate = (view(SCR + 96 * i, TT, NE) for i in range(3))
        top, idx = view(SCR + 288, TT, 8), view(SCR + 312, TT, 8)
        idx_u = idx.bitcast(U32)
        idxf, g4, gsum = view(SCR + 336, TT, 8), view(SCR + 360, TT, 4), view(SCR + 372, TT)
        eq, eg = view(SCR + 384, TT, NE), view(SCR + 480, TT, NE)
        lgt, rxt = view(SCR + 600, T, hi=NE), view(SCR + 376, TT)
        tile_rows = [P, P, T - 2 * P]

        block = ctx.enter_context(nc.Block())

        @block.sync
        def _(sp):
            sp.dma_start(xT, a["xT"]).then_inc(S("x_in"), 16)
            sp.dma_start(view(CONO, NCON), a["consts"]).then_inc(S("consts_in"), 16)
            sp.dma_start(view(VECO, NVEC), a["vecs"]).then_inc(S("vecs_in"), 16)
            for c in range(NPRE):
                if c == 1:
                    sp.dma_start(memT, a["memT"]).then_inc(S("mem_in"), 16)
                    sp.dma_start(view(S5O, NS5P), a["s5p"]).then_inc(S("s5p_in"), 16)
                if c == EARLY:
                    sp.dma_start(view(SMWO, NSMW), a["smw"]).then_inc(S("smw_in"), 16)
                if c == 2 * EARLY:
                    sp.dma_start(m0, a["m0"]).then_inc(S("m0_in"), 16)
                if SLOT[c] >= EARLY and PREV[c] is None:
                    sp.wait_ge(S("mix_ready"), CT)
                    if SLOT[c] == EARLY:
                        sp.wait_ge(S("wkv_stored"), 16)
                if PREV[c] is not None:
                    computed(sp, LAST_JOB[PREV[c]])
                sp.dma_start(view(SLOT[c] * CHUNK, CHUNK), a["dense"][c]).then_inc(ring_full[SLOT[c]], 16)

            def expert_chunk(j, e):
                return a["w_gu"][e, j * P:(j + 1) * P, :] if j < 8 else \
                    a["w_down"][e, (j - 8) * 2 * P:(j - 7) * 2 * P, :].rearrange("(i p) n -> p i n", i=2)

            def expert_dst(j):
                at = EXPERT_SLOT[j] * CHUNK
                return view(at, CHUNK) if j < 8 else view(at, 2, D)

            for j in range(EXPERT_CHUNKS):
                computed(sp, LAST_JOB[NPRE - EXPERT_CHUNKS + j])
                sp.dma_start(expert_dst(j), expert_chunk(j, 0)).then_inc(ring_full[EXPERT_SLOT[j]], 16)
            sp.wait_ge(S("bias_zero"), 1)
            sp.dma_start(BIG[0:1, BIAS:BIAS + 2 * FF], a["b_gu"][0:1, :]).then_inc(S("bias_in"), 16)

            def load_bias(it, e):
                sp.wait_ge(S("bias_used"), it + 1)
                sp.dma_start(BIG[0:1, BDOWN:BDOWN + D], a["b_down"][bass.ds(e, 1), :]).then_inc(S("bdown_in"), 16)
                sp.dma_start(BIG[0:1, BIAS:BIAS + 2 * FF], a["b_gu"][bass.ds(e + 1, 1), :]).then_inc(S("bias_in"), 16)

            sp.wait_ge(S("bdown_zero"), 1)
            load_bias(0, 0)

            def load_expert(it, e):
                for j in range(EXPERT_CHUNKS):
                    if j == 7:
                        sp.wait_ge(psum_full[1], it + BANK_USES[1])
                    elif j == 11:
                        sp.wait_ge(psum_full[4], it * 2 + (BANK_USES[4] - 1))
                    else:
                        sp.wait_ge(S("chunk_used"), it * 10 + ((j if j < 7 else j - 1) - 9))
                    sp.dma_start(expert_dst(j), expert_chunk(j, e)).then_inc(ring_full[EXPERT_SLOT[j]], 16)
                load_bias(it, e)

            with sp.Fori(1, NE) as e:
                load_expert(e, e)
            most = most_tokens(sp)
            with sp.Fori(1, PASSES) as p:
                with sp.If(most > p * CAP):
                    with sp.Fori(0, NE) as e:
                        load_expert(p * NE + e, e)
            for t in range(TT):
                sp.wait_ge(S("final"), t + 1)
                sp.dma_start(o["y"][:, t], view(HTOK, TT, D)[:, t]).then_inc(S("y_out"), 16)
            sp.wait_ge(S("stores"), 16 * 3)
            sp.wait_ge(S("wkv_p_stored"), 16)
            sp.wait_ge(S("wkv_stored"), 16)
            sp.wait_ge(S("s5_stored"), 16)
            sp.wait_ge(S("y_out"), 16 * TT)

        @block.tensor
        def _(pe):
            def start_job(job):
                for filler, k in FILL_AT.get(job, ()):
                    fill(filler, k)
                bank, n = JOB[job]
                if n:
                    pe.wait_ge(psum_free[bank], n)
                return ps[bank]

            def end_job(ins, job):
                ins.then_inc(psum_full[JOB[job][0]], 1)

            def chunk(c, *shape):
                pe.wait_ge(ring_full[SLOT[c]], 16 * (NTH[c] + 1))
                return view(SLOT[c] * CHUNK, *shape)

            mm = nc.tensor.matmul

            def sums(job, src, n, ones):
                b = start_job(job)
                for k in range(KT):
                    last = mm(b[:, 0:n], ones, src[:, k, :], start=(k == 0), stop=(k == KT - 1))
                end_job(last, job)

            def dense(job, w, src, n, kt=KT):
                b = start_job(job)
                for k in range(kt):
                    last = mm(b[:, 0:n], w[:, k, :], src[:, k, :], start=(k == 0), stop=(k == kt - 1))
                end_job(last, job)

            def dense_stream(first, i, job, src, n):
                dense(job, chunk(first + i // 2, 2, KT, P)[:, i % 2], src, n)

            pe.wait_ge(S("consts_in"), 16)
            ones, ident, headones = con("ones"), con("ident"), con("headones")
            pe.wait_ge(S("xsq"), KT)
            sums("ss_x", xsq, T, ones)
            pe.wait_ge(S("memsq"), 1)
            sums("ss_m", memsq, NM, ones)
            b, w = start_job("u0"), chunk(FIRST["in"], 2, KT, P)
            for k in range(KT):
                pe.wait_ge(S("n1"), k + 1)
                last = mm(b[:, 0:T], w[:, 0, k, :], n1[:, k, :], start=(k == 0), stop=(k == KT - 1))
            end_job(last, "u0")
            for i in range(1, 4):
                dense_stream(FIRST["in"], i, f"u{i}", n1, T)

            def s5_params(ct):
                pe.wait_ge(S("s5_f"), ct + 1)
                for nm, src in (("er", F_r), ("ei", F_i)):
                    b = start_job(f"{nm}{ct}")
                    for q in range(PAIRS):
                        last = nc.tensor.transpose(b[:, q * P:(q + 1) * P], src[:, q, :], ident)
                    end_job(last, f"{nm}{ct}")
                b = start_job(f"kk{ct}")
                for q in range(PAIRS):
                    mm(b[:, 32 * q:32 * q + 32], F_r[:, q, :], cbd_r[:, PAIRS * ct + q, :], start=True, stop=False)
                    last = mm(b[:, 32 * q:32 * q + 32], F_i[:, q, :], cbd_i[:, PAIRS * ct + q, :], start=False, stop=True)
                end_job(last, f"kk{ct}")

            def s5_block(ct):
                pe.wait_ge(S("uwin"), ct + 1)
                uwin = uwins[ct % 2]
                stored(pe, f"ei{ct}")
                b = start_job(f"ve{ct}")
                for q in range(PAIRS):
                    for g in range(2):
                        for ri, e in ((0, E_r), (1, E_i)):
                            at = (ri * PAIRS + q) * NBL
                            last = mm(b[64 * g:64 * g + 64, at:at + NBL], e[:, q, 64 * g:64 * g + 64],
                                      uwin[:, 2 * q + g, BL - 1::BL], start=True, stop=True)
                end_job(last, f"ve{ct}")
                stored(pe, f"kk{ct}")
                b = start_job(f"loc{ct}")
                for g in range(2):
                    for q in range(PAIRS):
                        last = mm(b[32 * q:32 * q + 32, 0:T], kkz[:, 2 * q + g, :], uwin[:, 2 * q + g, :],
                                  start=(g == 0), stop=(g == 1))
                end_job(last, f"loc{ct}")

            def s5_out(ct):
                pe.wait_ge(S("s5_ca"), ct + 1)
                pe.wait_ge(S("s5_x0"), ct + 1)
                b = start_job(f"st{ct}")
                for j in range(BL):
                    for ri, c in ((0, ca_r), (1, ca_i)):
                        for q in range(PAIRS):
                            last = mm(b[32 * q:32 * q + 32, j * NBL:(j + 1) * NBL], c[:, q, BL - 1 - j, :], x0[:, ri, q, :],
                                      start=(ri == 0), stop=(ri == 1))
                end_job(last, f"st{ct}")

            def mem_k(i):
                pe.wait_ge(S("nmem"), KT)
                dense_stream(FIRST["memk"], i, f"mk{i}", memT, NM)

            def fill(job, k):
                b = start_job(job) if k == 0 else ps[JOB[job][0]]
                if job.startswith("mk"):
                    n = int(job[2])
                    ins = mm(b[:, 0:NM], chunk(FIRST["memk"] + n // 2, 2, KT, P)[:, n % 2, k, :], memT[:, k, :],
                             start=(k == 0), stop=(k == KT - 1))
                else:
                    q, t = int(job[2]), int(job[3])
                    ins = mm(b[:, 0:256], memT[:, k, t * P:(t + 1) * P], chunk(FIRST["memv"] + q, KT, 256)[:, k, :],
                             start=(k == 0), stop=(k == KT - 1))
                if k == KT - 1:
                    end_job(ins, job)

            def lora_up():
                pe.wait_ge(S("smw_in"), 16)
                pe.wait_ge(S("z_mixed"), 12)
                for job, w, n, src in (("lw", smw("w1", CT, 64), 64, R[4]), ("la", smw("a1", CT, 64), 64, R[5]),
                                       ("lg", smw("g1", CT, P), P, R[6])):
                    b = start_job(job)
                    for k in range(CT):
                        last = mm(b[0:n, 0:T], w[:, k, :], src[:, k, :], start=(k == 0), stop=(k == CT - 1))
                    end_job(last, job)

            def lora_down():
                for nm, up, w, n in (("dw", "lw", "w2", 64), ("da", "la", "a2", 64), ("dg", "lg", "g2", P)):
                    stored(pe, up)
                    for i in TILES4:
                        b = start_job(f"{nm}{i}")
                        end_job(mm(b[:, 0:T], smw(w, CT, P)[0:n, i, :], hidden[nm][0:n, :], start=True, stop=True), f"{nm}{i}")

            def head_sums(nm, src, ready=None, each=0):
                for i in TILES4:
                    if ready:
                        pe.wait_ge(S(ready), 1 + i * each)
                    b = start_job(f"{nm}{i}")
                    end_job(mm(b[:, 0:T], headones, src[:, i, :], start=True, stop=True), f"{nm}{i}")

            for kind, n in MIX_ORDER:
                if kind == "in":
                    dense_stream(FIRST["in"] + 2 + 2 * IN_ORDER.index(n[0]), int(n[1]), n, n1, T)
                elif kind == "par":
                    s5_params(n)
                elif kind == "blk":
                    s5_block(n)
                elif kind == "out":
                    s5_out(n)
                elif kind == "lora_up":
                    lora_up()
                elif kind == "lora_down":
                    lora_down()
                elif kind == "memk":
                    mem_k(n)
                elif kind == "knorm":
                    head_sums("kn", R[6], "kk_squares")
                elif kind == "glu":
                    pe.wait_ge(S("s5_gelu"), CT)
                    w = chunk(FIRST["glu"], CT, CT, P)
                    for i in TILES4:
                        dense(f"gl{i}", w[:, i], mix, T, kt=CT)

            halves = [(0, slice(0, 64)), (1, slice(64, 128))]
            head_sums("bo", R[8], "rkr")
            pe.wait_ge(S("rw_keys"), 4)
            for i in TILES4:
                for nm, src in (("b", Rc[6]), ("v", Rc[2]), ("k", Rc[7]), ("a", ar[:, :, :, 0, :])):
                    b = start_job(f"t{nm}{i}")
                    for c in range(NC):
                        for _, h in halves:
                            last = mm(b[h, c * CH:(c + 1) * CH], src[h, i, c, :], con("ident64")[h, :], start=True, stop=True)
                    end_job(last, f"t{nm}{i}")
            for i in GRAM_ORDER:
                for nm, src in (("b", Rc[6]), ("k", Rc[7])):
                    b = start_job(f"g{nm}{i}")
                    for n in range(4):
                        t, c = (i, n) if i < 4 else (n, PC)
                        for _, h in halves:
                            last = mm(b[h, n * P:(n + 1) * P], src[h, t, c, :],
                                      ar[h, t, c, :, :].rearrange("p a b -> p (a b)"), start=True, stop=True)
                    end_job(last, f"g{nm}{i}")
            for i in TILES4:
                pe.wait_ge(S("a_level"), i + 1)
                b = start_job(f"y0_{i}")
                for c in range(NC):
                    for _, h in halves:
                        last = mm(b[h, c * CH:(c + 1) * CH], al[h, i, c, :], con("ident64")[h, :], start=True, stop=True)
                end_job(last, f"y0_{i}")
            for lv in range(1, 6):
                n = NC if lv < 3 else PC
                for i in TILES4:
                    pe.wait_ge(S("a_level"), 4 * lv + i + 1)
                    b = start_job(f"y{lv}_{i}")
                    for c in range(n):
                        for _, h in halves:
                            last = mm(b[h, c * CH:(c + 1) * CH], al[h, i, c, :], X[h, i, c, :], start=True, stop=True)
                    end_job(last, f"y{lv}_{i}")
                for i in TILES4:
                    stored(pe, f"y{lv}_{i}")
                    for job, lhs, rhs in ((f"dt{lv}_{i}", Y, XI), (f"dx{lv}_{i}", XI, Y))[:2 if lv < 5 else 1]:
                        b = start_job(job)
                        for c in range(n):
                            for _, h in halves:
                                last = mm(b[h, c * CH:(c + 1) * CH], lhs[h, i, c, :], rhs[h, i, c, :], start=True, stop=True)
                        end_job(last, job)
            for i in TILES4:
                stored(pe, f"dt5_{i}")
                for job, lhs, rhs in ((f"gt{i}", aT, XI), (f"bv{i}", BT, vT)):
                    b = start_job(job)
                    for c in range(NC):
                        for _, h in halves:
                            last = mm(b[h, c * CH:(c + 1) * CH], lhs[h, i, c, :], rhs[h, i, c, :], start=True, stop=True)
                    end_job(last, job)
            pe.wait_ge(S("m0_in"), 16)
            for i in TILES4:
                stored(pe, f"gt{i}")
                b = start_job(f"us{i}")
                for _, h in halves:
                    last = mm(b[h, :], GT[h, i, PC, :], m0[h, i].rearrange("p a b -> p (a b)"), start=True, stop=True)
                end_job(last, f"us{i}")
            for i in TILES4:
                stored(pe, f"bv{i}")
                b = start_job(f"hh{i}")
                for c in range(NC):
                    for _, h in halves:
                        last = mm(b[h, c * CH:(c + 1) * CH], XI[h, i, c, :], BV[h, i, c, :], start=True, stop=True)
                end_job(last, f"hh{i}")
            pe.wait_ge(S("u_first"), 1)
            for c in range(PC):
                if c:
                    stored(pe, f"m_{c - 1}")
                    if c > 1:
                        pe.wait_ge(S("m_ready"), c - 1)
                    b = start_job(f"u_{c}")
                    for i in TILES4:
                        for _, h in halves:
                            last = mm(b[h, i * HN:(i + 1) * HN], GT[h, i, c, :], M[h, c - 1, i, :], start=True, stop=True)
                    end_job(last, f"u_{c}")
                    stored(pe, f"u_{c}")
                b = start_job(f"m_{c}")
                for i in TILES4:
                    for _, h in halves:
                        mm(b[h, i * HN:(i + 1) * HN], kT[h, i, c, :], vT[h, i, c, :], start=True, stop=False)
                        last = mm(b[h, i * HN:(i + 1) * HN], bT[h, i, c, :], U[h, i, c, :], start=False, stop=True)
                end_job(last, f"m_{c}")
                b = start_job(f"yy{c}")
                for i in TILES4:
                    for _, h in halves:
                        mm(b[h, i * CH:(i + 1) * CH], vT[h, i, c, :], C2[h, i, c, :], start=True, stop=False)
                        last = mm(b[h, i * CH:(i + 1) * CH], U[h, i, c, :], C1[h, i, c, :], start=False, stop=(c == 0))
                        if c:
                            last = mm(b[h, i * CH:(i + 1) * CH], M[h, c - 1, i, :], ar[h, i, c, 1, :], start=False, stop=True)
                end_job(last, f"yy{c}")
            for i in TILES4:
                pe.wait_ge(S("u_sample"), 1)
                b = start_job(f"ys{i}")
                for _, h in halves:
                    mm(b[h, 0:CH], vT[h, i, PC, :], C2[h, i, PC, :], start=True, stop=False)
                    mm(b[h, 0:CH], U[h, i, PC, :], C1[h, i, PC, :], start=False, stop=False)
                    for s in range(NB):
                        last = mm(b[h, s * TS:(s + 1) * TS], m0[h, i, s, :], ar[h, i, PC, 1, s * TS:(s + 1) * TS],
                                  start=False, stop=(s == NB - 1))
                end_job(last, f"ys{i}")
            for i in TILES4:
                pe.wait_ge(S("uv_masked"), i + 1)
                b = start_job(f"sf{i}")
                for _, h in halves:
                    mm(b[h, :], kT[h, i, PC, :], vm[h, i % 2, :], start=True, stop=False)
                    last = mm(b[h, :], bT[h, i, PC, :], um[h, i % 2, :], start=False, stop=True)
                end_job(last, f"sf{i}")
            stored(pe, "ys3")
            head_sums("me", YT)
            head_sums("va", ysq, "y_squares", each=1)

            def w_out(n, ks):
                w = chunk(FIRST["out"] + n // 2, 2, KT, P)[:, n % 2]
                b = start_job(f"o{n}") if ks[0] == 0 else ps[JOB[f"o{n}"][0]]
                for k in ks:
                    last = mm(b[:, 0:T], w[:, k, :], mix[:, k, :], start=(k == 0), stop=(k == KT - 1))
                return last

            pe.wait_ge(S("s5_gated"), CT)
            for n in range(2 * EARLY):
                w_out(n, range(CT))
            pe.wait_ge(S("mix_ready"), CT)
            for n in range(2 * EARLY):
                end_job(w_out(n, range(CT, KT)), f"o{n}")
            for n in range(2 * EARLY, KT):
                end_job(w_out(n, range(KT)), f"o{n}")

            pe.wait_ge(S("x1g"), KT)
            for n in range(KT):
                if n == 2:
                    pe.wait_ge(S("x1sq"), KT)
                    sums("ss_c", qT, T, ones)
                dense_stream(FIRST["cq"], n, f"q{n}", nT, T)
            stored(pe, "q7")
            stored(pe, "mk7")
            for job in MEM_V[-2:]:
                stored(pe, job)
            for h in range(MH):
                b = start_job(f"sp{h}")
                for t in range(2):
                    for i in range(2):
                        last = mm(b[:, t * NM:(t + 1) * NM], qT[:, 2 * h + i, t * P:(t + 1) * P], mkT[:, 2 * h + i, :],
                                  start=(i == 0), stop=(i == 1))
                end_job(last, f"sp{h}")
            pe.wait_ge(S("qblk"), MH)
            for g in range(2):
                b = start_job(f"sb{g}")
                for n in range(KT):
                    for i in range(4):
                        s = 4 * g + i
                        w = chunk(FIRST["kcache"] + s, KT, NM)
                        last = mm(b[32 * i:32 * i + 32, 0:NM], qblk[:, n, s, :], w[:, n, :], start=(n == 0), stop=(n == KT - 1))
                end_job(last, f"sb{g}")
            for h in range(MH):
                pe.wait_ge(S("prob"), h + 1)
                b = start_job(f"tp{h}")
                for m in range(2):
                    for t in range(2):
                        last = nc.tensor.transpose(b[:, (2 * m + t) * P:(2 * m + t + 1) * P], prob[:, h, t, m * P:(m + 1) * P], ident)
                end_job(last, f"tp{h}")
            pe.wait_ge(S("prob"), MH + 2)
            b = start_job("tb")
            for g in range(2):
                for m in range(2):
                    last = nc.tensor.transpose(b[:, (2 * g + m) * P:(2 * g + m + 1) * P], sprob[:, g, m * P:(m + 1) * P], ident)
            end_job(last, "tb")
            for n in range(KT):
                stored(pe, f"tp{n // 2}")
                b = start_job(f"op{n}")
                for m in range(2):
                    last = mm(b[:, 0:TP], mv[:, m, n * P:(n + 1) * P], pT[:, n // 2, m, :], start=(m == 0), stop=(m == 1))
                end_job(last, f"op{n}")
            stored(pe, "tb")
            for g in range(2):
                for half in range(2):
                    b = start_job(f"ob{g}{half}")
                    for m in range(2):
                        for i in range(4):
                            w = chunk(FIRST["vcache"] + 4 * g + i, 2, D)
                            last = mm(b[32 * i:32 * i + 32, :], spT[:, g, m, i * 32:(i + 1) * 32], w[:, m, half * 512:half * 512 + 512],
                                      start=(m == 0), stop=(m == 1))
                    end_job(last, f"ob{g}{half}")
            for g in range(2):
                for half in range(2):
                    stored(pe, f"ob{g}{half}")
                    b = start_job(f"ox{g}{half}")
                    for n in range(4):
                        at = half * 512 + n * P
                        last = nc.tensor.transpose(b[:, n * P:(n + 1) * P], srow[:, g, at:at + P], ident)
                    end_job(last, f"ox{g}{half}")
            stored(pe, "ox11")
            for n in range(KT):
                dense_stream(FIRST["co"], n, f"co{n}", oT, T)

            pe.wait_ge(S("x2sq"), KT)
            sums("ss_f", nT, T, ones)
            pe.wait_ge(S("x2g"), KT)
            b = start_job("lgt")
            for k in range(KT):
                last = mm(b[0:NE, 0:T], smw("router_w", KT, NE)[:, k, :], hT[:, k, :], start=(k == 0), stop=(k == KT - 1))
            end_job(last, "lgt")
            for nm, src in (("tx", xT), ("th", hT)):
                if nm == "th":
                    stored(pe, "lgt")
                    b = start_job("lt")
                    for t in range(TT):
                        rows = slice(t * P, t * P + tile_rows[t])
                        mm(b[0:tile_rows[t], t * NE:(t + 1) * NE], lgt[:, rows], ident[0:NE, 0:NE], start=True, stop=True)
                        last = mm(b[0:tile_rows[t], TT * NE + t:TT * NE + t + 1], rx2[0:NE, rows], ident[0:NE, 0:1], start=True, stop=True)
                    end_job(last, "lt")
                for t in range(TT):
                    for h in range(2):
                        b = start_job(f"{nm}{t}{h}")
                        for i in range(4):
                            last = nc.tensor.transpose(b[0:tile_rows[t], i * P:(i + 1) * P], src[:, 4 * h + i, t * P:t * P + tile_rows[t]], ident)
                        end_job(last, f"{nm}{t}{h}")
            pe.wait_ge(S("mask"), 1)
            b = start_job("pos")
            for t in range(TT):
                for s in range(t + 1):
                    last = mm(b[:, t * NE:(t + 1) * NE], con("earlier") if s == t else ones, mask[:, s, :], start=(s == 0), stop=(s == t))
            end_job(last, "pos")
            b = start_job("cnt")
            for s in range(TT):
                last = mm(b[:, 0:NE], ones, mask[:, s, :], start=(s == 0), stop=(s == TT - 1))
            end_job(last, "cnt")

            sides = [(0, slice(0, CAP)), (1, slice(CAP, 2 * CAP))]

            def gather():
                for t in range(TT):
                    for s, part in sides:
                        last = mm(ps[2][part, :], sel[:, t, :], htok[:, t, s * 512:s * 512 + 512], start=(t == 0), stop=(t == TT - 1))
                last.then_inc(psum_full[2], 1)

            def gathered():
                for k in range(4):
                    last = nc.tensor.transpose(ps[2][:, k * P:(k + 1) * P], hrow[:, k * P:(k + 1) * P], ident)
                last.then_inc(psum_full[2], 1)

            def start_bias():
                for bank in (0, 1):
                    for s, part in sides:
                        last = mm(ps[bank][part, :], con("onerow"), bias[:, bank * FF + s * 512:bank * FF + s * 512 + 512], start=True, stop=False)
                last.then_inc(S("bias_used"), 1)

            pe.wait_ge(psum_free[2], BANK_USES[2])
            pe.wait_ge(S("selected"), 1)
            stored(pe, "th21")
            gather()
            for bank in (0, 1):
                pe.wait_ge(psum_free[bank], BANK_USES[bank])
            pe.wait_ge(S("bias_in"), 16)
            start_bias()
            pe.wait_ge(psum_free[2], BANK_USES[2] + 1)
            gathered()

            def expert(it, e):
                pe.wait_ge(psum_free[2], it * 2 + (BANK_USES[2] + 2))
                for k in range(KT):
                    slot = EXPERT_SLOT[k]
                    pe.wait_ge(ring_full[slot], it * 16 + 16 * (USES[slot] + 1))
                    w = view(slot * CHUNK, CHUNK)
                    for bank in (0, 1):
                        for s, part in sides:
                            at = bank * FF + s * 512
                            last = mm(ps[bank][part, :], xte[:, k, :], w[:, at:at + 512], start=False, stop=(k == KT - 1))
                        if k == KT - 1:
                            last.then_inc(psum_full[bank], 1)
                    if k < KT - 1:
                        last.then_inc(S("chunk_used"), 1)
                pe.wait_ge(psum_free[5], it + BANK_USES[5])
                pe.wait_ge(S("weighted"), it + 1)
                for t in range(TT):
                    last = nc.tensor.transpose(ps[5][:, t * P:(t + 1) * P], selg[:, t, :], ident)
                last.then_inc(psum_full[5], 1)
                pe.wait_ge(S("selected"), it + 2)
                gather()
                pe.wait_ge(psum_free[3], it * 2 + BANK_USES[3])
                pe.wait_ge(S("activated"), it + 1)
                for k in range(4):
                    last = nc.tensor.transpose(ps[3][:, k * P:(k + 1) * P], hact[:, k * P:(k + 1) * P], ident)
                last.then_inc(psum_full[3], 1)
                pe.wait_ge(psum_free[2], it * 2 + (BANK_USES[2] + 3))
                gathered()
                pe.wait_ge(psum_free[3], it * 2 + (BANK_USES[3] + 1))
                pe.wait_ge(psum_free[4], it * 2 + BANK_USES[4])
                pe.wait_ge(S("bdown_in"), it * 16 + 16)
                for s, part in sides:
                    mm(ps[4][part, :], con("onerow"), bdown[:, s * 512:s * 512 + 512], start=True, stop=False)
                for k in range(KT):
                    slot = EXPERT_SLOT[8 + k // 2]
                    if k % 2 == 0:
                        pe.wait_ge(ring_full[slot], it * 16 + 16 * (USES[slot] + 1))
                    w = view(slot * CHUNK, 2, D)
                    for s, part in sides:
                        last = mm(ps[4][part, :], actT[:, k % 4, (k // 4) * CAP:(k // 4 + 1) * CAP], w[:, k % 2, s * 512:s * 512 + 512],
                                  start=False, stop=(k == KT - 1))
                    if k == KT - 1:
                        last.then_inc(psum_full[4], 1)
                    elif k % 2:
                        last.then_inc(S("chunk_used"), 1)
                for bank in (0, 1):
                    pe.wait_ge(psum_free[bank], it + (BANK_USES[bank] + 1))
                pe.wait_ge(S("bias_in"), it * 16 + 32)
                start_bias()
                pe.wait_ge(psum_free[4], it * 2 + (BANK_USES[4] + 1))
                pe.wait_ge(psum_free[5], it + (BANK_USES[5] + 1))
                for t, banks, at in ((0, (6, 7), 0), (1, (3, 4), 1), (2, (6, 7), 1)):
                    for bank in banks:
                        pe.wait_ge(psum_free[bank], it * 2 + (BANK_USES[bank] + at))
                    for s, part in sides:
                        mm(ps[banks[s]][:, :], gtt[part, t, :], yb[part, :], start=True, stop=True).then_inc(psum_full[banks[s]], 1)

            all_passes(pe, expert)

        @block.scalar
        def _(act):
            step = Steps(act, "act_steps")
            af = nc.scalar.activation
            act.wait_ge(S("x_in"), 16)
            for k in range(KT):
                step(af(xsq[:, k, :], xT[:, k, :], ACT.Square), "xsq")
            stored(act, "ss_x")
            step(af(view(YL, T), view(YL, T), ACT.Sqrt), "rx_sqrt")
            stored(act, "ss_m")
            step(af(view(KKO, NM), view(KKO, NM), ACT.Sqrt), "rm_sqrt")
            act.wait_ge(S("s5p_in"), 16)
            step(af(s5p("dt", 16), s5p("dt", 16), ACT.Exp), "s5_dt")
            act.wait_ge(S("s5_mag_arg"), 1)
            step(af(view(SCAN, 16), view(SCAN, 16), ACT.Exp), "s5_mag")
            act.wait_ge(S("s5_angles"), 1)
            step(af(view(SCAN + 32, 32), view(SCAN + 32, 32), ACT.Sin), "s5_sincos")

            def copy(dst, job, src=None):
                b = computed(act, job)
                step.read_out(af(dst, b[:, 0:T] if src is None else src(b), ACT.Identity), job)

            for i in TILES4:
                copy(uT[:, i, 7:], f"u{i}")
            act.wait_ge(S("u_pad"), 1)
            act.dma_start(u_dram.ap().rearrange("(c p) t -> p c t", p=P), uT).then_inc(S("u_stored"), 16)

            def s5_params(ct):
                copy(E_r, f"er{ct}", lambda b: b[:, :].rearrange("p (q n) -> p q n", q=PAIRS))
                copy(E_i, f"ei{ct}", lambda b: b[:, :].rearrange("p (q n) -> p q n", q=PAIRS))
                if ct == 0:
                    act.wait_ge(S("kk_zero"), 1)
                b = computed(act, f"kk{ct}")[:, 0:128].rearrange("p (q n) -> p q n", q=PAIRS)
                dst = view(KKO, PAIRS, 2, 32)
                step(af(dst[:, :, 0, 0:16], b[:, :, 0:16], ACT.Identity))
                step.read_out(af(dst[:, :, 1, 16:32], b[:, :, 16:32], ACT.Identity), f"kk{ct}")

            def load_windows(ct):
                if ct >= 2:
                    computed(act, f"loc{ct - 2}")
                for tap in range(BL):
                    src = bass.AP(u_dram, ct * P * (T + 7) + tap, [[T + 7, GC], [GC * (T + 7), 8], [1, T]])
                    act.dma_start(uwins[ct % 2][tap * GC:(tap + 1) * GC], src).then_inc(S(f"uwin_in{ct % 2}"), 16)

            act.wait_ge(S("u_stored"), 16)
            for kind, n in MIX_ORDER:
                if kind == "in":
                    copy(prj[n[0]][:, int(n[1]), :], n)
                elif kind == "par":
                    s5_params(n)
                elif kind == "load":
                    load_windows(n)
                elif kind == "blk":
                    if n >= 2:
                        act.wait_ge(S("s5_x0"), n - 1)
                    copy(xes[n % 2], f"ve{n}", lambda b: b[:, 0:2 * PAIRS * NBL].rearrange("p (r q n) -> p r q n", r=2, q=PAIRS))
                elif kind == "out":
                    act.wait_ge(S("gelu_arg"), n + 1)
                    step(af(mix[:, n, :], mix[:, n, :], ACT.Tanh, scale=float(np.sqrt(2 / np.pi))), "gelu_tanh")
                elif kind == "lora_up":
                    for job, dst, rows, fn in (("lw", hidden["dw"], 64, ACT.Tanh), ("la", hidden["da"], 64, ACT.Identity),
                                               ("lg", hidden["dg"], P, ACT.Sigmoid)):
                        b = computed(act, job)
                        step.read_out(af(dst[0:rows, :], b[0:rows, 0:T], fn), job)
                elif kind == "lora_down":
                    for i in TILES4:
                        b = computed(act, f"dw{i}")
                        step.read_out(af(R[3][:, i, :], b[:, 0:T], ACT.Sigmoid, bias=vec("rwkv_w0", i)), f"dw{i}")
                    act.wait_ge(S("delta_free"), 1)
                    for i in TILES4:
                        b = computed(act, f"da{i}")
                        step.read_out(af(R[7][:, i, :], b[:, 0:T], ACT.Sigmoid, bias=vec("rwkv_a0", i)), f"da{i}")
                    for i in TILES4:
                        copy(R[5][:, i, :], f"dg{i}")
                    step(af(R[3], R[3], ACT.Exp, scale=-DECAY), "decay")
                elif kind == "memk":
                    copy(mkT[:, n, :], f"mk{n}", lambda b: b[:, 0:NM])
                elif kind == "knorm":
                    stored(act, "kn3")
                    step(af(R[9], R[9], ACT.Sqrt), "kk_norm")
                elif kind == "glu":
                    for i in TILES4:
                        b = computed(act, f"gl{i}")
                        step.read_out(af(view(UWIN, CT, T)[:, i, :], b[:, 0:T], ACT.Sigmoid, bias=vec("s5_glu_b", i)), f"gl{i}")
            act.wait_ge(S("s5_final"), CT)
            act.dma_start(o["s5"], s5fin).then_inc(S("s5_stored"), 16)
            act.wait_ge(S("shifts"), 4)
            act.dma_start(o["shift"], shift).then_inc(S("stores"), 16)
            reached = [0]

            def fillers(job=None):
                while reached[0] < len(RWKV_JOBS) and (job is None or reached[0] <= RWKV_JOBS.index(job)):
                    for f in FILL_DONE[RWKV_JOBS[reached[0]]]:
                        dst = mkT[:, int(f[2]), :] if f.startswith("mk") else mv[:, int(f[3]), int(f[2]) * 256:int(f[2]) * 256 + 256]
                        copy(dst, f, lambda b: b[:, 0:256])
                    reached[0] += 1

            def rwkv_copy(dst, job, n):
                fillers(job)
                copy(dst, job, lambda b: b[:, 0:n * CH].rearrange("p (c n) -> p c n", c=n))

            for i in TILES4:
                for nm, dst in (("b", bT), ("v", vT), ("k", kT), ("a", aT)):
                    rwkv_copy(dst[:, i], f"t{nm}{i}", NC)
            act.wait_ge(S("s5_gated"), CT)
            for lv in range(1, 6):
                n = NC if lv < 3 else PC
                for i in TILES4:
                    rwkv_copy(Y[:, i, 0:n], f"y{lv}_{i}", n)
            for i in TILES4:
                rwkv_copy(GT[:, i], f"gt{i}", NC)
                rwkv_copy(BV[:, i], f"bv{i}", NC)
            for c in range(PC):
                fillers(f"yy{c}")
                copy(YT[:, :, c * CH:(c + 1) * CH], f"yy{c}", lambda b: b[:, 0:CT * CH].rearrange("p (i n) -> p i n", i=CT))
            act.wait_ge(S("m_ready"), PC - 1)
            act.dma_start(o["wkv_p"], M[:, PC - 1]).then_inc(S("wkv_p_stored"), 16)
            for i in TILES4:
                fillers(f"ys{i}")
                copy(YT[:, i, TP:T], f"ys{i}", lambda b: b[:, 0:CH])
            fillers()
            act.dma_start(o["mem_k"], mkT).then_inc(S("stores"), 16)
            act.dma_start(o["mem_v"], mv).then_inc(S("stores"), 16)
            for i in TILES4:
                stored(act, f"me{i}")
                step(af(ysq[:, i, :], YT[:, i, :], ACT.Square), "y_squares")
            act.wait_ge(S("m0_done"), CT)
            act.dma_start(o["wkv_s"], m0).then_inc(S("wkv_stored"), 16)
            stored(act, "va3")
            step(af(gn, gn, ACT.Sqrt), "gn_sqrt")

            for n in range(KT):
                stored(act, f"o{n}")
                step(af(nT[:, n, :], xT[:, n, :], ACT.Identity, scale=vec("norm_ca_g", n)), "x1g")
                step(af(qT[:, n, :], xT[:, n, :], ACT.Square), "x1sq")
            stored(act, "ss_c")
            step(af(rx2, rx2, ACT.Sqrt), "rc_sqrt")
            act.wait_ge(S("wkv_p_stored"), 16)
            mx, sm = view(STAT, 16), view(STAT + 16, 16)
            for h in range(MH):
                act.wait_ge(S("neg_max"), h + 1)
                b = computed(act, f"sp{h}")
                for t in range(2):
                    i = 2 * h + t
                    ins = af(prob[:, h, t, :], b[:, t * NM:(t + 1) * NM], ACT.Exp, bias=mx[:, i:i + 1], scale=SCALE, accum_out=sm[:, i:i + 1])
                    step.read_out(ins, f"sp{h}") if t else step(ins)
            for g in range(2):
                act.wait_ge(S("neg_max"), MH + g + 1)
                b, i = computed(act, f"sb{g}"), 8 + g
                step.read_out(af(sprob[:, g, :], b[:, 0:NM], ACT.Exp, bias=mx[:, i:i + 1], scale=SCALE, accum_out=sm[:, i:i + 1]), f"sb{g}")
            for h in range(MH):
                copy(pT[:, h], f"tp{h}", lambda b: b[:, :].rearrange("p (m t) -> p m t", m=2))
            copy(spT, "tb", lambda b: b[:, :].rearrange("p (g m t) -> p g m t", g=2, m=2))
            for n in range(KT):
                copy(oT[:, n, 0:TP], f"op{n}", lambda b: b[:, 0:TP])
            for g in range(2):
                for half in range(2):
                    copy(srow[:, g, half * 512:half * 512 + 512], f"ob{g}{half}", lambda b: b[:, :])
            for g in range(2):
                for half in range(2):
                    b = computed(act, f"ox{g}{half}")[:, :].rearrange("p (n i r) -> p n i r", n=4, i=4)
                    for n in (0, 2):
                        h = (4 * half + n) // 2
                        dst = oT[:, 4 * half + n:4 * half + n + 2, TP + 32 * g:TP + 32 * g + 32].rearrange("p n (i t) -> p n i t", i=4)
                        ins = af(dst, b[:, n:n + 2, :, h * TS:(h + 1) * TS], ACT.Identity)
                        step.read_out(ins, f"ox{g}{half}") if n else step(ins)
            for n in range(KT):
                stored(act, f"co{n}")
                step(af(nT[:, n, :], xT[:, n, :], ACT.Square), "x2sq")
                step(af(hT[:, n, :], xT[:, n, :], ACT.Identity, scale=vec("norm_ffn_g", n)), "x2g")
            computed(act, "co7")
            act.dma_start(gfin, bass.AP(a["final_g"].tensor, 0, [[0, P], [1, D]])).then_inc(S("gfin_in"), 16)
            act.dma_start(rbias, bass.AP(a["router_b"].tensor, 0, [[0, P], [1, NE]])).then_inc(S("rbias_in"), 16)
            stored(act, "ss_f")
            step(af(rx2, rx2, ACT.Sqrt), "rf_sqrt")
            act.wait_ge(S("stores"), 16 * 3)
            act.wait_ge(S("tok_zero"), 2)
            for dst, nm in ((yacc, "tx"), (htok, "th")):
                if nm == "th":
                    stored(act, "lt")
                for t in range(TT):
                    for h in range(2):
                        b, rows = computed(act, f"{nm}{t}{h}"), slice(0, tile_rows[t])
                        factor = rxt[rows, t:t + 1] if nm == "th" else 1.0
                        step.read_out(af(dst[rows, t, h * 512:h * 512 + 512], b[rows, :], ACT.Identity, scale=factor), f"{nm}{t}{h}")
            act.wait_ge(S("top_shifted"), 1)
            step(af(g4, g4, ACT.Exp), "top_exp")

            def row_copies(it, part):
                act.wait_ge(psum_full[2], it * 2 + (BANK_USES[2] + 1 + part))
                if part == 0:
                    ins = af(hrow, ps[2][:, :], ACT.Identity)
                else:
                    ins = af(xte.rearrange("p (s k) c -> p k s c", s=2), ps[2][:, :].rearrange("p (k s c) -> p k s c", k=4, s=2), ACT.Identity)
                ins.then_inc(psum_free[2], 1)

            row_copies(0, 0)
            row_copies(0, 1)

            def expert(it, e):
                act.wait_ge(psum_free[0], it + (BANK_USES[0] + 1))
                af(sig, hg, ACT.Sigmoid, scale=ALPHA).then_inc(S("sigmoid"), 1)
                act.wait_ge(psum_full[5], it + (BANK_USES[5] + 1))
                af(gtt, ps[5][:, 0:TT * P].rearrange("p (t n) -> p t n", t=TT), ACT.Identity).then_inc(psum_free[5], 1)
                row_copies(it + 1, 0)
                act.wait_ge(psum_full[3], it * 2 + (BANK_USES[3] + 1))
                af(actT, ps[3][:, :].rearrange("p (k c) -> p k c", k=4), ACT.Identity).then_inc(psum_free[3], 1)
                row_copies(it + 1, 1)
                act.wait_ge(psum_full[4], it * 2 + (BANK_USES[4] + 1))
                af(yb, ps[4][:, :], ACT.Identity).then_inc(psum_free[4], 1)

            all_passes(act, expert)
            sm = view(SCR + 1100, 16)
            act.wait_ge(S("experts_done"), 1)
            for t in range(TT):
                step(af(view(HG, D), yacc[:, t, :], ACT.Square, accum_out=sm[:, t:t + 1]), "y_sq")
            act.wait_ge(S("y_var"), 1)
            step(af(sm[:, 0:TT], sm[:, 0:TT], ACT.Sqrt), "y_sqrt")

        @block.gpsimd
        def _(pool):
            step = Steps(pool, "pool_steps")
            tt, ts = nc.gpsimd.tensor_tensor, nc.gpsimd.tensor_scalar
            pool.wait_ge(S("mem_in"), 16)
            step(tt(memsq, memT, memT, ALU.mult), "memsq")
            step(nc.gpsimd.memset(uT[:, :, 0:7], 0.0), "u_pad")
            pool.wait_ge(S("nmem"), KT)
            step(nc.gpsimd.memset(view(KKO, 256), 0.0), "kk_zero")
            pool.wait_ge(S("consts_in"), 16)

            def advance(dst, src, lr, li, n):
                a_r = over(lr, 2, n)
                a_i = over(li, 2, n)
                u, v = w1[:, :, :, 0:n], w2[:, :, :, 0:n]
                step(tt(u, src, over(a_r, 1, 2), ALU.mult))
                step(tt(v[:, 0], src[:, 1], a_i, ALU.mult))
                step(tt(v[:, 1], src[:, 0], a_i, ALU.mult))
                step(tt(u[:, 0], u[:, 0], v[:, 0], ALU.subtract))
                step(tt(u[:, 1], u[:, 1], v[:, 1], ALU.add))
                step(tt(dst, dst, u, ALU.add))

            def scan(ct):
                qs = slice(PAIRS * ct, PAIRS * ct + PAIRS)
                h0 = s5p("h0", 2, 16, NB)[:, :, qs, :]
                stored(pool, f"ve{ct}")
                xe = xes[ct % 2]
                advance(xe[:, :, :, PBL:NBL], h0, pw_r[:, 0, qs], pw_i[:, 0, qs], NB)
                for lv in range(5):
                    d = 1 << lv
                    lr, li = (view(PWO + 288 + 80 * i, 5, 16)[:, lv, qs] for i in range(2))
                    advance(xe[:, :, :, d:PBL], xe[:, :, :, 0:PBL - d], lr, li, PBL - d)
                step(nc.gpsimd.tensor_copy(s5fin[:, :, qs, :], xe[:, :, :, PBL - 1:NBL]), "s5_final")

            def starts(ct):
                h0 = s5p("h0", 2, 16, NB)[:, :, PAIRS * ct:PAIRS * ct + PAIRS, :]
                if ct:
                    computed(pool, f"st{ct - 1}")
                else:
                    step(nc.gpsimd.memset(x0[:, :, :, 0:1], 0.0))
                step(nc.gpsimd.tensor_copy(x0[:, :, :, PBL:NBL], h0))
                step(nc.gpsimd.tensor_copy(x0[:, :, :, 1:PBL], xes[ct % 2][:, :, :, 0:PBL - 1]), "s5_x0")

            pool.wait_ge(S("s5_ready"), 1)
            for ct in range(CT):
                scan(ct)
                starts(ct)
            pool.wait_ge(S("decay"), 1)
            computed(pool, "dg3")
            computed(pool, "v3")
            step(tt(R[13], R[3], over(con("carry"), 1, CT), ALU.mult))
            step(tt(R[8], R[3], R[13], ALU.subtract), "carried")

        @block.vector
        def _(dve):
            step = Steps(dve, "dve_steps")
            v = nc.vector
            tt, ts, stt, cp = v.tensor_tensor, v.tensor_scalar, v.scalar_tensor_tensor, v.tensor_copy
            add, sub, mul = ALU.add, ALU.subtract, ALU.mult
            dve.wait_ge(S("consts_in"), 16)
            dve.wait_ge(S("vecs_in"), 16)
            dve.wait_ge(S("x_in"), 16)

            dve.wait_ge(S("s5p_in"), 16)
            t = [view(SCAN + 16 * i, 16) for i in range(16)]
            rx, rm = view(YL, T), view(KKO, NM)
            b = computed(dve, "ss_x")
            step.read_out(ts(rx, b[:, 0:T], 1.0 / D, RMS_EPS, mul, add), "ss_x")
            dve.wait_ge(S("rx_sqrt"), 1)
            step(v.reciprocal(rx, rx))
            for k in range(KT):
                step(stt(n1[:, k, :], xT[:, k, :], vec("norm_mix_g", k), rx, mul, mul), "n1")
            b = computed(dve, "ss_m")
            step.read_out(ts(rm, b[:, 0:NM], 1.0 / D, RMS_EPS, mul, add), "ss_m")

            lr, li, dt = s5p("lr", 16), s5p("li", 16), s5p("dt", 16)
            dve.wait_ge(S("s5_dt"), 1)
            step(tt(t[0], lr, dt, mul), "s5_mag_arg")
            step(tt(t[1], li, dt, mul))
            for n, quarter in ((2, 0.0), (3, float(np.pi / 2))):
                step(ts(t[4], t[1], quarter, 1.0 / (2 * np.pi), add, mul))
                step(ts(t[4], t[4], ROUND, None, add))
                step(ts(t[4], t[4], ROUND, None, sub))
                step(stt(t[5], t[4], -TWO_PI_HI, t[1], mul, add))
                step(stt(t[5], t[4], -TWO_PI_LO, t[5], mul, add))
                step(ts(t[5], t[5], quarter, 3.1415925, add, ALU.min))
                step(ts(t[n], t[5], -3.1415925, None, ALU.max), "s5_angles" if n == 3 else None)
            dve.wait_ge(S("s5_mag"), 1)
            dve.wait_ge(S("s5_sincos"), 1)
            one_r, one_i = pw_r[:, BL - 1, :], pw_i[:, BL - 1, :]
            step(tt(one_r, t[0], t[3], mul))
            step(tt(one_i, t[0], t[2], mul))
            step(v.memset(pw_r[:, BL, :], 1.0))
            step(v.memset(pw_i[:, BL, :], 0.0))
            step(tt(t[6], lr, lr, mul))
            step(tt(t[7], li, li, mul))
            step(tt(t[6], t[6], t[7], add))
            step(v.reciprocal(t[6], t[6]))
            step(ts(t[7], one_r, 1.0, None, sub))
            step(tt(t[8], t[7], lr, mul))
            step(tt(t[9], one_i, li, mul))
            step(tt(t[8], t[8], t[9], add))
            step(tt(t[8], t[8], t[6], mul))
            step(tt(t[9], one_i, lr, mul))
            step(tt(t[10], t[7], li, mul))
            step(tt(t[9], t[9], t[10], sub))
            step(tt(t[9], t[9], t[6], mul))
            br, bi = s5p("br", 16, GC), s5p("bi", 16, GC)
            cr, ci = over(t[8], 2, GC), over(t[9], 2, GC)
            m = [view(SCAN + 256 + 256 * i, 16, GC) for i in range(3)]
            step(tt(m[0], br, cr, mul))
            step(tt(m[1], bi, ci, mul))
            step(tt(m[0], m[0], m[1], sub))
            step(tt(m[1], bi, cr, mul))
            step(tt(m[2], br, ci, mul))
            step(tt(bi, m[1], m[2], add))
            step(cp(br, m[0]))
            step(ts(view(S5O + S5P["ci"][0], 512), view(S5O + S5P["ci"][0], 512), -1.0, None, mul))

            def cmul(dst, src, by, n, signal=None):
                (dr, di), (sr, si), (qr, qi) = dst, src, by
                qr, qi = over(qr, 1, n), over(qi, 1, n)
                p, q = (view(SCAN + 256 + 64 * i, n, 16) for i in range(2))
                step(tt(p, si, qi, mul))
                step(tt(dr, sr, qr, mul))
                step(tt(dr, dr, p, sub))
                step(tt(q, si, qr, mul))
                step(tt(di, sr, qi, mul))
                step(tt(di, di, q, add), signal)

            def rows(lo, hi):
                return pw_r[:, lo:hi, :], pw_i[:, lo:hi, :]

            for lo, n in ((6, 1), (4, 2), (0, 4)):
                cmul(rows(lo, lo + n), rows(lo + n, lo + 2 * n), (pw_r[:, lo + n, :], pw_i[:, lo + n, :]), n)
            lvl_r, lvl_i = (view(PWO + 288 + 80 * i, 5, 16) for i in range(2))
            step(cp(lvl_r[:, 0, :], pw_r[:, 0, :]))
            step(cp(lvl_i[:, 0, :], pw_i[:, 0, :]))
            for i in range(1, 5):
                one = (lvl_r[:, i - 1, :], lvl_i[:, i - 1, :])
                cmul((lvl_r[:, i:i + 1, :], lvl_i[:, i:i + 1, :]), (lvl_r[:, i - 1:i, :], lvl_i[:, i - 1:i, :]), one, 1,
                     signal="s5_ready" if i == 4 else None)

            prev = view(VECO + VEC["prev"][0], 4, CT, NB)
            DELTA = R[7]

            def mixes(c):
                p, n = prj[c], PRJ_ORDER.index(c)
                stored(dve, f"{c}3")
                step(cp(shift[:, n], p[:, :, TP - 1::TS]), "shifts")
                ps_, ds_ = (x[:, :, TP:T].rearrange("p i (s t) -> p i s t", s=NB) for x in (p, DELTA))
                step(tt(DELTA[:, :, 1:TP], p[:, :, 0:TP - 1], p[:, :, 1:TP], sub))
                step(ts(DELTA[:, :, 0:1], p[:, :, 0:1], -1.0, None, mul))
                step(tt(ds_[:, :, :, 1:TS], ps_[:, :, :, 0:TS - 1], ps_[:, :, :, 1:TS], sub))
                step(tt(ds_[:, :, :, 0], prev[:, n], ps_[:, :, :, 0], sub))
                outs = [(R[4], 3), (R[5], 4), (R[6], 5)] if c == "z" else [(p, "rkv".index(c))]
                for dst, mu in outs:
                    for i in TILES4:
                        last = stt(dst[:, i, :], DELTA[:, i, :], vec("rwkv_mu", 4 * mu + i), p[:, i, :], mul, add)
                        step(last, "z_mixed" if c == "z" else ("delta_free" if (c, i) == ("v", 3) else None))

            def f_matrices(ct):
                if ct:
                    computed(dve, f"kk{ct - 1}")
                qs = slice(PAIRS * ct, PAIRS * ct + PAIRS)
                shape = "p q (j c) -> p q j c"
                fr, fi = F_r.rearrange(shape, j=BL), F_i.rearrange(shape, j=BL)
                tmp = view(RW[7], PAIRS, BL, GC)
                pr, pi = (over(p[:, 1:BL + 1, qs].rearrange("p j q -> p q j"), 3, GC) for p in (pw_r, pw_i))
                br, bi = (over(s5p(nm, 16, GC)[:, qs, :], 2, BL) for nm in ("br", "bi"))
                step(tt(fr, pr, br, mul))
                step(tt(tmp, pi, bi, mul))
                step(tt(fr, fr, tmp, sub))
                step(tt(fi, pr, bi, mul))
                step(tt(tmp, pi, br, mul))
                step(tt(fi, fi, tmp, add), "s5_f")

            def c_matrices(ct):
                if ct:
                    computed(dve, f"st{ct - 1}")
                qs = slice(PAIRS * ct, PAIRS * ct + PAIRS)
                pr, pi = (over(p[:, 0:BL, qs].rearrange("p j q -> p q j"), 3, 32) for p in (pw_r, pw_i))
                cr, ci = (over(c[:, qs, :], 2, BL) for c in (cbd_r, cbd_i))
                tmp = view(MV, PAIRS, BL, 32)
                step(tt(ca_r, pr, cr, mul))
                step(tt(tmp, pi, ci, mul))
                step(tt(ca_r, ca_r, tmp, add))
                step(tt(ca_i, pr, ci, mul))
                step(tt(tmp, pi, cr, mul))
                step(tt(ca_i, ca_i, tmp, sub), "s5_ca")

            def mask_windows(ct):
                dve.wait_ge(S(f"uwin_in{ct % 2}"), 16 * BL * (ct // 2 + 1))
                step(tt(uwins[ct % 2], uwins[ct % 2], over(con("window"), 1, 8), mul), "uwin")

            def s5_local(ct):
                b = computed(dve, f"loc{ct}")
                step.read_out(stt(yl[ct], uT[:, ct, 7:], vec("s5_d", ct), b[:, 0:T], mul, add), f"loc{ct}")

            def s5_gelu(ct):
                b = computed(dve, f"st{ct}")
                y = yl[ct].rearrange("p (c j) -> p j c", j=BL)
                step.read_out(tt(y, y, b[:, 0:T].rearrange("p (j c) -> p j c", j=BL), add), f"st{ct}")
                z = mix[:, ct, :]
                step(tt(z, yl[ct], yl[ct], mul))
                step(ts(z, z, 0.044715, 1.0, mul, add))
                step(tt(z, z, yl[ct], mul), "gelu_arg")
                dve.wait_ge(S("gelu_tanh"), ct + 1)
                step(stt(z, z, 1.0, yl[ct], add, mul))
                step(ts(z, z, 0.5, None, mul), "s5_gelu")

            kk, w, a_, k, r, prod = R[4], R[3], R[7], R[1], R[0], Rc[12]

            def kk_squares():
                computed(dve, "lg")
                for i in TILES4:
                    step(ts(kk[:, i, :], R[1][:, i, :], vec("rwkv_k_k", i), None, mul))
                step(tt(R[6], kk, kk, mul), "kk_squares")

            def k_norm():
                for i in TILES4:
                    b = computed(dve, f"kn{i}")
                    step.read_out(ts(R[9][:, i, :], b[:, 0:T], 1e-24, None, ALU.max), f"kn{i}")
                dve.wait_ge(S("kk_norm"), 1)
                step(v.reciprocal(R[9], R[9]))
                step(tt(kk, kk, R[9], mul))

            def decays():
                dve.wait_ge(S("carried"), 1)
                flat = [view(RW[i], ROW) for i in (13, 8, 12)]
                step(v.tensor_tensor_scan(flat[2], flat[0], flat[1], 0.0, mul, add))
                step(cp(pend[:, :, 0:PC], prod[:, :, 0:PC, CH - 1]))
                step(cp(pend[:, :, PC:], prod[:, :, PC, TS - 1::TS]))
                step(v.reciprocal(R[9], R[12]))
                stored(dve, "da3")
                computed(dve, "kn3")
                for i in TILES4:
                    ka, one = vec("rwkv_k_a", i), view(SCAN + 700, 1)
                    step(ts(one, ka, -1.0, 1.0, mul, add))
                    step(ts(R[6][:, i, :], a_[:, i, :], ka, one, mul, add))
                step(tt(k, k, R[6], mul))
                step(tt(R[6], kk, a_, mul))

            def keys():
                flatc = [x.rearrange("p i c n -> p (i c) n") for x in (Rc[4], prod, Rc[0])]
                arf = ar.rearrange("p i c a n -> p (i c) a n")
                computed(dve, "st3")
                step(stt(arf[:, :, 0, 1:], flatc[0][:, :, 1:], -1.0, flatc[1][:, :, 0:CH - 1], mul, mul))
                step(ts(arf[:, :, 0, 0:1], flatc[0][:, :, 0:1], -1.0, None, mul))
                step(ts(ar[:, :, PC, 0, TS::TS], Rc[4][:, :, PC, TS::TS], -1.0, None, mul), "rw_keys")
                step(tt(arf[:, :, 1, :], flatc[2], flatc[1], mul), "rw_keys")
                for i in TILES4:
                    step(stt(R[8][:, i, :], r[:, i, :], vec("rwkv_r_k", i), k[:, i, :], mul, mul), "rkr" if i == 3 else None)
                step(tt(R[6], R[6], R[9], mul), "rw_keys")
                step(tt(R[7], k, R[9], mul), "rw_keys")
                for i in TILES4:
                    b = computed(dve, f"bo{i}")
                    step.read_out(tt(R[1][:, i, :], b[:, 0:T], R[2][:, i, :], mul), f"bo{i}")

            def glu():
                for i in TILES4:
                    stored(dve, f"gl{i}")
                for i in TILES4:
                    step(tt(mix[:, i, :], mix[:, i, :], view(UWIN, CT, T)[:, i, :], mul), "s5_gated")

            def mem_norm():
                dve.wait_ge(S("rm_sqrt"), 1)
                step(v.reciprocal(rm, rm))
                dve.wait_ge(S("mem_in"), 16)
                dve.wait_ge(S("memsq"), 1)
                for k in range(KT):
                    step(stt(memT[:, k, :], memT[:, k, :], vec("norm_mem_g", k), rm, mul, mul), "nmem")

            for kind, n in MIX_ORDER:
                if kind == "mix":
                    mixes(n)
                elif kind == "memnorm":
                    mem_norm()
                elif kind == "f":
                    f_matrices(n)
                elif kind == "win":
                    mask_windows(n)
                elif kind == "c":
                    c_matrices(n)
                elif kind == "y":
                    s5_local(n)
                elif kind == "out":
                    s5_gelu(n)
                elif kind == "kk":
                    kk_squares()
                elif kind == "knorm":
                    k_norm()
                elif kind == "decays":
                    decays()
            keys()
            glu()

            strict, incl = (con(nm).rearrange("p (a n) -> p a n", a=2) for nm in ("strict", "incl"))
            level = con("level").rearrange("p (l n) -> p l n", l=6)
            def a_level(lv, i):
                n = NC if lv < 3 else PC
                step(tt(al[:, i, 0:n], AT[:, i, 0:n], over(level[:, lv], 1, n), mul), "a_level")

            for i in GRAM_ORDER:
                kind, blocks = (0, lambda x: x[:, i, 0:PC]) if i < 4 else (1, lambda x: x[:, :, PC])
                for nm, first, second in (("b", AT, C1), ("k", BT, C2)):
                    b = computed(dve, f"g{nm}{i}")[:, :].rearrange("p (c a n) -> p c a n", c=4, a=2)
                    if nm == "b":
                        step(cp(blocks(first), b[:, :, 0, :]))
                        if i < 4:
                            a_level(0, i)
                    else:
                        step(tt(blocks(first), b[:, :, 0, :], over(strict[:, kind], 1, 4), mul))
                    step.read_out(tt(blocks(second), b[:, :, 1, :], over(incl[:, kind], 1, 4), mul), f"g{nm}{i}")

            for i in TILES4:
                b = computed(dve, f"y0_{i}")[:, 0:T].rearrange("p (c n) -> p c n", c=NC)
                step.read_out(tt(X[:, i], b, over(con("ident64"), 1, NC), add), f"y0_{i}")
                step(tt(XI[:, i], al[:, i], over(con("ident64"), 1, NC), add))
                a_level(1, i)
            for lv in range(1, 6):
                n = NC if lv < 3 else PC
                for i in TILES4:
                    if lv < 5:
                        b = computed(dve, f"dx{lv}_{i}")[:, 0:n * CH].rearrange("p (c n) -> p c n", c=n)
                        step.read_out(tt(X[:, i, 0:n], X[:, i, 0:n], b, add), f"dx{lv}_{i}")
                    b = computed(dve, f"dt{lv}_{i}")[:, 0:n * CH].rearrange("p (c n) -> p c n", c=n)
                    step.read_out(tt(XI[:, i, 0:n], XI[:, i, 0:n], b, add), f"dt{lv}_{i}")
                    if lv < 5:
                        a_level(lv + 1, i)
            seq = con("seqmask")
            own = view(RW[8] + 512, CT, HN)
            for i in TILES4:
                tmp = view(RW[8], NB, HN)
                b = computed(dve, f"us{i}")[:, :].rearrange("p (s n) -> p s n", s=NB)
                step.read_out(tt(tmp, b, over(seq, 2, HN), mul), f"us{i}")
                step(v.reduce_sum(own[:, i], tmp.rearrange("p s n -> p n s"), AX.X))
            for i in TILES4:
                b = computed(dve, f"hh{i}")[:, 0:T].rearrange("p (c n) -> p c n", c=NC)
                step.read_out(cp(H[:, i], b), f"hh{i}")
            step(cp(U[:, :, 0], H[:, :, 0]), "u_first")
            for c in range(PC):
                if c:
                    b = computed(dve, f"u_{c}")[:, 0:CT * HN].rearrange("p (i n) -> p i n", i=CT)
                    step.read_out(tt(U[:, :, c], b, H[:, :, c], add), f"u_{c}")
                b = computed(dve, f"m_{c}")[:, 0:CT * HN].rearrange("p (i n) -> p i n", i=CT)
                scale = over(pend[:, :, c], 2, HN)
                if c:
                    step.read_out(tt(M[:, c], b, M[:, c - 1], add), f"m_{c}")
                    step(tt(M[:, c], M[:, c], scale, mul), "m_ready")
                else:
                    step.read_out(tt(M[:, 0], b, scale, mul), "m_0")
            step(tt(U[:, :, PC], own, H[:, :, PC], add), "u_sample")
            for i in TILES4:
                if i >= 2:
                    computed(dve, f"sf{i - 2}")
                for src, dst, signal in ((U, um, None), (vT, vm, "uv_masked")):
                    step(tt(dst[:, i % 2].rearrange("p (s n) -> p s n", s=NB), over(src[:, i, PC], 1, NB), over(seq, 2, HN), mul), signal)
            for i in TILES4:
                b = computed(dve, f"sf{i}")[:, :].rearrange("p (s n) -> p s n", s=NB)
                step.read_out(tt(m0[:, i], m0[:, i], b, add), f"sf{i}")
                step(tt(m0[:, i], m0[:, i], over(pend[:, i, PC:], 2, HN), mul), "m0_done")
            for i in TILES4:
                b = computed(dve, f"me{i}")
                step.read_out(stt(YT[:, i, :], b[:, 0:T], -1.0 / HN, YT[:, i, :], mul, add), f"me{i}")
            for i in TILES4:
                b = computed(dve, f"va{i}")
                step.read_out(ts(gn[:, i, :], b[:, 0:T], 1.0 / HN, GN_EPS, mul, add), f"va{i}")
            dve.wait_ge(S("gn_sqrt"), 1)
            step(v.reciprocal(gn, gn))
            dve.wait_ge(S("s5_stored"), 16)
            for i in TILES4:
                y = YT[:, i, :]
                step(stt(y, y, vec("rwkv_ln_w", i), gn[:, i, :], mul, mul))
                step(stt(y, y, vec("rwkv_ln_b", i), R[1][:, i, :], add, add))
                step(tt(mix[:, CT + i, :], y, R[5][:, i, :], mul), "mix_ready")

            def token_factors(sumsq, sqrt):
                b = computed(dve, sumsq)
                step.read_out(ts(rx2, b[:, 0:T], 1.0 / D, RMS_EPS, mul, add), sumsq)
                dve.wait_ge(S(sqrt), 1)
                step(v.reciprocal(rx2, rx2))

            for n in range(KT):
                b = computed(dve, f"o{n}")
                step.read_out(tt(xT[:, n, :], xT[:, n, :], b[:, 0:T], add), f"o{n}")
            computed(dve, MEM_V[-1])
            step(v.memset(view(QBLK, 2048), 0.0))
            token_factors("ss_c", "rc_sqrt")
            for n in range(KT):
                b = computed(dve, f"q{n}")
                step.read_out(tt(qT[:, n, :], b[:, 0:T], rx2, mul), f"q{n}")
            stored(dve, "q7")
            for h in range(MH):
                step(cp(qblk[:, 2 * h:2 * h + 2, :, h * TS:(h + 1) * TS],
                        qT[:, 2 * h:2 * h + 2, TP:T].rearrange("p n (s t) -> p n s t", s=NB)), "qblk")
            mx, sm = view(STAT, 16), view(STAT + 16, 16)
            for h in range(MH):
                b = computed(dve, f"sp{h}")
                step(v.reduce_max(mx[:, 2 * h:2 * h + 2], b[:, :].rearrange("p (t m) -> p t m", t=2), AX.X))
                step(ts(mx[:, 2 * h:2 * h + 2], mx[:, 2 * h:2 * h + 2], -SCALE, None, mul), "neg_max")
            for g in range(2):
                b = computed(dve, f"sb{g}")
                step(v.reduce_max(mx[:, 8 + g:9 + g], b[:, 0:NM], AX.X))
                step(ts(mx[:, 8 + g:9 + g], mx[:, 8 + g:9 + g], -SCALE, None, mul), "neg_max")
            for h in range(MH):
                stored(dve, f"sp{h}")
                step(v.reciprocal(sm[:, 2 * h:2 * h + 2], sm[:, 2 * h:2 * h + 2]))
                step(tt(prob[:, h], prob[:, h], over(sm[:, 2 * h:2 * h + 2], 2, NM), mul), "prob")
            for g in range(2):
                stored(dve, f"sb{g}")
                step(v.reciprocal(sm[:, 8 + g:9 + g], sm[:, 8 + g:9 + g]))
                step(ts(sprob[:, g, :], sprob[:, g, :], sm[:, 8 + g:9 + g], None, mul), "prob")
            for n in range(KT):
                b = computed(dve, f"co{n}")
                step.read_out(tt(xT[:, n, :], xT[:, n, :], b[:, 0:T], add), f"co{n}")
                if n == 2:
                    step(v.memset(bias, 0.0), "bias_zero")
                if n == 4:
                    dve.wait_ge(S("stores"), 16 * 3)
                    step(v.memset(htok[CAP:, TT - 1, :], 0.0), "tok_zero")
                    step(v.memset(yacc[CAP:, TT - 1, :], 0.0), "tok_zero")
            token_factors("ss_f", "rf_sqrt")
            step(v.memset(bdown, 0.0), "bdown_zero")

            b = computed(dve, "lgt")
            step.read_out(tt(lgt, b[0:NE, 0:T], rx2[0:NE, :], mul), "lgt")
            step(v.memset(logit, 0.0))
            dve.wait_ge(S("rbias_in"), 16)
            b = computed(dve, "lt")
            step(tt(logit[:, 0:2], b[:, 0:2 * NE].rearrange("p (t e) -> p t e", t=2), over(rbias, 1, 2), add))
            step(tt(logit[0:tile_rows[2], 2], b[0:tile_rows[2], 2 * NE:3 * NE], rbias[0:tile_rows[2], :], add))
            step(cp(rxt[:, 0:2], b[:, TT * NE:TT * NE + 2]))
            step.read_out(cp(rxt[0:tile_rows[2], 2:3], b[0:tile_rows[2], TT * NE + 2:TT * NE + 3]), "lt")
            for t in range(TT):
                step(v.max(top[:, t], logit[:, t]))
                step(v.max_index(idx_u[:, t], top[:, t], logit[:, t]))
            step(cp(idxf, idx_u))
            step(tt(g4, top[:, :, 0:TOPK], over(top[:, :, 0], 2, TOPK), sub), "top_shifted")
            expert_no = over(con("iota")[:, 0:NE], 1, TT)
            step(tt(mask, expert_no, over(idxf[:, :, 0], 2, NE), ALU.is_equal))
            for j in range(1, TOPK):
                step(tt(eq, expert_no, over(idxf[:, :, j], 2, NE), ALU.is_equal))
                step(tt(mask, mask, eq, add))
            step(v.memset(mask[CAP:, TT - 1, :], 0.0), "mask")
            dve.wait_ge(S("top_exp"), 1)
            step(v.reduce_sum(gsum, g4, AX.X))
            step(v.reciprocal(gsum, gsum))
            step(tt(g4, g4, over(gsum, 2, TOPK), mul))
            step(tt(gate, expert_no, over(idxf[:, :, 0], 2, NE), ALU.is_equal))
            step(tt(gate, gate, over(g4[:, :, 0], 2, NE), mul))
            tabt = tab.rearrange("p e s -> p s e")
            b = computed(dve, "pos")[:, 0:TT * NE].rearrange("p (t e) -> p t e", t=TT)
            step.read_out(stt(eg, b, 1.0, mask, add, mul), "pos")
            step(ts(tabt[:, 0:TT, 0:NE], eg, -1.0, None, add))
            step(cp(cur[:, 0:TT], tab[:, 0, 0:TT]))
            step(tt(sel, over(con("iota")[:, 0:CAP], 1, TT), over(cur[:, 0:TT], 2, CAP), ALU.is_equal), "selected")
            for j in range(1, TOPK):
                step(tt(eq, expert_no, over(idxf[:, :, j], 2, NE), ALU.is_equal))
                step(tt(eq, eq, over(g4[:, :, j], 2, NE), mul))
                step(tt(gate, gate, eq, add))
            step(v.memset(gate[CAP:, TT - 1, :], 0.0))
            step(cp(tabt[:, TT:, 0:NE], gate))
            step(ts(tab[:, NE, 0:TT], tab[:, 0, 0:TT], -float(CAP), None, add))
            step(cp(tab[:, NE, TT:], tab[:, 0, TT:]))
            step(cp(cur[:, TT:2 * TT], tab[:, 0, TT:]))
            b = computed(dve, "cnt")
            step.read_out(v.reduce_max(gsum[:, 0:1], b[:, 0:NE], AX.X), "cnt")
            step(cp(most_i32[:, :], gsum[:, 0:1]), "counts")
            stored(dve, "tx21")

            def next_pass(p):
                ts(tab[:, :, 0:TT], tab[:, :, 0:TT], -float(CAP), None, add).then_inc(S("ranks_moved"), 1)
                dve.wait_ge(S("ranks_moved"), p)
                cp(cur[:, 7:8], tab[:, 0, 0:1])

            CHAIN = 2

            def expert(it, e):
                n = [0]

                def chain(ins):
                    n[0] += 1
                    ins.then_inc(S("expert_steps"), 1)
                    dve.wait_ge(S("expert_steps"), it * CHAIN + n[0])

                dve.wait_ge(psum_full[5], it + BANK_USES[5])
                for t in range(TT):
                    ins = ts(selg[:, t, :], con("iota"), cur[:, t:t + 1], cur[:, TT + t:TT + t + 1], ALU.is_equal, mul)
                ins.then_inc(S("weighted"), 1)
                dve.wait_ge(S("weighted"), it + 1)
                chain(cp(cur[:, 0:6], tab.rearrange("p e s -> p (e s)")[:, bass.ds(e * 6 + 6, 6)]))
                dve.wait_ge(psum_full[2], it * 2 + (BANK_USES[2] + 1))
                tt(sel, over(con("iota")[:, 0:CAP], 1, TT), over(cur[:, 0:TT], 2, CAP), ALU.is_equal).then_inc(S("selected"), 1)
                dve.wait_ge(psum_full[0], it + (BANK_USES[0] + 1))
                dve.wait_ge(S("selected"), it + 2)
                ts(hg, ps[0][:, :], LIMIT, None, ALU.min).then_inc(psum_free[0], 1)
                dve.wait_ge(psum_full[1], it + (BANK_USES[1] + 1))
                ts(hu, ps[1][:, :], LIMIT, -LIMIT, ALU.min, ALU.max).then_inc(psum_free[1], 1)
                dve.wait_ge(psum_free[0], it + (BANK_USES[0] + 1))
                dve.wait_ge(psum_free[1], it + (BANK_USES[1] + 1))
                chain(stt(hu, hu, 1.0, hg, add, mul))
                dve.wait_ge(S("sigmoid"), it + 1)
                tt(hact, hu, sig, mul).then_inc(S("activated"), 1)
                dve.wait_ge(S("activated"), it + 1)
                for t, banks, at in ((0, (6, 7), 1), (1, (3, 4), 2), (2, (6, 7), 2)):
                    for s, bank in enumerate(banks):
                        dve.wait_ge(psum_full[bank], it * 2 + (BANK_USES[bank] + at))
                        part = yacc[:, t, s * 512:s * 512 + 512]
                        tt(part, part, ps[bank][:, :], add).then_inc(psum_free[bank], 1)
                for bank in (3, 4, 6, 7):
                    dve.wait_ge(psum_free[bank], it * 2 + (BANK_USES[bank] + 2))
                assert n[0] == CHAIN

            all_passes(dve, expert, next_pass)
            step(cp(cur[:, 6:7], cur[:, 0:1]), "experts_done")
            sm = view(SCR + 1100, 16)
            dve.wait_ge(S("y_sq"), TT)
            step(ts(sm[:, 0:TT], sm[:, 0:TT], 1.0 / D, RMS_EPS, mul, add), "y_var")
            dve.wait_ge(S("y_sqrt"), 1)
            step(v.reciprocal(sm[:, 0:TT], sm[:, 0:TT]))
            dve.wait_ge(S("gfin_in"), 16)
            for t in range(TT):
                step(stt(htok[:, t, :], yacc[:, t, :], sm[:, t:t + 1], gfin, mul, mul), "final")


def _stationary(w, np_):
    k, n = w.shape
    return np_.ascontiguousarray(w.reshape(k // 128, 128, n // 256, 2, 128).transpose(2, 1, 3, 0, 4)).reshape(n // 256, 128, -1)


def _columns(v):
    return v.reshape(-1, 128).T


def _constants(np_):
    c = {n: np_.zeros((128, w), np_.float32) for n, (_, w) in CON.items()}
    p = np_.arange(128)
    s, t = p[:, None] % 64, np_.arange(64)[None, :]
    c["ident"][p, p] = 1
    c["headones"][:] = p[:, None] // 64 == p[None, :] // 64
    c["ones"][:] = 1
    for lv in range(6):
        b = 1 << lv
        c["level"][:, 64 * lv:64 * lv + 64] = (t // (2 * b) == s // (2 * b)) & (t // b % 2 == 1) & (s // b % 2 == 0)
    c["strict"][:, :64], c["strict"][:, 64:] = s < t, (s < t) & (s // TS == t // TS)
    c["incl"][:, :64], c["incl"][:, 64:] = s <= t, (s <= t) & (s // TS == t // TS)
    c["seqmask"][:] = s // TS == np_.arange(NB)[None, :]
    tok = np_.arange(T)
    c["carry"][:] = np_.where(tok < TP, tok % CH != 0, tok % TS != 0)[None, :]
    c["window"][:] = tok[None, :] % BL >= BL - 1 - p[:, None] // GC
    c["iota"][:] = (np_.arange(128) % CAP)[None, :]
    c["earlier"][:] = p[:, None] < p[None, :]
    c["ident64"][:] = s == t
    c["onerow"][0, :] = 1
    return np_.concatenate([c[n] for n in CON], axis=1)


def _pack(table, parts, rows, np_):
    out = np_.zeros((rows, sum(n for _, n in table.values())), np_.float32)
    for name, part in parts.items():
        at, n = table[name]
        part = np_.asarray(part)
        out[:part.shape[0], at:at + n] = part.reshape(part.shape[0], n)
    return out


def _layout(x, np_):
    w_in = x["w_in"][0]
    u, r, k, v, z = (w_in[:, i * 512:(i + 1) * 512] for i in range(5))
    kc = x["cache_mem_k"][0].reshape(NB, NM, KT, P).transpose(0, 3, 2, 1).reshape(NB, P, -1)
    vc = x["cache_mem_v"][0].reshape(NB, 2, P, D).transpose(0, 2, 1, 3).reshape(NB, P, -1)
    w_v = x["w_mem_kv"][0][:, D:].reshape(KT, P, 4, 256).transpose(2, 1, 0, 3).reshape(4, P, -1)
    glu = x["s5_glu_w"][0].reshape(4, P, 4, P).transpose(1, 2, 0, 3).reshape(1, P, -1)
    dense = np_.concatenate([_stationary(w, np_) for w in (u, k, z, r, v)]
                            + [_stationary(x["w_mem_kv"][0][:, :D], np_), glu, w_v, _stationary(x["w_out"][0], np_), _stationary(x["w_cq"][0], np_), kc, vc,
                               _stationary(x["w_co"][0], np_)])
    tokens = np_.concatenate([x["x_prompt"].reshape(-1, D), x["x_sample"].reshape(-1, D)])
    prev = x["state_rwkv_shift"][0].reshape(NB, 4, CT, P).transpose(3, 1, 2, 0).reshape(P, -1)
    vecs = {n: _columns(x[n]) for n in VEC if n != "prev"}
    vecs["prev"] = prev
    per_state = lambda w: w.reshape(16, 2, NS, -1).transpose(1, 2, 0, 3).reshape(P, -1)
    cpad = {}
    for n in ("s5_c_re", "s5_c_im"):
        c = x[n][0].reshape(16, 2, GC, NS).transpose(1, 3, 0, 2)
        out = np_.zeros((2, NS, 16, 2, GC), np_.float32)
        for g in range(2):
            out[g, :, :, g, :] = c[g]
        cpad[n] = out.reshape(P, -1)
    h0 = np_.stack([x[n][0].reshape(NB, 16, 2, NS).transpose(2, 3, 1, 0) for n in ("state_s5_re", "state_s5_im")], axis=2)
    s5p = {"lr": per_state(x["s5_lambda_re"][0]), "li": per_state(x["s5_lambda_im"][0]),
           "dt": per_state(np_.broadcast_to(x["s5_log_dt"][0][:, None], (32, NS))),
           "br": per_state(x["s5_b_re"][0]), "bi": per_state(x["s5_b_im"][0]),
           "cr": cpad["s5_c_re"], "ci": cpad["s5_c_im"], "h0": h0.reshape(P, -1)}
    up = lambda w: w[0].reshape(CT, P, -1).transpose(1, 0, 2).reshape(P, -1)
    smw = {"w1": up(x["rwkv_w1"]), "a1": up(x["rwkv_a1"]), "g1": up(x["rwkv_g1"]), "w2": x["rwkv_w2"][0], "a2": x["rwkv_a2"][0],
           "g2": x["rwkv_g2"][0], "router_w": x["router_w"][0].reshape(KT, P, NE).transpose(1, 0, 2).reshape(P, -1)}
    m0 = x["state_rwkv_wkv"][0].reshape(NB, CT, 2, HN, HN).transpose(2, 4, 1, 0, 3).reshape(P, CT, NB, HN)
    return {
        "xT": tokens.T.reshape(KT, P, T).transpose(1, 0, 2), "memT": x["mem_prompt"][0].T.reshape(KT, P, NM).transpose(1, 0, 2),
        "dense": dense, "vecs": _pack(VEC, vecs, P, np_), "consts": _constants(np_), "smw": _pack(SMW, smw, P, np_),
        "s5p": _pack(S5P, s5p, P, np_), "m0": m0, "w_gu": x["ex_w_gu"][0], "w_down": x["ex_w_down"][0], "b_gu": x["ex_b_gu"][0][list(range(NE)) + [0]],
        "b_down": x["ex_b_down"][0], "router_b": x["router_b"][0].reshape(1, NE), "final_g": x["norm_final_g"].reshape(1, D),
    }


_OUTS = {"y": (P, TT, D), "s5": (P, 2, 16, NB + 1), "shift": (P, 4, CT, NB + 1), "wkv_p": (P, CT, HN), "wkv_s": (P, CT, NB, HN),
         "mem_k": (P, KT, NM), "mem_v": (P, 2, D)}


def kernel(**inputs):
    import numpy as _np
    import concourse.bacc as _bacc
    from concourse import mybir as _mybir
    from concourse.bass_utils import run_bass_kernel_spmd as _run

    nc = _bacc.Bacc("TRN2", target_bir_lowering=False, num_devices=1)
    arrays, a = {}, {}
    for name, arr in _layout({k: _np.asarray(v) for k, v in inputs.items()}, _np).items():
        arr = _np.ascontiguousarray(arr)
        arrays[f"in_{name}"] = arr
        a[name] = nc.dram_tensor(f"in_{name}", arr.shape, _mybir.dt.from_np(arr.dtype), kind="ExternalInput").ap()
    o = {name: nc.dram_tensor(f"out_{name}", shape, _mybir.dt.float32, kind="ExternalOutput").ap() for name, shape in _OUTS.items()}
    build(nc, a, o)
    r = _run(nc, [arrays], core_ids=[0])
    g = {name: r.results[0][f"out_{name}"] for name in _OUTS}
    y = g["y"].transpose(1, 0, 2).reshape(TT * P, D)
    s5 = g["s5"].reshape(2, NS, 2, 16, NB + 1).transpose(2, 4, 3, 0, 1).reshape(2, NB + 1, 32, NS)
    shift = g["shift"].transpose(3, 1, 2, 0).reshape(NB + 1, 4 * W5)
    wkv = lambda w: w.transpose(3, 2, 0, 4, 1).reshape(-1, 8, HN, HN)
    wkv_p = wkv(g["wkv_p"].reshape(2, HN, CT, 1, HN))
    wkv_s = wkv(g["wkv_s"].reshape(2, HN, CT, NB, HN))
    mk = g["mem_k"].transpose(2, 1, 0).reshape(1, 1, NM, MH, MD)
    mv = g["mem_v"].transpose(1, 0, 2).reshape(1, 1, NM, MH, MD)
    c = _np.ascontiguousarray
    return (c(y[:TP].reshape(1, TP, D)), c(y[TP:T].reshape(NB, TS, D)), c(s5[0, None, :1]), c(s5[1, None, :1]), c(shift[None, :1]),
            c(wkv_p[None]), c(mk), c(mv), c(s5[0, None, 1:]), c(s5[1, None, 1:]), c(shift[None, 1:]), c(wkv_s[None]))
```
